# Optimizing a Trainium2 kernel written in Bass

```python
import math
import jax
import jax.numpy as jnp
from jax import lax
import numpy as np

D_MODEL = 1024
BATCH = 1
SEQ = 512
DEPTH = 2

CHUNK = 64
Q_BLOCK = 128
ROPE_THETA = 10000.0
NORM_EPS = 1e-6

A_HEADS = 4
A_QK_DIM = 64
A_V_DIM = 2 * A_QK_DIM
B_HEADS = 8
B_Q_RANK = 256
B_KV_RANK = 128
B_NOPE_DIM = 64
B_ROPE_DIM = 32
B_V_DIM = 64
C_HEADS = 16
C_HEAD_DIM = 64
C_WIDTH = C_HEADS * C_HEAD_DIM

A_Q_COLS = A_HEADS * 2 * A_QK_DIM
A_V_COLS = A_HEADS * A_V_DIM
AB_IN_SPLITS = (A_Q_COLS, A_Q_COLS, A_V_COLS, B_Q_RANK, B_KV_RANK, B_ROPE_DIM)
AB_IN_DIM = sum(AB_IN_SPLITS)
AB_OUT_DIM = A_HEADS * A_V_DIM + B_HEADS * B_V_DIM

D_FF = ((8 * D_MODEL // 3 + 255) // 256) * 256
N_EVEN = (DEPTH + 1) // 2
N_ODD = DEPTH // 2

kernel_name = "hybrid_diff_mla_stickbreak_trunk"

def lambda_init(layer_idx):
    return 0.8 - 0.6 * math.exp(-0.3 * layer_idx)

def rms_norm(x, gain):
    xf = x.astype(jnp.float32)
    y = xf * lax.rsqrt(jnp.mean(xf * xf, axis=-1, keepdims=True) + NORM_EPS)
    return (y * gain.astype(jnp.float32)).astype(x.dtype)

def rope(x, pos):
    d = x.shape[-1]
    half = d // 2
    inv_freq = jnp.power(ROPE_THETA, -jnp.arange(half, dtype=jnp.float32) / half)
    ang = pos.astype(jnp.float32)[:, None] * inv_freq[None, :]
    bshape = (1, x.shape[1]) + (1,) * (x.ndim - 3) + (half,)
    cos = jnp.cos(ang).reshape(bshape)
    sin = jnp.sin(ang).reshape(bshape)
    xf = x.astype(jnp.float32)
    x1, x2 = xf[..., :half], xf[..., half:]
    return jnp.concatenate([x1 * cos - x2 * sin, x2 * cos + x1 * sin], axis=-1).astype(x.dtype)

def split_cols(x, sizes):
    idx = [int(i) for i in np.cumsum(sizes)[:-1]]
    return jnp.split(x, idx, axis=-1)

def sweep_query_blocks(block_fn, seq):
    return jnp.concatenate([block_fn(lo, lo + Q_BLOCK) for lo in range(0, seq, Q_BLOCK)], axis=1)

def chunk_causal_mask(lo, hi):
    q_chunk = jnp.arange(lo, hi) // CHUNK
    k_chunk = jnp.arange(hi) // CHUNK
    return k_chunk[None, :] <= q_chunk[:, None]

def masked_softmax(scores, mask):
    return jax.nn.softmax(jnp.where(mask, scores, -jnp.inf), axis=-1)

def differential_attention(q1, q2, k1, k2, v, lam, scale):
    def block(lo, hi):
        mask = chunk_causal_mask(lo, hi)
        s1 = jnp.einsum('bqhd,bkhd->bhqk', q1[:, lo:hi], k1[:, :hi]).astype(jnp.float32) * scale
        s2 = jnp.einsum('bqhd,bkhd->bhqk', q2[:, lo:hi], k2[:, :hi]).astype(jnp.float32) * scale
        p = masked_softmax(s1, mask) - lam * masked_softmax(s2, mask)
        return jnp.einsum('bhqk,bkhd->bqhd', p.astype(v.dtype), v[:, :hi])
    return sweep_query_blocks(block, q1.shape[1])

def latent_attention(q_nope, q_rope, k_nope, k_rope, v, scale):
    def block(lo, hi):
        mask = chunk_causal_mask(lo, hi)
        s = (jnp.einsum('bqhd,bkhd->bhqk', q_nope[:, lo:hi], k_nope[:, :hi])
             + jnp.einsum('bqhr,bkr->bhqk', q_rope[:, lo:hi], k_rope[:, :hi])).astype(jnp.float32) * scale
        p = masked_softmax(s, mask)
        return jnp.einsum('bhqk,bkhd->bqhd', p.astype(v.dtype), v[:, :hi])
    return sweep_query_blocks(block, q_nope.shape[1])

def stick_breaking_attention(q, k, v, scale):
    def block(lo, hi):
        q_pos = jnp.arange(lo, hi)
        k_pos = jnp.arange(hi)
        mask = k_pos[None, :] < q_pos[:, None]
        z = jnp.einsum('bqhd,bkhd->bhqk', q[:, lo:hi], k[:, :hi]).astype(jnp.float32) * scale
        sp = jnp.where(mask, jax.nn.softplus(z), 0.0)
        tail = lax.cumsum(sp, axis=3, reverse=True) - sp
        w = jnp.where(mask, jnp.exp(jax.nn.log_sigmoid(z) - tail), 0.0)
        return jnp.einsum('bhqk,bkhd->bqhd', w.astype(v.dtype), v[:, :hi])
    return sweep_query_blocks(block, q.shape[1])

def diff_mla_mixer(h, pos, layer_idx, w_in, a_q_norm, a_k_norm, a_lambda, a_out_norm,
                   b_q_a_norm, b_w_q_b, b_kv_a_norm, b_w_kv_b,
                   b_q_nope_norm, b_q_rope_norm, b_k_nope_norm, b_k_rope_norm, w_out):
    B, S, _ = h.shape
    a_q, a_k, a_v, b_ql, b_kvl, b_kr = split_cols(h @ w_in, AB_IN_SPLITS)

    a_q = rope(rms_norm(a_q.reshape(B, S, 2 * A_HEADS, A_QK_DIM), a_q_norm), pos)
    a_k = rope(rms_norm(a_k.reshape(B, S, 2 * A_HEADS, A_QK_DIM), a_k_norm), pos)
    a_q = a_q.reshape(B, S, A_HEADS, 2, A_QK_DIM)
    a_k = a_k.reshape(B, S, A_HEADS, 2, A_QK_DIM)
    a_v = a_v.reshape(B, S, A_HEADS, A_V_DIM)
    lam_f = a_lambda.astype(jnp.float32)
    lam_0 = lambda_init(layer_idx)
    lam = jnp.exp(jnp.sum(lam_f[0] * lam_f[1])) - jnp.exp(jnp.sum(lam_f[2] * lam_f[3])) + lam_0
    out_a = differential_attention(a_q[:, :, :, 0], a_q[:, :, :, 1], a_k[:, :, :, 0], a_k[:, :, :, 1],
                                   a_v, lam, A_QK_DIM ** -0.5)
    out_a = rms_norm(out_a, a_out_norm) * (1.0 - lam_0)

    q_b = (rms_norm(b_ql, b_q_a_norm) @ b_w_q_b).reshape(B, S, B_HEADS, B_NOPE_DIM + B_ROPE_DIM)
    kv_b = (rms_norm(b_kvl, b_kv_a_norm) @ b_w_kv_b).reshape(B, S, B_HEADS, B_NOPE_DIM + B_V_DIM)
    q_nope, q_rope = q_b[..., :B_NOPE_DIM], q_b[..., B_NOPE_DIM:]
    k_nope, b_v = kv_b[..., :B_NOPE_DIM], kv_b[..., B_NOPE_DIM:]
    q_nope = rms_norm(q_nope, b_q_nope_norm)
    k_nope = rms_norm(k_nope, b_k_nope_norm)
    q_rope = rope(rms_norm(q_rope, b_q_rope_norm), pos)
    k_rope = rope(rms_norm(b_kr, b_k_rope_norm), pos)
    out_b = latent_attention(q_nope, q_rope, k_nope, k_rope, b_v,
                             (B_NOPE_DIM + B_ROPE_DIM) ** -0.5)

    mixed = jnp.concatenate([out_a.reshape(B, S, A_HEADS * A_V_DIM),
                             out_b.reshape(B, S, B_HEADS * B_V_DIM)], axis=-1)
    return mixed @ w_out

def stick_breaking_mixer(h, w_in, w_out):
    B, S, _ = h.shape
    q, k, v = jnp.split(h @ w_in, 3, axis=-1)
    q = q.reshape(B, S, C_HEADS, C_HEAD_DIM)
    k = k.reshape(B, S, C_HEADS, C_HEAD_DIM)
    v = v.reshape(B, S, C_HEADS, C_HEAD_DIM)
    out = stick_breaking_attention(q, k, v, C_HEAD_DIM ** -0.5)
    return out.reshape(B, S, C_WIDTH) @ w_out

def swiglu(h, w_gate, w_up, w_down):
    return (jax.nn.silu(h @ w_gate) * (h @ w_up)) @ w_down

def setup_inputs(seed: int = 0) -> dict:
    key = jax.random.key(seed)
    keys = list(jax.random.split(key, 32))

    def dense(shape, fan_in):
        return jax.random.normal(keys.pop(), shape, jnp.float32) * fan_in ** -0.5

    def gain(shape):
        return 1.0 + 0.02 * jax.random.normal(keys.pop(), shape, jnp.float32)

    return {
        "x": jax.random.normal(keys.pop(), (BATCH, SEQ, D_MODEL), jnp.float32),
        "norm_mix": gain((DEPTH, D_MODEL)),
        "norm_ffn": gain((DEPTH, D_MODEL)),
        "ab_w_in": dense((N_EVEN, D_MODEL, AB_IN_DIM), D_MODEL),
        "a_q_norm": gain((N_EVEN, A_QK_DIM)),
        "a_k_norm": gain((N_EVEN, A_QK_DIM)),
        "a_lambda": 0.1 * jax.random.normal(keys.pop(), (N_EVEN, 4, A_QK_DIM), jnp.float32),
        "a_out_norm": gain((N_EVEN, A_V_DIM)),
        "b_q_a_norm": gain((N_EVEN, B_Q_RANK)),
        "b_w_q_b": dense((N_EVEN, B_Q_RANK, B_HEADS * (B_NOPE_DIM + B_ROPE_DIM)), B_Q_RANK),
        "b_kv_a_norm": gain((N_EVEN, B_KV_RANK)),
        "b_w_kv_b": dense((N_EVEN, B_KV_RANK, B_HEADS * (B_NOPE_DIM + B_V_DIM)), B_KV_RANK),
        "b_q_nope_norm": gain((N_EVEN, B_NOPE_DIM)),
        "b_q_rope_norm": gain((N_EVEN, B_ROPE_DIM)),
        "b_k_nope_norm": gain((N_EVEN, B_NOPE_DIM)),
        "b_k_rope_norm": gain((N_EVEN, B_ROPE_DIM)),
        "ab_w_out": dense((N_EVEN, AB_OUT_DIM, D_MODEL), AB_OUT_DIM),
        "c_w_in": dense((N_ODD, D_MODEL, 3 * C_WIDTH), D_MODEL),
        "c_w_out": dense((N_ODD, C_WIDTH, D_MODEL), C_WIDTH),
        "ffn_w_gate": dense((DEPTH, D_MODEL, D_FF), D_MODEL),
        "ffn_w_up": dense((DEPTH, D_MODEL, D_FF), D_MODEL),
        "ffn_w_down": dense((DEPTH, D_FF, D_MODEL), D_FF),
    }

def reference(x, norm_mix, norm_ffn, ab_w_in, a_q_norm, a_k_norm, a_lambda, a_out_norm,
              b_q_a_norm, b_w_q_b, b_kv_a_norm, b_w_kv_b,
              b_q_nope_norm, b_q_rope_norm, b_k_nope_norm, b_k_rope_norm, ab_w_out,
              c_w_in, c_w_out, ffn_w_gate, ffn_w_up, ffn_w_down):
    pos = jnp.arange(x.shape[1], dtype=jnp.int32)
    for l in range(DEPTH):
        h = rms_norm(x, norm_mix[l])
        i = l // 2
        if l % 2 == 0:
            x = x + diff_mla_mixer(h, pos, l, ab_w_in[i], a_q_norm[i], a_k_norm[i], a_lambda[i],
                                   a_out_norm[i], b_q_a_norm[i], b_w_q_b[i], b_kv_a_norm[i],
                                   b_w_kv_b[i], b_q_nope_norm[i], b_q_rope_norm[i],
                                   b_k_nope_norm[i], b_k_rope_norm[i], ab_w_out[i])
        else:
            x = x + stick_breaking_mixer(h, c_w_in[i], c_w_out[i])
        h = rms_norm(x, norm_ffn[l])
        x = x + swiglu(h, ffn_w_gate[l], ffn_w_up[l], ffn_w_down[l])
    return x


_drawn_inputs = setup_inputs


def setup_inputs(seed=0):
    import zlib

    import numpy as np

    out = dict(_drawn_inputs(seed))
    spreads = {}
    factors = {'norm_ffn': 3.15,
     'a_q_norm': 4.466,
     'a_k_norm': 5.018,
     'a_out_norm': 4.832,
     'b_q_a_norm': 8.0,
     'b_kv_a_norm': 8.0,
     'b_q_nope_norm': 8.0,
     'b_q_rope_norm': 8.0,
     'b_k_nope_norm': 8.0,
     'b_k_rope_norm': 8.0}
    for name, (base, spread) in spreads.items():
        noise = np.random.default_rng([zlib.crc32(name.encode()), seed]).standard_normal(out[name].shape)
        drawn = base * np.exp(spread * noise) if base else spread * noise
        out[name] = jnp.asarray(drawn.astype(out[name].dtype))
    for name, factor in factors.items():
        out[name] = (out[name] * factor).astype(out[name].dtype)
    return out
```

```python
import math

import numpy as np

import concourse.bass as bass
from concourse import mybir

F32 = mybir.dt.float32
F32R = mybir.dt.float32r
ALU = mybir.AluOpType
ACT = mybir.ActivationFunctionType
AX = mybir.AxisListType.X

P = 128
D = 1024
SEQ = 512
KT = D // P
NB = SEQ // P
CHUNK = 64
EPS = 1e-6
THETA = 10000.0
BIG = -1e30

A_HEADS, A_DIM = 4, 64
B_HEADS, B_NOPE, B_ROPE, B_V = 8, 64, 32, 64
B_QK = B_NOPE + B_ROPE
B_QRANK, B_KVRANK = 256, 128
C_HEADS, C_DIM = 16, 64
C_PAIRS = C_HEADS // 2
D_FF = 2816
HALF_F = D_FF // P // 2
LAM0 = 0.8 - 0.6 * math.exp(-0.3 * 0)

WSLOTS = 3
W_IN = KT * P
W_DOWN = HALF_F * P
WB = 2 * B_QK + P

G_LAT = 0
G_A = G_LAT + 4
G_OUT0 = G_A + 3 * A_HEADS
G_FFN0 = G_OUT0 + KT
FFN_HALF = 2 * HALF_F + KT
G_C = G_FFN0 + 2 * FFN_HALF
G_OUT1 = G_C + 3 * C_PAIRS
G_FFN1 = G_OUT1 + KT
N_CHUNKS = G_FFN1 + 2 * FFN_HALF

SW = [max(256, (b + 1) * P) for b in range(NB)]
TQ = [min(b * P, SEQ - 256) for b in range(NB)]
TW = [SEQ - q for q in TQ]
TO = [sum(TW[:b]) for b in range(NB)]
TWS = sum(TW)

MATS = ["ident", "rot_a", "rot_b", "blk64", "blk_b", "ones"]
V_GAIN = 0
V_AQ, V_AK, V_AO, V_BQL, V_BKVL, V_BQ, V_BK, V_BKR, V_LAM, V_EPS = 32, 33, 34, 35, 37, 38, 39, 40, 41, 45
V_N = 46


def width_of(g):
    for first in (G_FFN0, G_FFN1):
        if first <= g < first + 2 * FFN_HALF and (g - first) % FFN_HALF >= 2 * HALF_F:
            return W_DOWN
    return W_IN


def trunk(nc, xt, w_in, w_b, w_down, mats, masks_a, masks_c, tabs_a, tabs_b, vecs, out, upto="all"):
    cursor = [nc.sbuf_base]
    count = [0]

    def place(name, shape, dt, at=None):
        size = 4 * int(np.prod(shape[1:]))
        off = cursor[0] if at is None else at
        off = (off + 31) // 32 * 32
        t = nc.alloc_sbuf_tensor_at(name, list(shape), dt, offset=off)
        if at is None:
            cursor[0] = off + size
        return t, off + size

    def pair(name, shape, at=None):
        a, end = place(name + "_hi", shape, F32R, at)
        b, end = place(name + "_lo", shape, F32R, None if at is None else end)
        return (a, b), end

    x, _ = place("x", [P, KT, SEQ], F32)
    wraw, _ = place("wraw", [P, WSLOTS, W_DOWN], F32)
    (whi, wlo), _ = pair("w", [P, WSLOTS, W_DOWN])
    mat, _ = place("mat", [P, len(MATS), P], F32)
    ident_r, _ = place("ident_r", [P, P], F32R)
    cmask, _ = place("cmask", [P, 2, 256], F32R)
    vec, _ = place("vec", [P, V_N], F32)
    tiny, _ = place("tiny", [P, 32], F32)
    rstd, _ = place("rstd", [P, SEQ], F32)
    h0 = cursor[0]
    (hhi, hlo), _ = pair("h", [P, KT, SEQ])
    phase0 = cursor[0]

    (mhi, mlo), _ = pair("mixed", [P, KT, SEQ])
    (qlhi, qllo), _ = pair("ql", [P, 2, SEQ])
    (kvhi, kvlo), _ = pair("kvl", [P, SEQ])
    tabb, _ = place("tabb", [P, 2, SEQ], F32)
    (qhi, qlo), _ = pair("q", [P, 2, SEQ])
    (khi, klo), _ = pair("k", [P, SEQ])
    (vhi, vlo), _ = pair("v", [P, NB, P])
    e1, _ = place("e1", [P, SEQ], F32)
    pn0 = cursor[0]
    pn, _ = place("pn", [P, NB, SEQ], F32)
    (pthi, ptlo), _ = pair("pt", [P, TWS])
    yq, _ = place("yq", [P, SEQ], F32)
    yk, _ = place("yk", [P, SEQ], F32)
    yv, _ = place("yv", [P, SEQ], F32)
    sqb, _ = place("sqb", [P, SEQ], F32)
    rsb, _ = place("rsb", [P, SEQ], F32)
    tb, _ = place("tb", [P, SEQ], F32)
    assert cursor[0] <= nc.sbuf_usable_end, cursor[0]
    taba, end = place("taba", [P, 2, SEQ], F32, at=phase0 + 4 * 4 * SEQ)
    rope_keep, end = place("rope_keep", [P, SEQ], F32, at=end)
    assert end <= phase0 + 4 * KT * SEQ
    bwraw, end = place("bwraw", [P, 2, WB], F32, at=h0)
    (bwhi, bwlo), end = pair("bw", [P, 2, WB], at=end)
    rawm, _ = place("rawm", [P, 2, 256], F32, at=pn0 + 12 * SEQ)
    sqn, end = place("sqn", [P, 2, SEQ], F32, at=pn0)
    ssum, _ = place("ssum", [P, SEQ], F32, at=end)

    (fhi, flo), end = pair("f", [P, HALF_F, SEQ], at=phase0)
    fy, end = place("fy", [P, SEQ], F32, at=end)
    fs, end = place("fs", [P, SEQ], F32, at=end)
    fu, end = place("fu", [P, SEQ], F32, at=end)
    fa, end = place("fa", [P, SEQ], F32, at=end)
    assert end <= pn0, (end, pn0)

    c0 = phase0 + 2 * 4 * KT * SEQ
    (cqhi, cqlo), end = pair("cq", [P, 2, SEQ], at=c0)
    (ckhi, cklo), end = pair("ck", [P, SEQ], at=end)
    (cvhi, cvlo), end = pair("cv", [P, NB, P], at=end)
    cyq, end = place("cyq", [P, SEQ], F32, at=end)
    cyk, end = place("cyk", [P, SEQ], F32, at=end)
    cyv, end = place("cyv", [P, SEQ], F32, at=end)
    cmats, end = place("cmats", [P, 2, P], F32R, at=end)
    csmask, end = place("csmask", [P, 2, 256], F32R, at=end)
    (cz0, cz0lo), end = pair("cs0", [P, TWS], at=end)
    (cz1, cz1lo), end = pair("cs1", [P, TWS], at=end)
    cshi, cslo = (cz0, cz1), (cz0lo, cz1lo)
    ca0, end = place("ca0", [P, TWS], F32, at=end)
    ca1, end = place("ca1", [P, TWS], F32, at=end)
    ca = (ca0, ca1)
    cs, end = place("cs", [P, TWS], F32, at=end)
    crawm, end = place("crawm", [P, 768], F32, at=end - 4 * TWS)
    assert end <= nc.sbuf_usable_end and end <= nc.sbuf_usable_end, end

    bank = [nc.alloc_psum_tensor(f"bank{i}", [P, SEQ], F32) for i in range(8)]

    sems = {}

    def S(name):
        if name not in sems:
            sems[name] = nc.alloc_semaphore(name)
        return sems[name]

    def wait(eng, name, value):
        if not isinstance(value, int) or value > 0:
            eng.wait_ge(S(name), value)

    M = {n: mat[:, i, :] for i, n in enumerate(MATS)}

    def v(col, n=1, rows=P):
        return vec[0:rows, col:col + n]

    def tile_at(t, k, rows=slice(0, P)):
        return t[rows, k, :] if isinstance(k, int) else t[rows, bass.ds(k, 1), :]

    def as3(ap, k):
        return ap if isinstance(k, int) else ap.rearrange("p (o n) -> p o n", o=1)

    def at_norm(n, what, value):
        return S("norm_" + what), value + n * {"sq": KT, "hi": KT, "lo": KT, "sum": KT - 1}.get(what, 1)

    def at_net(L, what, value):
        return S("net_" + what), value + L * 2 * (KT if what == "x" else HALF_F)

    def at_head(ph, what, value):
        a_only = {"e": 2 * NB, "mx": 2 * NB, "qlo": 2, "qhi": 2, "whi": 0, "wlo": 0, "q": 0, "kv": 0}
        of_a = A_HEADS * (NB if what in ("s", "nm", "r", "p", "tr", "phi", "plo") else a_only.get(what, 1))
        of_r = 1 if what in ("qsq", "qss", "qln", "qrs", "qt", "qrot", "qc", "qs", "qy2") else 0
        return S("head_" + what), value + (0 if ph == "r" else of_r) + (of_a if ph == "b" else 0)

    def slot(g_static):
        return g_static % WSLOTS

    def load_chunk(sp, g, s, n, src, width):
        wait(sp, "w_lo", g - (WSLOTS - 1))
        sp.dma_start(wraw[:, s, 0:width], src).then_inc(S(f"w_in{s}"), 16)

    def split_hi(act, g, s, use, width=W_IN):
        act.wait_ge(S(f"w_in{s}"), 16 * use)
        wait(act, "chunk_done", g - (WSLOTS - 1))
        nc.scalar.activation(whi[:, s, 0:width], wraw[:, s, 0:width], ACT.Copy).then_inc(S("w_hi"), 1)

    def hi_static(act, g):
        if g < N_CHUNKS:
            split_hi(act, g, slot(g), g // WSLOTS + 1, width_of(g))

    def hi_at(act, g0, i, step):
        split_hi(act, g0 + i * step, slot(g0), g0 // WSLOTS + 1 + i * (step // WSLOTS))

    def split_lo(pool, g, s, width):
        pool.wait_ge(S("w_hi"), g + 1)
        nc.gpsimd.tensor_tensor(wlo[:, s, 0:width], wraw[:, s, 0:width], whi[:, s, 0:width],
                                ALU.subtract).then_inc(S("w_lo"), 1)

    def project(pe, g, s, out_bank, src_hi, src_lo, first=None):
        n = len(src_hi)
        pe.wait_ge(S("w_hi"), g + 1)
        for kt in range(n):
            if first is not None:
                first(kt)
            w = whi[:, s, kt * P:(kt + 1) * P]
            nc.tensor.matmul(out_bank, w, src_hi[kt], start=(kt == 0), stop=False)
            nc.tensor.matmul(out_bank, w, src_lo[kt], start=False, stop=False)
        pe.wait_ge(S("w_lo"), g + 1)
        for kt in range(n):
            last = nc.tensor.matmul(out_bank, wlo[:, s, kt * P:(kt + 1) * P], src_hi[kt],
                                    start=False, stop=(kt == n - 1))
        last.then_inc(S("chunk_done"), 1)

    h_hi = [hhi[:, k, :] for k in range(KT)]
    h_lo = [hlo[:, k, :] for k in range(KT)]
    m_hi = [mhi[:, k, :] for k in range(KT)]
    m_lo = [mlo[:, k, :] for k in range(KT)]

    def norm_act(act, n, d):
        if d >= 2:
            act.wait_ge(*at_norm(n, "sum", max(1, d - 2)))
        nc.scalar.activation(sqn[:, d % 2, :], x[:, d, :], ACT.Square).then_inc(S("norm_sq"), 1)
        nc.scalar.activation(hhi[:, d, :], x[:, d, :], ACT.Copy,
                             scale=v(V_GAIN + KT * n + d)).then_inc(S("norm_hi"), 1)

    def norm_dve(dve, n, d):
        dve.wait_ge(*at_norm(n, "hi", d + 1))
        nc.vector.scalar_tensor_tensor(hlo[:, d, :], x[:, d, :], v(V_GAIN + KT * n + d), hhi[:, d, :],
                                       ALU.mult, ALU.subtract).then_inc(S("norm_lo"), 1)

    def norm_pool(pool, n, d):
        if d == 0:
            return
        pool.wait_ge(*at_norm(n, "sq", d + 1))
        if d > 1:
            pool.wait_ge(*at_norm(n, "sum", d - 1))
        nc.gpsimd.tensor_tensor(ssum[:], sqn[:, 0, :] if d == 1 else ssum[:], sqn[:, d % 2, :],
                                ALU.add).then_inc(S("norm_sum"), 1)

    def norm_pe(pe, n, b):
        pe.wait_ge(*at_norm(n, "sum", KT - 1))
        nc.tensor.matmul(bank[b][:], M["ones"], ssum[:], start=True, stop=True).then_inc(S("norm_tot"), 1)

    def rsqrt(act, dst, src, scale, summed, ln, done, rows=P):
        act.wait_ge(*summed)
        nc.scalar.activation(dst, src, ACT.Ln, bias=v(V_EPS, rows=rows), scale=scale).then_inc(ln[0], 1)
        act.wait_ge(*ln)
        nc.scalar.activation(dst, dst, ACT.Exp, scale=-0.5).then_inc(done, 1)

    def norm_rstd(act, n, b):
        rsqrt(act, rstd[:], bank[b][:], 1.0 / D, at_norm(n, "tot", 1), at_norm(n, "ln", 1), S("norm_rstd"))

    def need_h(pe, n):
        def first(kt):
            pe.wait_ge(*at_norm(n, "lo", kt + 1))
        return first

    def out_pe(pe, g0, L, heads_done):
        def need_heads(kt):
            if kt == KT - 1:
                pe.wait_ge(*heads_done)
        for d in range(KT):
            if d >= 2:
                pe.wait_ge(S("out_x"), L * KT + d - 1)
            project(pe, g0 + d, slot(g0 + d), bank[6 + d % 2][:], m_hi, m_lo, need_heads if d == 0 else None)

    def out_act(act, g0, L, n):
        for d in range(KT):
            act.wait_ge(S("out_x"), L * KT + d + 1)
            hi_static(act, g0 + d + 3)
            norm_act(act, n, d)

    def out_dve(dve, g0, L, n):
        for d in range(KT):
            dve.wait_ge(S("chunk_done"), g0 + d + 1)
            nc.vector.tensor_tensor(x[:, d, :], bank[6 + d % 2][:], x[:, d, :], ALU.add).then_inc(S("out_x"), 1)
            norm_dve(dve, n, d)

    GU_LOOP = HALF_F // 3 * 3

    def ffn_each(eng, body):
        with eng.Fori(0, GU_LOOP // 3) as i:
            for j in range(3):
                body(i * 3 + j, j)
        for f in range(GU_LOOP, HALF_F):
            body(f, f % 3)

    def ffn_pe(pe, L, n):
        g_first = (G_FFN0, G_FFN1)[L]
        for s in range(2):
            g0 = g_first + s * FFN_HALF

            def gate_up(f, j):
                for c in range(2):
                    g = f * 2 + (g0 + c)
                    sl = slot(g0 + 2 * j + c)
                    if isinstance(f, int):
                        if s or f >= 3:
                            pe.wait_ge(*at_net(L, "yu"[c], s * HALF_F + f - 2 if f >= 3 else HALF_F))
                    elif s:
                        pe.wait_ge(*at_net(L, "yu"[c], f + (HALF_F - 2)))
                    project(pe, g, sl, bank[2 * j + c][:], h_hi, h_lo)
            if s == 0:
                for f in range(3):
                    for c in range(2):
                        g = g0 + 2 * f + c
                        project(pe, g, slot(g), bank[2 * f + c][:], h_hi, h_lo,
                                need_h(pe, n) if f == 0 and c == 0 else None)
                        if f == 0 and c == 0:
                            norm_pe(pe, n, 7)
                with pe.Fori(1, GU_LOOP // 3) as i:
                    for j in range(3):
                        for c in range(2):
                            pe.wait_ge(*at_net(L, "yu"[c], i * 3 + (j - 2)))
                            project(pe, i * 6 + (g0 + 2 * j + c), slot(g0 + 2 * j + c),
                                    bank[2 * j + c][:], h_hi, h_lo)
                for f in range(GU_LOOP, HALF_F):
                    gate_up(f, f % 3)
            else:
                pe.wait_ge(*at_net(L, "x", 6))
                with pe.Fori(0, GU_LOOP // 3) as i:
                    for j in range(3):
                        for c in range(2):
                            pe.wait_ge(*at_net(L, "yu"[c], i * 3 + (j - 2 + HALF_F)))
                            project(pe, i * 6 + (g0 + 2 * j + c), slot(g0 + 2 * j + c),
                                    bank[2 * j + c][:], h_hi, h_lo)
                for f in range(GU_LOOP, HALF_F):
                    gate_up(f, f % 3)
            gd = g0 + 2 * HALF_F
            f_hi = [fhi[:, k, :] for k in range(HALF_F)]
            f_lo = [flo[:, k, :] for k in range(HALF_F)]

            def need_f(kt):
                pe.wait_ge(*at_net(L, "lo", s * HALF_F + kt + 1))
            down_banks = (6, 7, 0)
            for d in range(3):
                if s:
                    pe.wait_ge(*at_net(L, "x", KT))
                project(pe, gd + d, slot(gd + d), bank[down_banks[d]][:], f_hi, f_lo,
                        need_f if d == 0 else None)
            for d in range(3, KT):
                pe.wait_ge(*at_net(L, "x", s * KT + d - 2))
                project(pe, gd + d, slot(gd + d), bank[down_banks[d % 3]][:], f_hi, f_lo)

    def ffn_act(act, L, n_next):
        g_first = (G_FFN0, G_FFN1)[L]
        for s in range(2):
            g0 = g_first + s * FFN_HALF

            def tile(i, j):
                f = i * 3 + j

                def split_ahead(c):
                    g = g0 + 2 * j + c
                    split_hi(act, i * 6 + g, slot(g), i * 2 + (g // WSLOTS + 1),
                             width_of(i * 6 + g) if isinstance(i, int) else W_IN)
                act.wait_ge(*at_net(L, "y", f + (s * HALF_F + 1)))
                nc.scalar.activation(fs[:], fy[:], ACT.Silu).then_inc(S("net_s"), 1)
                split_ahead(3)
                act.wait_ge(*at_net(L, "a", f + (s * HALF_F + 1)))
                nc.scalar.activation(tile_at(fhi, f), as3(fa[:], f), ACT.Copy).then_inc(S("net_hi"), 1)
                split_ahead(4)
            with act.Fori(0, GU_LOOP // 3) as i:
                for j in range(3):
                    tile(i, j)
            for f in range(GU_LOOP, HALF_F):
                tile(GU_LOOP // 3, f - GU_LOOP)
            for d in range(KT):
                act.wait_ge(*at_net(L, "x", s * KT + d + 1))
                hi_static(act, g0 + 2 * HALF_F + d + 3)
                if s and n_next is not None:
                    norm_act(act, n_next, d)

    def ffn_dve(dve, L, n, n_next):
        g_first = (G_FFN0, G_FFN1)[L]
        dve.wait_ge(*at_norm(n, "rstd", 1))
        for s in range(2):
            g0 = g_first + s * FFN_HALF

            def tile(f, j):
                dve.wait_ge(S("chunk_done"), f * 2 + (g0 + 1))
                nc.vector.tensor_tensor(fy[:], bank[2 * j][:], rstd[:], ALU.mult).then_inc(S("net_y"), 1)
                dve.wait_ge(S("chunk_done"), f * 2 + (g0 + 2))
                nc.vector.tensor_tensor(fu[:], bank[2 * j + 1][:], rstd[:], ALU.mult).then_inc(S("net_u"), 1)
                dve.wait_ge(*at_net(L, "u", f + (s * HALF_F + 1)))
                dve.wait_ge(*at_net(L, "s", f + (s * HALF_F + 1)))
                nc.vector.tensor_tensor(fa[:], fu[:], fs[:], ALU.mult).then_inc(S("net_a"), 1)
                dve.wait_ge(*at_net(L, "hi", f + (s * HALF_F + 1)))
                nc.vector.tensor_tensor(tile_at(flo, f), as3(fa[:], f), tile_at(fhi, f),
                                        ALU.subtract).then_inc(S("net_lo"), 1)
            ffn_each(dve, tile)
            gd = g0 + 2 * HALF_F
            for d in range(KT):
                dve.wait_ge(S("chunk_done"), gd + d + 1)
                if s:
                    dve.wait_ge(*at_net(L, "x", KT))
                b = bank[(6, 7, 0)[d % 3]]
                nc.vector.tensor_tensor(x[:, d, :], b[:], x[:, d, :], ALU.add).then_inc(S("net_x"), 1)
                if s and n_next is not None:
                    norm_dve(dve, n_next, d)

    def scores_pe(pe, ph, u, b):
        sub = 2 if ph == "a" else 1
        if b == 0:
            pe.wait_ge(*at_head(ph, "qlo", u * sub + sub))
            pe.wait_ge(*at_head(ph, "klo", u + 1))
        if b >= 3 - sub:
            pe.wait_ge(*at_head(ph, "e", u * (NB * sub) + sub * (b if sub == 2 else b - 1)))
        w = SW[b]
        rows = P if ph == "a" else B_QK
        for j in range(sub):
            o = bank[j if sub == 2 else b % 2]
            for n, (a, c) in enumerate(((qhi, khi), (qhi, klo), (qlo, khi))):
                nc.tensor.matmul(o[:, 0:w], a[0:rows, j, b * P:(b + 1) * P], c[0:rows, 0:w],
                                 start=(n == 0), stop=False)
            last = nc.tensor.matmul(o[:, w - 256:w], ident_r[:], cmask[:, 0 if b == 0 else 1, :],
                                    start=False, stop=True)
        last.then_inc(S("head_s"), 1)

    T_MX, T_NM, T_L, T_R, T_RL = 0, 2, 4, 6, 8

    def softmax_dve(dve, ph, u, b, scale):
        sub = 2 if ph == "a" else 1
        w = SW[b]
        n = u * NB + (b + 1)
        dve.wait_ge(*at_head(ph, "s", n))
        for j in range(sub):
            o = bank[j if sub == 2 else b % 2]
            nc.vector.reduce_max(tiny[:, T_MX + j:T_MX + j + 1], o[:, 0:w], AX).then_inc(S("head_mx"), 1)
        dve.wait_ge(*at_head(ph, "mx", n * sub))
        nc.vector.tensor_scalar(tiny[:, T_NM:T_NM + sub], tiny[:, T_MX:T_MX + sub], -scale, None,
                                ALU.mult).then_inc(S("head_nm"), 1)

    def softmax_act(act, ph, u, b, scale):
        sub = 2 if ph == "a" else 1
        w = SW[b]
        act.wait_ge(*at_head(ph, "nm", u * NB + (b + 1)))
        for j in range(sub):
            o = bank[j if sub == 2 else b % 2]
            dst = pn[:, b, 0:w] if j == 0 else e1[:, 0:w]
            nc.scalar.activation(dst, o[:, 0:w], ACT.Exp, bias=tiny[:, T_NM + j:T_NM + j + 1],
                                 scale=scale, accum_out=tiny[:, T_L + j:T_L + j + 1]).then_inc(S("head_e"), 1)

    def probs_dve(dve, ph, u, b):
        sub = 2 if ph == "a" else 1
        w = SW[b]
        n = u * NB + (b + 1)
        dve.wait_ge(*at_head(ph, "e", n * sub))
        nc.vector.reciprocal(tiny[:, T_R:T_R + sub], tiny[:, T_L:T_L + sub]).then_inc(S("head_r"), 1)
        dve.wait_ge(*at_head(ph, "r", n))
        if sub == 2:
            nc.vector.tensor_tensor(tiny[:, T_RL:T_RL + 1], tiny[:, T_R + 1:T_R + 2],
                                    tiny[:, 16:17], ALU.mult).then_inc(S("head_rl"), 1)
            dve.wait_ge(*at_head(ph, "rl", n))
            nc.vector.tensor_scalar(e1[:, 0:w], e1[:, 0:w], tiny[:, T_RL:T_RL + 1], None,
                                    ALU.mult).then_inc(S("head_e1"), 1)
            dve.wait_ge(*at_head(ph, "e1", n))
            nc.vector.scalar_tensor_tensor(pn[:, b, 0:w], pn[:, b, 0:w], tiny[:, T_R:T_R + 1], e1[:, 0:w],
                                           ALU.mult, ALU.subtract).then_inc(S("head_p"), 1)
        else:
            nc.vector.tensor_scalar(pn[:, b, 0:w], pn[:, b, 0:w], tiny[:, T_R:T_R + 1], None,
                                    ALU.mult).then_inc(S("head_p"), 1)

    TRB = (5, 6)
    OB = 7
    MMB = 4

    def ptrans_pe(pe, ph, u, kb):
        if kb == 0:
            pe.wait_ge(*at_head(ph, "p", u * NB + NB))
            pe.wait_ge(*at_head(ph, "vlo", u + 1))
        if kb >= 2:
            pe.wait_ge(*at_head(ph, "plo", u * NB + (kb - 1)))
        for b in range(kb, NB):
            last = nc.tensor.transpose(bank[TRB[kb % 2]][:, b * P:(b + 1) * P], pn[:, b, kb * P:(kb + 1) * P],
                                       M["ident"])
        last.then_inc(S("head_tr"), 1)

    def pt_slice(t, kb):
        return t[:, TO[kb] + TW[kb] - (SEQ - kb * P):TO[kb] + TW[kb]]

    def ptrans_act(act, ph, u, kb):
        act.wait_ge(*at_head(ph, "tr", u * NB + (kb + 1)))
        nc.scalar.activation(pt_slice(pthi, kb), bank[TRB[kb % 2]][:, kb * P:SEQ], ACT.Copy).then_inc(S("head_phi"), 1)

    def ptrans_dve(dve, ph, u, kb):
        dve.wait_ge(*at_head(ph, "phi", u * NB + (kb + 1)))
        nc.vector.tensor_tensor(pt_slice(ptlo, kb), bank[TRB[kb % 2]][:, kb * P:SEQ], pt_slice(pthi, kb),
                                ALU.subtract).then_inc(S("head_plo"), 1)

    def values_pe(pe, ph, u, kb):
        pe.wait_ge(*at_head(ph, "plo", u * NB + (kb + 1)))
        dv = P if ph == "a" else B_V
        for n, (a, c) in enumerate(((vhi, pthi), (vhi, ptlo), (vlo, pthi))):
            last = nc.tensor.matmul(bank[OB][0:dv, TQ[kb]:SEQ], a[:, kb, 0:dv], c[:, TO[kb]:TO[kb] + TW[kb]],
                                    start=(kb == 0 and n == 0), stop=(kb == NB - 1 and n == 2))
        if kb == NB - 1:
            last.then_inc(S("head_o"), 1)

    def attn_tail_pe(pe, ph, u):
        ptrans_pe(pe, ph, u, 0)
        ptrans_pe(pe, ph, u, 1)
        values_pe(pe, ph, u, 0)
        ptrans_pe(pe, ph, u, 2)
        values_pe(pe, ph, u, 1)
        ptrans_pe(pe, ph, u, 3)
        values_pe(pe, ph, u, 2)
        values_pe(pe, ph, u, 3)

    def vtrans_pe(pe, ph, u):
        pe.wait_ge(*at_head(ph, "vy", u + 1))
        for b in range(NB):
            last = nc.tensor.transpose(bank[TRB[0]][:, b * P:(b + 1) * P], yv[:, b * P:(b + 1) * P], M["ident"])
        last.then_inc(S("head_vt"), 1)

    def v_parts(ph, t):
        dv, at = (P, 0) if ph == "a" else (B_V, P - B_V)
        src = bank[TRB[0]][:].rearrange("p (b n) -> p b n", n=P)[:, :, at:at + dv]
        return t[:, :, 0:dv], src

    def v_act(act, ph, u):
        act.wait_ge(*at_head(ph, "vt", u + 1))
        o, i = v_parts(ph, vhi)
        nc.scalar.activation(o, i, ACT.Copy).then_inc(S("head_vhi"), 1)

    def v_dve(dve, ph, u):
        dve.wait_ge(*at_head(ph, "vhi", u + 1))
        o, i = v_parts(ph, vlo)
        nc.vector.tensor_tensor(o, i, v_parts(ph, vhi)[0], ALU.subtract).then_inc(S("head_vlo"), 1)

    def a_out_pe(pe, u):
        pe.wait_ge(*at_head("a", "osq", u + 1))
        nc.tensor.matmul(bank[MMB][:], M["ones"], sqb[:], start=True, stop=True).then_inc(S("head_oss"), 1)

    def a_out_act(act, u):
        act.wait_ge(*at_head("a", "o", u + 1))
        nc.scalar.activation(sqb[:], bank[OB][:], ACT.Square).then_inc(S("head_osq"), 1)
        rsqrt(act, rsb[:], bank[MMB][:], 1.0 / (2 * A_DIM), at_head("a", "oss", u + 1),
              at_head("a", "oln", u + 1), S("head_ors"))
        act.wait_ge(*at_head("a", "on", u + 1))
        nc.scalar.activation(tile_at(mhi, u), as3(tb[:], u), ACT.Copy).then_inc(S("head_mhi"), 1)

    def a_out_dve(dve, u):
        dve.wait_ge(*at_head("a", "ors", u + 1))
        nc.vector.scalar_tensor_tensor(tb[:], bank[OB][:], tiny[:, 17:18], rsb[:], ALU.mult,
                                       ALU.mult).then_inc(S("head_on"), 1)
        dve.wait_ge(*at_head("a", "mhi", u + 1))
        nc.vector.tensor_tensor(tile_at(mlo, u), as3(tb[:], u), tile_at(mhi, u),
                                ALU.subtract).then_inc(S("head_mlo"), 1)
        dve.wait_ge(*at_head("a", "mlo", u + 1))

    def qk_ssq_pe(pe, ph, t, u, rows, m):
        pe.wait_ge(*at_head(ph, t + "sq", u + 1))
        nc.tensor.matmul(bank[MMB][0:rows, :], M[m][0:rows, 0:rows], sqb[0:rows, :], start=True,
                         stop=True).then_inc(S(f"head_{t}ss"), 1)

    def qk_rot_pe(pe, ph, t, u, rows, m):
        pe.wait_ge(*at_head(ph, t + "t", u + 1))
        nc.tensor.matmul(bank[MMB][0:rows, :], M[m][0:rows, 0:rows], tb[0:rows, :], start=True,
                         stop=True).then_inc(S(f"head_{t}rot"), 1)

    def qk_rs_act(act, ph, t, u, rows, scale):
        rsqrt(act, rsb[0:rows, :], bank[MMB][0:rows, :], scale, at_head(ph, t + "ss", u + 1),
              at_head(ph, t + "ln", u + 1), S(f"head_{t}rs"), rows)

    def qk_t_dve(dve, ph, t, u, rows, src, gain):
        dve.wait_ge(*at_head(ph, t + "rs", u + 1))
        nc.vector.scalar_tensor_tensor(tb[0:rows, :], src, gain, rsb[0:rows, :], ALU.mult,
                                       ALU.mult).then_inc(S(f"head_{t}t"), 1)

    def qk_rope_dve(dve, ph, t, u, rows, y, tab):
        dve.wait_ge(*at_head(ph, t + "t", u + 1))
        nc.vector.tensor_tensor(y[0:rows, :], tb[0:rows, :], tab[0:rows, 0, :], ALU.mult).then_inc(S(f"head_{t}c"), 1)
        dve.wait_ge(*at_head(ph, t + "rot", u + 1))
        dve.wait_ge(*at_head(ph, t + "c", u + 1))
        nc.vector.tensor_tensor(tb[0:rows, :], bank[MMB][0:rows, :], tab[0:rows, 1, :], ALU.mult).then_inc(S(f"head_{t}s"), 1)
        dve.wait_ge(*at_head(ph, t + "s", u + 1))
        nc.vector.tensor_tensor(y[0:rows, :], y[0:rows, :], tb[0:rows, :], ALU.add).then_inc(S(f"head_{t}y2"), 1)
        dve.wait_ge(*at_head(ph, t + "y2", u + 1))

    PJ = (2, 3)

    def a_proj_pe(pe, u, t):
        c = "qkv".index(t)
        g = u * 3 + (G_A + c)
        if t == "q" and not (isinstance(u, int) and u == 0):
            pe.wait_ge(*at_head("a", "vy", u))
        if t == "v":
            pe.wait_ge(*at_head("a", "qy", u + 1))
        project(pe, g, slot(G_A + c), bank[PJ[c % 2]][:], h_hi, h_lo)

    def a_y_dve(dve, u, t):
        c = "qkv".index(t)
        dve.wait_ge(S("chunk_done"), u * 3 + (G_A + c + 1))
        y = (yq, yk, yv)[c]
        nc.vector.tensor_tensor(y[:], bank[PJ[c % 2]][:], rstd[:], ALU.mult).then_inc(S(f"head_{t}y"), 1)

    def a_sq_act(act, u, t):
        act.wait_ge(*at_head("a", t + "y", u + 1))
        nc.scalar.activation(sqb[:], (yq, yk)["qk".index(t)][:], ACT.Square).then_inc(S(f"head_{t}sq"), 1)

    def a_slots_act(act, u):
        act.wait_ge(*at_head("a", "qy2", u + 1))
        if not (isinstance(u, int) and u == 0):
            act.wait_ge(*at_head("a", "s", u * NB))
        for j in range(2):
            r = slice(64 * j, 64 * j + 64)
            nc.scalar.activation(qhi[r, j, :], yq[r, :], ACT.Copy).then_inc(S("head_qhi"), 1)
        act.wait_ge(*at_head("a", "ky2", u + 1))
        nc.scalar.activation(khi[:], yk[:], ACT.Copy).then_inc(S("head_khi"), 1)

    def a_slots_dve(dve, u):
        dve.wait_ge(*at_head("a", "qhi", u * 2 + 2))
        for j in range(2):
            r = slice(64 * j, 64 * j + 64)
            nc.vector.tensor_tensor(qlo[r, j, :], yq[r, :], qhi[r, j, :], ALU.subtract).then_inc(S("head_qlo"), 1)
        dve.wait_ge(*at_head("a", "khi", u + 1))
        nc.vector.tensor_tensor(klo[:], yk[:], khi[:], ALU.subtract).then_inc(S("head_klo"), 1)

    A_SCALE = A_DIM ** -0.5
    B_SCALE = B_QK ** -0.5

    def b_load(sp, u, s):
        src = w_b[u, :, :] if isinstance(u, int) else w_b[bass.ds(u, 1), :, :].rearrange("o p n -> p (o n)")
        sp.dma_start(bwraw[:, s, :], src).then_inc(S(f"b_in{s}"), 16)

    def b_hi_act(act, u, s, use):
        act.wait_ge(S(f"b_in{s}"), 16 * use if isinstance(use, int) else use * 16)
        nc.scalar.activation(bwhi[:, s, :], bwraw[:, s, :], ACT.Copy).then_inc(S("head_whi"), 1)

    def b_lo_pool(pool, u, s):
        pool.wait_ge(*at_head("b", "whi", u + 1))
        nc.gpsimd.tensor_tensor(bwlo[:, s, :], bwraw[:, s, :], bwhi[:, s, :], ALU.subtract).then_inc(S("head_wlo"), 1)

    def b_proj_pe(pe, u, s):
        pe.wait_ge(*at_head("b", "wlo", u + 1))
        n = 0
        for kt in range(2):
            c = slice(kt * B_QK, (kt + 1) * B_QK)
            for a, o in ((bwhi, qlhi), (bwhi, qllo), (bwlo, qlhi)):
                last = nc.tensor.matmul(bank[PJ[0]][0:B_QK, :], a[:, s, c], o[:, kt, :], start=(n == 0), stop=(n == 5))
                n += 1
        last.then_inc(S("head_q"), 1)
        for n, (a, o) in enumerate(((bwhi, kvhi), (bwhi, kvlo), (bwlo, kvhi))):
            last = nc.tensor.matmul(bank[PJ[1]][:], a[:, s, 2 * B_QK:], o[:], start=(n == 0), stop=(n == 2))
        last.then_inc(S("head_kv"), 1)

    def b_prep_pe(pe, u):
        qk_ssq_pe(pe, "b", "q", u, B_QK, "blk_b")
        qk_rot_pe(pe, "b", "q", u, B_QK, "rot_b")
        pe.wait_ge(*at_head("b", "qs", u + 1))
        qk_ssq_pe(pe, "b", "k", u, P, "blk64")

    def b_prep_act(act, u, part):
        if part == 0:
            act.wait_ge(*at_head("b", "q", u + 1))
            nc.scalar.activation(sqb[0:B_QK, :], bank[PJ[0]][0:B_QK, :], ACT.Square).then_inc(S("head_qsq"), 1)
            act.wait_ge(*at_head("b", "kv", u + 1))
            nc.scalar.activation(yv[:], bank[PJ[1]][:], ACT.Copy).then_inc(S("head_vy"), 1)
            qk_rs_act(act, "b", "q", u, B_QK, 1.0)
        else:
            nc.scalar.activation(sqb[:], bank[PJ[1]][:], ACT.Square).then_inc(S("head_ksq"), 1)
            qk_rs_act(act, "b", "k", u, P, 1.0 / B_NOPE)

    def b_prep_dve(dve, u, part):
        if part == 0:
            qk_t_dve(dve, "b", "q", u, B_QK, bank[PJ[0]][0:B_QK, :], v(V_BQ, rows=B_QK))
            qk_rope_dve(dve, "b", "q", u, B_QK, yq, tabb)
        else:
            dve.wait_ge(*at_head("b", "krs", u + 1))
            nc.vector.scalar_tensor_tensor(yk[0:B_NOPE, :], bank[PJ[1]][0:B_NOPE, :], v(V_BK, rows=B_NOPE),
                                           rsb[0:B_NOPE, :], ALU.mult, ALU.mult).then_inc(S("head_ky2"), 1)

    def b_slots_act(act, u):
        act.wait_ge(*at_head("b", "qy2", u + 1))
        act.wait_ge(*at_head("b", "s", u * NB))
        nc.scalar.activation(qhi[0:B_QK, 0, :], yq[0:B_QK, :], ACT.Copy).then_inc(S("head_qhi"), 1)
        act.wait_ge(*at_head("b", "ky2", u + 1))
        nc.scalar.activation(khi[0:B_NOPE, :], yk[0:B_NOPE, :], ACT.Copy).then_inc(S("head_khi"), 1)

    def b_slots_dve(dve, u):
        dve.wait_ge(*at_head("b", "qhi", u + 1))
        nc.vector.tensor_tensor(qlo[0:B_QK, 0, :], yq[0:B_QK, :], qhi[0:B_QK, 0, :], ALU.subtract).then_inc(S("head_qlo"), 1)
        dve.wait_ge(*at_head("b", "khi", u + 1))
        nc.vector.tensor_tensor(klo[0:B_NOPE, :], yk[0:B_NOPE, :], khi[0:B_NOPE, :], ALU.subtract).then_inc(S("head_klo"), 1)

    def head_out_act(act, ph, u, j, k):
        act.wait_ge(*at_head(ph, "o", u + 1))
        nc.scalar.activation(tile_at(mhi, k, slice(64 * j, 64 * j + 64)), as3(bank[OB][0:64, :], k),
                             ACT.Copy).then_inc(S("head_mhi"), 1)

    def head_out_dve(dve, ph, u, j, k):
        dve.wait_ge(*at_head(ph, "mhi", u + 1))
        r = slice(64 * j, 64 * j + 64)
        nc.vector.tensor_tensor(tile_at(mlo, k, r), as3(bank[OB][0:64, :], k), tile_at(mhi, k, r),
                                ALU.subtract).then_inc(S("head_mlo"), 1)

    ZB = ((0, 1, 2), (3, 4, 5))
    CP, CO = 6, 7
    ZAT = ((0, 0), (1, 0), (2, 0), (2, 256))
    BW = (512, 384, 512)
    BO = (0, 512, 896)

    def c_proj_pe(pe, u, t, n=None):
        c = "qkv".index(t)
        if not (isinstance(u, int) and u == 0 and t == "q"):
            if t == "q":
                pe.wait_ge(S("c_vy"), u)
            else:
                pe.wait_ge(S("c_qy" if t == "k" else "c_ky"), u + 1)
        project(pe, u * 3 + (G_C + c), slot(G_C + c), bank[CP][:], h_hi, h_lo, n)

    def c_scores_pe(pe, u, j):
        if j == 0:
            pe.wait_ge(S("c_qlo"), u * 2 + 2)
            pe.wait_ge(S("c_klo"), u + 1)
        for kb in range(NB):
            b, o = ZAT[kb]
            z = bank[ZB[j][b]][:, o:o + TW[kb]]
            for n, (a, c) in enumerate(((ckhi, cqhi), (ckhi, cqlo), (cklo, cqhi))):
                nc.tensor.matmul(z, a[:, kb * P:(kb + 1) * P], c[:, j, TQ[kb]:SEQ],
                                 start=(n == 0 and kb < 3), stop=False, skip_group_check=True)
            last = nc.tensor.matmul(z[:, 0:256], ident_r[:], csmask[:, 1 if kb == 3 else 0, :], start=False,
                                    stop=True, skip_group_check=True)
            if kb != 2:
                last.then_inc(S(f"c_z{j}"), 1)

    def c_chain_act(act, u, j, b):
        z, a = bank[ZB[j][b]][:, 0:BW[b]], ca[j][:, BO[b]:BO[b] + BW[b]]
        n = u * 3 + (b + 1)
        act.wait_ge(S(f"c_z{j}"), n)
        nc.scalar.activation(a, z, ACT.Abs).then_inc(S(f"c_abs{j}"), 1)
        act.wait_ge(S(f"c_abs{j}"), n)
        nc.scalar.activation(a, a, ACT.Exp, scale=-1.0).then_inc(S(f"c_ex{j}"), 1)
        act.wait_ge(S(f"c_ex{j}"), n)
        nc.scalar.activation(a, a, ACT.Ln, bias=1.0).then_inc(S(f"c_ln{j}"), 1)

    def c_chain_dve(dve, u, j, b):
        z = bank[ZB[j][b]][:, 0:BW[b]]
        r = slice(BO[b], BO[b] + BW[b])
        n = u * 3 + (b + 1)
        dve.wait_ge(S(f"c_ln{j}"), n)
        nc.vector.scalar_tensor_tensor(cs[:, r], z, 0.0, ca[j][:, r], ALU.max, ALU.add).then_inc(S(f"c_sp{j}"), 1)
        dve.wait_ge(S(f"c_sp{j}"), n)
        nc.vector.tensor_copy(cshi[j][:, r], cs[:, r]).then_inc(S(f"c_shi{j}"), 1)
        dve.wait_ge(S(f"c_shi{j}"), n)
        nc.vector.tensor_tensor(cslo[j][:, r], cs[:, r], cshi[j][:, r], ALU.subtract).then_inc(S(f"c_slo{j}"), 1)

    def c_tail_pe(pe, u, j):
        pe.wait_ge(S(f"c_slo{j}"), u * 3 + 3)
        for kb in range(NB):
            b, o = ZAT[kb]
            for src in range(kb, NB):
                w = TW[src]
                z = bank[ZB[j][b]][:, o + TW[kb] - w:o + TW[kb]]
                for t in (cshi, cslo):
                    last = nc.tensor.matmul(z, cmats[:, 0 if src == kb else 1, :], t[j][:, TO[src]:TO[src] + w],
                                            start=False, stop=True, skip_group_check=True)
            if kb != 2:
                last.then_inc(S(f"c_tail{j}"), 1)

    def c_w_act(act, u, j, b):
        act.wait_ge(S(f"c_tail{j}"), u * 3 + (b + 1))
        a = ca[j][:, BO[b]:BO[b] + BW[b]]
        nc.scalar.activation(a, bank[ZB[j][b]][:, 0:BW[b]], ACT.Exp).then_inc(S(f"c_w{j}"), 1)

    def c_w_dve(dve, u, j, b):
        r = slice(BO[b], BO[b] + BW[b])
        n = u * 3 + (b + 1)
        dve.wait_ge(S(f"c_w{j}"), n)
        if b == 0:
            dve.wait_ge(S(f"c_tail{j}"), u * 3 + 3)
        nc.vector.tensor_copy(cshi[j][:, r], ca[j][:, r]).then_inc(S(f"c_whi{j}"), 1)
        dve.wait_ge(S(f"c_whi{j}"), n)
        nc.vector.tensor_tensor(cslo[j][:, r], ca[j][:, r], cshi[j][:, r], ALU.subtract).then_inc(S(f"c_wlo{j}"), 1)

    def c_values_pe(pe, u, j):
        if j == 0:
            pe.wait_ge(S("c_vlo"), u + 1)
        else:
            pe.wait_ge(S("c_mlo"), u * 2 + 1)
        for kb in range(NB):
            if kb < 3:
                pe.wait_ge(S(f"c_wlo{j}"), u * 3 + (kb + 1))
            for n, (a, c) in enumerate(((cvhi, cshi), (cvhi, cslo), (cvlo, cshi))):
                last = nc.tensor.matmul(bank[CO][0:64, TQ[kb]:SEQ], a[:, kb, 64 * j:64 * j + 64],
                                        c[j][:, TO[kb]:TO[kb] + TW[kb]], start=(kb == 0 and n == 0),
                                        stop=(kb == NB - 1 and n == 2))
        last.then_inc(S("c_o"), 1)

    def c_y_dve(dve, u, t):
        c = "qkv".index(t)
        dve.wait_ge(S("chunk_done"), u * 3 + (G_C + c + 1))
        y = (cyq, cyk, cyv)[c]
        if t == "q":
            nc.vector.scalar_tensor_tensor(y[:], bank[CP][:], C_DIM ** -0.5, rstd[:], ALU.mult,
                                           ALU.mult).then_inc(S("c_qy"), 1)
        else:
            nc.vector.tensor_tensor(y[:], bank[CP][:], rstd[:], ALU.mult).then_inc(S(f"c_{t}y"), 1)

    def c_slot_act(act, u, t):
        act.wait_ge(S(f"c_{t}y"), u + 1)
        if t == "k":
            nc.scalar.activation(ckhi[:], cyk[:], ACT.Copy).then_inc(S("c_khi"), 1)
        else:
            for j in range(2):
                r = slice(64 * j, 64 * j + 64)
                nc.scalar.activation(cqhi[r, j, :], cyq[r, :], ACT.Copy).then_inc(S("c_qhi"), 1)

    def c_slot_dve(dve, u, t):
        if t == "k":
            dve.wait_ge(S("c_khi"), u + 1)
            nc.vector.tensor_tensor(cklo[:], cyk[:], ckhi[:], ALU.subtract).then_inc(S("c_klo"), 1)
        else:
            dve.wait_ge(S("c_qhi"), u * 2 + 2)
            for j in range(2):
                r = slice(64 * j, 64 * j + 64)
                nc.vector.tensor_tensor(cqlo[r, j, :], cyq[r, :], cqhi[r, j, :], ALU.subtract).then_inc(S("c_qlo"), 1)

    def c_vt_pe(pe, u):
        pe.wait_ge(S("c_vy"), u + 1)
        for b in range(NB):
            last = nc.tensor.transpose(bank[CO][:, b * P:(b + 1) * P], cyv[:, b * P:(b + 1) * P], M["ident"])
        last.then_inc(S("c_vt"), 1)

    def c_v_act(act, u):
        act.wait_ge(S("c_vt"), u + 1)
        nc.scalar.activation(cvhi[:], bank[CO][:].rearrange("p (b n) -> p b n", n=P), ACT.Copy).then_inc(S("c_vhi"), 1)

    def c_v_dve(dve, u):
        dve.wait_ge(S("c_vhi"), u + 1)
        nc.vector.tensor_tensor(cvlo[:], bank[CO][:].rearrange("p (b n) -> p b n", n=P), cvhi[:],
                                ALU.subtract).then_inc(S("c_vlo"), 1)

    with nc.Block() as block:

        @block.sync
        def _(sp):
            for d in range(KT):
                sp.dma_start(x[:, d, :], xt[d, :, :]).then_inc(S(f"x_in{d}"), 16)
                if d == 0:
                    load_chunk(sp, 0, 0, 1, w_in[0, :, :], W_IN)
                if d == 3:
                    load_chunk(sp, 1, 1, 1, w_in[1, :, :], W_IN)
            load_chunk(sp, 2, 2, 1, w_in[2, :, :], W_IN)

            def run(g0, n, src, first, width):
                loops = n // WSLOTS
                if loops > 1:
                    with sp.Fori(0, loops) as i:
                        for j in range(WSLOTS):
                            load_chunk(sp, i * WSLOTS + (g0 + j), slot(g0 + j), None,
                                       src[bass.ds(i * WSLOTS + (first + j), 1), :, :].rearrange("o p n -> p (o n)"),
                                       width)
                else:
                    loops = 0
                for k in range(loops * WSLOTS, n):
                    load_chunk(sp, g0 + k, slot(g0 + k), None, src[first + k, :, :], width)

            run(3, G_OUT0, w_in, 3, W_IN)
            sp.wait_ge(S("chunk_done"), G_OUT0)
            for u in range(2):
                b_load(sp, u, u)
            with sp.Fori(1, B_HEADS // 2) as i:
                for s in range(2):
                    sp.wait_ge(*at_head("b", "wlo", i * 2 + (s - 1)))
                    b_load(sp, i * 2 + s, s)
            run(G_OUT0 + 3, KT - 3, w_in, G_OUT0 + 3, W_IN)
            sp.wait_ge(S("chunk_done"), G_OUT0 + 1)
            sp.dma_start(crawm[:], masks_c[:, :]).then_inc(S("crawm_in"), 16)
            row, down = G_OUT0 + KT, 0
            for s in range(2):
                run(G_FFN0 + s * FFN_HALF, 2 * HALF_F, w_in, row, W_IN)
                row += 2 * HALF_F
                run(G_FFN0 + s * FFN_HALF + 2 * HALF_F, KT, w_down, down, W_DOWN)
                down += KT
            run(G_C, 3 * C_PAIRS, w_in, row, W_IN)
            row += 3 * C_PAIRS
            run(G_OUT1, KT, w_in, row, W_IN)
            row += KT
            for s in range(2):
                run(G_FFN1 + s * FFN_HALF, 2 * HALF_F, w_in, row, W_IN)
                row += 2 * HALF_F
                run(G_FFN1 + s * FFN_HALF + 2 * HALF_F, KT, w_down, down, W_DOWN)
                down += KT
            for d in range(KT):
                sp.wait_ge(*at_net(1, "x", KT + d + 1))
                sp.dma_start(out[d, :, :], x[:, d, :]).then_inc(S("out"), 16)
            sp.wait_ge(S("out"), 16 * KT)

        @block.gpsimd
        def _(pool):
            def run(g0, n, width):
                loops = n // WSLOTS
                if loops > 1:
                    with pool.Fori(0, loops) as i:
                        for j in range(WSLOTS):
                            split_lo(pool, i * WSLOTS + (g0 + j), slot(g0 + j), width)
                else:
                    loops = 0
                for k in range(loops * WSLOTS, n):
                    split_lo(pool, g0 + k, slot(g0 + k), width)

            split_lo(pool, 0, 0, W_IN)
            for d in range(1, KT):
                norm_pool(pool, 0, d)
                if d in (3, 6):
                    split_lo(pool, d // 3, d // 3, W_IN)
            run(3, G_OUT0, W_IN)
            for s in range(2):
                b_lo_pool(pool, s, s)
            with pool.Fori(1, B_HEADS // 2) as i:
                for s in range(2):
                    b_lo_pool(pool, i * 2 + s, s)
            for d in range(KT):
                split_lo(pool, G_OUT0 + d + 3, slot(G_OUT0 + d + 3), width_of(G_OUT0 + d + 3))
                norm_pool(pool, 1, d)
            for L, g_first in ((0, G_FFN0), (1, G_FFN1)):
                run(g_first + 3, 2 * HALF_F - 3, W_IN)
                run(g_first + 2 * HALF_F, KT, W_DOWN)
                run(g_first + FFN_HALF, 2 * HALF_F, W_IN)
                gd = g_first + FFN_HALF + 2 * HALF_F
                run(gd, 3, W_DOWN)
                for d in range(KT):
                    if gd + d + 3 < N_CHUNKS:
                        split_lo(pool, gd + d + 3, slot(gd + d + 3), width_of(gd + d + 3))
                    if L == 0:
                        norm_pool(pool, 2, d)
                if L == 0:
                    run(G_C + 3, 3 * C_PAIRS - 3, W_IN)
                    run(G_OUT1, 3, W_IN)
                    for d in range(KT):
                        split_lo(pool, G_OUT1 + d + 3, slot(G_OUT1 + d + 3), width_of(G_OUT1 + d + 3))
                        norm_pool(pool, 3, d)

        @block.scalar
        def _(act):
            act.dma_start(vec[:], vecs[:, :]).then_inc(S("vec_in"), 16)
            act.dma_start(mat[:], mats[:, :, :]).then_inc(S("mat_in"), 16)
            act.dma_start(rawm[:], masks_a[:, :, :]).then_inc(S("masks_in"), 16)
            act.dma_start(tabb[:], tabs_b[:, :, :]).then_inc(S("tabb_in"), 16)
            act.dma_start(taba[:], tabs_a[:, :, :]).then_inc(S("taba_in"), 16)
            act.wait_ge(S("vec_in"), 16)
            for d in range(KT):
                act.wait_ge(S(f"x_in{d}"), 16)
                norm_act(act, 0, d)
                if d in (0, 3, 6):
                    hi_static(act, d // 3)
            act.wait_ge(S("lam_sum"), 1)
            nc.scalar.activation(tiny[:, 12:14], bank[MMB][:, 0:2], ACT.Exp).then_inc(S("lam_exp"), 1)
            norm_rstd(act, 0, MMB)
            hi_static(act, 3)
            for c in range(3):
                act.wait_ge(S("l_y"), c + 1)
                if c == 0:
                    nc.scalar.activation(sqb[:], yq[:], ACT.Square).then_inc(S("l_sq"), 1)
                if c == 1:
                    nc.scalar.activation(tb[:], yk[:], ACT.Square).then_inc(S("l_sq"), 1)
                    hi_static(act, 4)
                    hi_static(act, 5)
                    rsqrt(act, rsb[:], bank[MMB][:], 1.0 / B_QRANK, (S("l_ss"), 1), (S("l_ln"), 1), S("l_rs"))
                if c == 2:
                    nc.scalar.activation(sqb[:], yv[:], ACT.Square).then_inc(S("l_sq"), 1)
                    hi_static(act, 6)
                    for k in range(2):
                        act.wait_ge(S("l_n"), k + 1)
                        nc.scalar.activation(qlhi[:, k, :], (yq, yk)[k][:], ACT.Copy).then_inc(S("l_hi"), 1)
                    rsqrt(act, rsb[:], bank[MMB][:], 1.0 / B_KVRANK, (S("l_ss"), 2), (S("l_ln"), 2), S("l_rs"))
            act.wait_ge(S("l_y"), 4)
            nc.scalar.activation(sqb[0:B_QK, :], yq[0:B_QK, :], ACT.Square).then_inc(S("head_qsq"), 1)
            act.wait_ge(S("l_n"), 3)
            nc.scalar.activation(kvhi[:], yv[:], ACT.Copy).then_inc(S("l_hi"), 1)
            qk_rs_act(act, "r", "q", 0, B_QK, 1.0)

            def a_act(u, nxt, hi):
                if u is not None:
                    v_act(act, "a", u)
                    softmax_act(act, "a", u, 0, A_SCALE)
                if nxt is not None:
                    a_sq_act(act, nxt, "q")
                    hi(0)
                if u is not None:
                    softmax_act(act, "a", u, 1, A_SCALE)
                if nxt is not None:
                    qk_rs_act(act, "a", "q", nxt, P, 1.0 / A_DIM)
                    act.wait_ge(*at_head("a", "ky", nxt + 1))
                    hi(1)
                if u is not None:
                    softmax_act(act, "a", u, 2, A_SCALE)
                if nxt is not None:
                    a_sq_act(act, nxt, "k")
                    qk_rs_act(act, "a", "k", nxt, P, 1.0 / A_DIM)
                if u is not None:
                    softmax_act(act, "a", u, 3, A_SCALE)
                if nxt is not None:
                    act.wait_ge(*at_head("a", "vy", nxt + 1))
                    hi(2)
                if u is not None:
                    for kb in range(NB):
                        ptrans_act(act, "a", u, kb)
                if nxt is not None:
                    a_slots_act(act, nxt)
                if u is not None:
                    a_out_act(act, u)

            a_act(None, 0, lambda c: hi_static(act, G_A + 3 + c))
            with act.Fori(0, A_HEADS - 1) as i:
                a_act(i, i + 1, lambda c: hi_at(act, G_A + 6 + c, i, 3))
            a_act(A_HEADS - 1, None, None)
            act.wait_ge(*at_head("a", "s", A_HEADS * NB))
            act.wait_ge(*at_head("r", "kept", 1))
            nc.scalar.activation(khi[64:96, :], rope_keep[64:96, :], ACT.Copy).then_inc(S("kr_hi"), 1)
            for s in range(2):
                b_hi_act(act, s, s, 1)
            b_prep_act(act, 0, 0)
            b_prep_act(act, 0, 1)
            b_slots_act(act, 0)

            def b_act(u, nxt, s, use, j, k):
                v_act(act, "b", u)
                softmax_act(act, "b", u, 0, B_SCALE)
                softmax_act(act, "b", u, 1, B_SCALE)
                if nxt is not None:
                    b_prep_act(act, nxt, 0)
                softmax_act(act, "b", u, 2, B_SCALE)
                softmax_act(act, "b", u, 3, B_SCALE)
                if nxt is not None:
                    b_prep_act(act, nxt, 1)
                for kb in range(NB):
                    ptrans_act(act, "b", u, kb)
                if use is not None:
                    b_hi_act(act, None, s, use)
                if nxt is not None:
                    b_slots_act(act, nxt)
                head_out_act(act, "b", u, j, k)

            with act.Fori(0, B_HEADS // 2 - 1) as i:
                for s in range(2):
                    b_act(i * 2 + s, i * 2 + (s + 1), s, i + 2, s, i + 4)
            b_act(B_HEADS - 2, B_HEADS - 1, 0, None, 0, 7)
            b_act(B_HEADS - 1, None, 1, None, 1, 7)
            out_act(act, G_OUT0, 0, 1)
            norm_rstd(act, 1, 7)
            ffn_act(act, 0, 2)

            norm_rstd(act, 2, CO)

            def c_act(u, nxt, hi):
                if u is not None:
                    for b in range(3):
                        c_chain_act(act, u, 0, b)
                if nxt is not None:
                    c_slot_act(act, nxt, "q")
                    hi(0)
                if u is not None:
                    for b in range(3):
                        c_chain_act(act, u, 1, b)
                    for b in range(3):
                        c_w_act(act, u, 0, b)
                    c_v_act(act, u)
                if nxt is not None:
                    c_slot_act(act, nxt, "k")
                    hi(1)
                if u is not None:
                    for b in range(3):
                        c_w_act(act, u, 1, b)
                    act.wait_ge(S("c_o"), u * 2 + 1)
                    cout_act(u, 0)
                if nxt is not None:
                    act.wait_ge(S("c_vy"), nxt + 1)
                    hi(2)
                if u is not None:
                    act.wait_ge(S("c_o"), u * 2 + 2)
                    cout_act(u, 1)

            def cout_act(u, j):
                nc.scalar.activation(tile_at(mhi, u, slice(64 * j, 64 * j + 64)), as3(bank[CO][0:64, :], u),
                                     ACT.Copy).then_inc(S("c_mhi"), 1)

            c_act(None, 0, lambda c: hi_static(act, G_C + 3 + c))
            with act.Fori(0, C_PAIRS - 1) as i:
                c_act(i, i + 1, lambda c: hi_at(act, G_C + 6 + c, i, 3))
            c_act(C_PAIRS - 1, None, None)
            out_act(act, G_OUT1, 1, 3)
            norm_rstd(act, 3, 7)
            ffn_act(act, 1, None)

        @block.vector
        def _(dve):
            nc.vector.memset(qhi[64:128, 0, :].bitcast(F32), 0.0)
            nc.vector.memset(qhi[0:64, 1, :].bitcast(F32), 0.0)
            nc.vector.memset(qlo[64:128, 0, :].bitcast(F32), 0.0)
            nc.vector.memset(qlo[0:64, 1, :].bitcast(F32), 0.0)
            nc.vector.memset(pthi[:, TO[3]:TO[3] + P].bitcast(F32), 0.0)
            nc.vector.memset(ptlo[:, TO[3]:TO[3] + P].bitcast(F32), 0.0)
            dve.wait_ge(S("mat_in"), 16)
            nc.vector.tensor_copy(ident_r[:], M["ident"])
            dve.wait_ge(S("masks_in"), 16)
            nc.vector.tensor_copy(cmask[:], rawm[:])
            dve.wait_ge(S("vec_in"), 16)
            nc.vector.tensor_tensor(tiny[:, 10:11], v(V_LAM), v(V_LAM + 1), ALU.mult).then_inc(S("lam_prod"), 1)
            nc.vector.tensor_tensor(tiny[:, 11:12], v(V_LAM + 2), v(V_LAM + 3), ALU.mult).then_inc(S("lam_prod"), 1)
            nc.vector.tensor_scalar(tiny[:, 17:18], v(V_AO), 1.0 - LAM0, None, ALU.mult).then_inc(S("head_og"), 1)
            for d in range(KT):
                norm_dve(dve, 0, d)
            dve.wait_ge(S("lam_exp"), 1)
            nc.vector.tensor_tensor(tiny[:, 14:15], tiny[:, 12:13], tiny[:, 13:14], ALU.subtract).then_inc(S("lam_dif"), 1)
            dve.wait_ge(S("lam_dif"), 1)
            nc.vector.tensor_scalar(tiny[:, 16:17], tiny[:, 14:15], LAM0, None, ALU.add).then_inc(S("lam"), 1)
            dve.wait_ge(S("lam"), 1)
            dve.wait_ge(*at_norm(0, "rstd", 1))
            for c in range(3):
                dve.wait_ge(S("chunk_done"), c + 1)
                nc.vector.tensor_tensor((yq, yk, yv)[c][:], bank[(2, 3, 0)[c]][:], rstd[:], ALU.mult).then_inc(S("l_y"), 1)
            dve.wait_ge(S("l_rs"), 1)
            for k in range(2):
                y = (yq, yk)[k]
                nc.vector.scalar_tensor_tensor(y[:], y[:], v(V_BQL + k), rsb[:], ALU.mult, ALU.mult).then_inc(S("l_n"), 1)
                dve.wait_ge(S("l_hi"), k + 1)
                nc.vector.tensor_tensor(qllo[:, k, :], y[:], qlhi[:, k, :], ALU.subtract).then_inc(S("l_lo"), 1)
            dve.wait_ge(S("chunk_done"), 4)
            dve.wait_ge(S("l_lo"), 1)
            nc.vector.tensor_tensor(yq[:], bank[1][:], rstd[:], ALU.mult).then_inc(S("l_y"), 1)
            dve.wait_ge(S("l_rs"), 2)
            nc.vector.scalar_tensor_tensor(yv[:], yv[:], v(V_BKVL), rsb[:], ALU.mult, ALU.mult).then_inc(S("l_n"), 1)
            dve.wait_ge(S("l_hi"), 3)
            nc.vector.tensor_tensor(kvlo[:], yv[:], kvhi[:], ALU.subtract).then_inc(S("l_lo"), 1)
            dve.wait_ge(S("tabb_in"), 16)
            qk_t_dve(dve, "r", "q", 0, B_QK, yq[0:B_QK, :], v(V_BKR, rows=B_QK))
            qk_rope_dve(dve, "r", "q", 0, B_QK, yq, tabb)
            dve.wait_ge(*at_head("r", "qy2", 1))
            nc.vector.tensor_copy(rope_keep[64:96, :], yq[64:96, :]).then_inc(S("head_kept"), 1)
            dve.wait_ge(*at_head("r", "kept", 1))
            dve.wait_ge(S("taba_in"), 16)

            def a_dve(u, nxt):
                if u is not None:
                    v_dve(dve, "a", u)
                    softmax_dve(dve, "a", u, 0, A_SCALE)
                    probs_dve(dve, "a", u, 0)
                if nxt is not None:
                    a_y_dve(dve, nxt, "q")
                if u is not None:
                    softmax_dve(dve, "a", u, 1, A_SCALE)
                    probs_dve(dve, "a", u, 1)
                if nxt is not None:
                    qk_t_dve(dve, "a", "q", nxt, P, yq[:], v(V_AQ))
                    a_y_dve(dve, nxt, "k")
                    qk_rope_dve(dve, "a", "q", nxt, P, yq, taba)
                if u is not None:
                    softmax_dve(dve, "a", u, 2, A_SCALE)
                    probs_dve(dve, "a", u, 2)
                if nxt is not None:
                    qk_t_dve(dve, "a", "k", nxt, P, yk[:], v(V_AK))
                    a_y_dve(dve, nxt, "v")
                    qk_rope_dve(dve, "a", "k", nxt, P, yk, taba)
                if u is not None:
                    softmax_dve(dve, "a", u, 3, A_SCALE)
                    probs_dve(dve, "a", u, 3)
                    for kb in range(NB):
                        ptrans_dve(dve, "a", u, kb)
                if nxt is not None:
                    a_slots_dve(dve, nxt)
                if u is not None:
                    a_out_dve(dve, u)

            a_dve(None, 0)
            with dve.Fori(0, A_HEADS - 1) as i:
                a_dve(i, i + 1)
            a_dve(A_HEADS - 1, None)
            dve.wait_ge(S("kr_hi"), 1)
            nc.vector.tensor_tensor(klo[64:96, :], rope_keep[64:96, :], khi[64:96, :], ALU.subtract).then_inc(S("kr_lo"), 1)
            b_prep_dve(dve, 0, 0)
            b_prep_dve(dve, 0, 1)
            b_slots_dve(dve, 0)

            def b_dve(u, nxt, j, k):
                v_dve(dve, "b", u)
                for b in range(NB):
                    softmax_dve(dve, "b", u, b, B_SCALE)
                    probs_dve(dve, "b", u, b)
                    if b == 1 and nxt is not None:
                        b_prep_dve(dve, nxt, 0)
                if nxt is not None:
                    b_prep_dve(dve, nxt, 1)
                for kb in range(NB):
                    ptrans_dve(dve, "b", u, kb)
                if nxt is not None:
                    b_slots_dve(dve, nxt)
                head_out_dve(dve, "b", u, j, k)

            with dve.Fori(0, B_HEADS // 2 - 1) as i:
                for s in range(2):
                    b_dve(i * 2 + s, i * 2 + (s + 1), s, i + 4)
            b_dve(B_HEADS - 2, B_HEADS - 1, 0, 7)
            b_dve(B_HEADS - 1, None, 1, 7)
            out_dve(dve, G_OUT0, 0, 1)
            ffn_dve(dve, 0, 1, 2)

            for t in (cqhi, cqlo):
                nc.vector.memset(t[64:128, 0, :].bitcast(F32), 0.0)
                nc.vector.memset(t[0:64, 1, :].bitcast(F32), 0.0)
            dve.wait_ge(S("crawm_in"), 16)
            nc.vector.tensor_copy(cmats[:].rearrange("p m n -> p (m n)"), crawm[:, 0:256])
            nc.vector.tensor_copy(csmask[:].rearrange("p m n -> p (m n)"), crawm[:, 256:768])
            dve.wait_ge(*at_norm(2, "rstd", 1))

            def c_out(u, j):
                dve.wait_ge(S("c_mhi"), u * 2 + (j + 1))
                r = slice(64 * j, 64 * j + 64)
                nc.vector.tensor_tensor(tile_at(mlo, u, r), as3(bank[CO][0:64, :], u), tile_at(mhi, u, r),
                                        ALU.subtract).then_inc(S("c_mlo"), 1)

            def c_dve(u, nxt):
                if u is not None:
                    for b in range(3):
                        c_chain_dve(dve, u, 0, b)
                if nxt is not None:
                    c_y_dve(dve, nxt, "q")
                    c_slot_dve(dve, nxt, "q")
                if u is not None:
                    for b in range(3):
                        c_chain_dve(dve, u, 1, b)
                    for b in range(3):
                        c_w_dve(dve, u, 0, b)
                    c_v_dve(dve, u)
                if nxt is not None:
                    c_y_dve(dve, nxt, "k")
                    c_slot_dve(dve, nxt, "k")
                if u is not None:
                    for b in range(3):
                        c_w_dve(dve, u, 1, b)
                    c_out(u, 0)
                if nxt is not None:
                    c_y_dve(dve, nxt, "v")
                if u is not None:
                    c_out(u, 1)

            c_dve(None, 0)
            with dve.Fori(0, C_PAIRS - 1) as i:
                c_dve(i, i + 1)
            c_dve(C_PAIRS - 1, None)
            out_dve(dve, G_OUT1, 1, 3)
            ffn_dve(dve, 1, 3, None)

        @block.tensor
        def _(pe):
            pe.wait_ge(S("mat_in"), 16)
            pe.wait_ge(S("lam_prod"), 2)
            nc.tensor.matmul(bank[MMB][:, 0:2], M["ones"], tiny[:, 10:12], start=True, stop=True).then_inc(S("lam_sum"), 1)
            project(pe, 0, 0, bank[2][:], h_hi, h_lo, need_h(pe, 0))
            pe.wait_ge(S("lam_exp"), 1)
            norm_pe(pe, 0, MMB)
            project(pe, 1, 1, bank[3][:], h_hi, h_lo)
            project(pe, 2, 2, bank[0][:], h_hi, h_lo)
            pe.wait_ge(S("l_sq"), 2)
            nc.tensor.matmul(bank[MMB][:], M["ones"], sqb[:], start=True, stop=False)
            nc.tensor.matmul(bank[MMB][:], M["ones"], tb[:], start=False, stop=True).then_inc(S("l_ss"), 1)
            project(pe, 3, 0, bank[1][:], h_hi, h_lo)
            pe.wait_ge(S("l_sq"), 3)
            nc.tensor.matmul(bank[MMB][:], M["ones"], sqb[:], start=True, stop=True).then_inc(S("l_ss"), 1)

            def a_pe(u, nxt):
                if u is not None:
                    vtrans_pe(pe, "a", u)
                    scores_pe(pe, "a", u, 0)
                if nxt is not None:
                    a_proj_pe(pe, nxt, "q")
                if u is None:
                    qk_ssq_pe(pe, "r", "q", 0, B_QK, "blk_b")
                else:
                    scores_pe(pe, "a", u, 1)
                if nxt is not None and u is not None:
                    qk_ssq_pe(pe, "a", "q", nxt, P, "blk64")
                    a_proj_pe(pe, nxt, "k")
                    qk_rot_pe(pe, "a", "q", nxt, P, "rot_a")
                elif nxt is not None:
                    a_proj_pe(pe, nxt, "k")
                    qk_rot_pe(pe, "r", "q", 0, B_QK, "rot_b")
                    qk_ssq_pe(pe, "a", "q", nxt, P, "blk64")
                    qk_rot_pe(pe, "a", "q", nxt, P, "rot_a")
                if u is not None:
                    scores_pe(pe, "a", u, 2)
                if nxt is not None:
                    pe.wait_ge(*at_head("a", "qs", nxt + 1))
                    qk_ssq_pe(pe, "a", "k", nxt, P, "blk64")
                    a_proj_pe(pe, nxt, "v")
                    qk_rot_pe(pe, "a", "k", nxt, P, "rot_a")
                if u is not None:
                    scores_pe(pe, "a", u, 3)
                    attn_tail_pe(pe, "a", u)
                    if nxt is not None:
                        pe.wait_ge(*at_head("a", "ks", nxt + 1))
                    a_out_pe(pe, u)

            a_pe(None, 0)
            with pe.Fori(0, A_HEADS - 1) as i:
                a_pe(i, i + 1)
            a_pe(A_HEADS - 1, None)
            b_proj_pe(pe, 0, 0)
            b_prep_pe(pe, 0)

            def b_pe(u, nxt, s):
                vtrans_pe(pe, "b", u)
                scores_pe(pe, "b", u, 0)
                scores_pe(pe, "b", u, 1)
                if nxt is not None:
                    b_proj_pe(pe, nxt, s)
                scores_pe(pe, "b", u, 2)
                if nxt is not None:
                    qk_ssq_pe(pe, "b", "q", nxt, B_QK, "blk_b")
                scores_pe(pe, "b", u, 3)
                if nxt is not None:
                    qk_rot_pe(pe, "b", "q", nxt, B_QK, "rot_b")
                    pe.wait_ge(*at_head("b", "qs", nxt + 1))
                    qk_ssq_pe(pe, "b", "k", nxt, P, "blk64")
                attn_tail_pe(pe, "b", u)

            with pe.Fori(0, B_HEADS // 2 - 1) as i:
                for s in range(2):
                    b_pe(i * 2 + s, i * 2 + (s + 1), 1 - s)
            b_pe(B_HEADS - 2, B_HEADS - 1, 1)
            b_pe(B_HEADS - 1, None, None)
            out_pe(pe, G_OUT0, 0, at_head("b", "mlo", B_HEADS))
            ffn_pe(pe, 0, 1)

            def c_pe(u, nxt):
                if u is not None:
                    c_scores_pe(pe, u, 0)
                    c_scores_pe(pe, u, 1)
                if u is None:
                    pe.wait_ge(*at_net(0, "x", KT + 7))
                if nxt is not None:
                    c_proj_pe(pe, nxt, "q", need_h(pe, 2) if u is None else None)
                if u is not None:
                    c_tail_pe(pe, u, 0)
                    c_vt_pe(pe, u)
                else:
                    norm_pe(pe, 2, CO)
                if nxt is not None:
                    c_proj_pe(pe, nxt, "k")
                if u is not None:
                    c_tail_pe(pe, u, 1)
                    c_values_pe(pe, u, 0)
                if nxt is not None:
                    c_proj_pe(pe, nxt, "v")
                if u is not None:
                    c_values_pe(pe, u, 1)

            c_pe(None, 0)
            with pe.Fori(0, C_PAIRS - 1) as i:
                c_pe(i, i + 1)
            c_pe(C_PAIRS - 1, None)
            out_pe(pe, G_OUT1, 1, (S("c_mlo"), C_HEADS))
            ffn_pe(pe, 1, 3)


def constants():
    f = np.float32
    i = np.arange(P)

    def rot(first, rows, half):
        m = np.zeros((P, P), f)
        for r in range(first, first + rows):
            up = (r - first) % (2 * half) < half
            m[r + half if up else r - half, r] = -1.0 if up else 1.0
        return m
    blk64 = (i[:, None] // 64 == i[None, :] // 64).astype(f)
    blk_b = np.zeros((P, P), f)
    blk_b[:B_NOPE, :B_NOPE] = 1.0 / B_NOPE
    blk_b[B_NOPE:B_QK, B_NOPE:B_QK] = 1.0 / B_ROPE
    mats = np.stack([np.eye(P, dtype=f), rot(0, P, A_DIM // 2), rot(B_NOPE, B_ROPE, B_ROPE // 2), blk64,
                     blk_b, np.ones((P, P), f)], axis=1)
    hidden = np.where(i[:, None] // CHUNK < i[None, :] // CHUNK, f(BIG), f(0))
    masks_a = np.zeros((P, 2, 256), f)
    masks_a[:, 0, :P], masks_a[:, 0, P:], masks_a[:, 1, P:] = hidden, BIG, hidden
    later = np.where(i[None, :] <= i[:, None], f(BIG), f(0))
    masks_c = np.zeros((P, 768), f)
    masks_c[:, 0:P] = -(i[:, None] >= i[None, :]).astype(f)
    masks_c[:, P:2 * P] = -1.0
    masks_c[:, 256:384] = later
    masks_c[:, 512:640] = BIG
    masks_c[:, 640:768] = later

    def table(half, rows):
        freq = np.power(f(THETA), -np.arange(half, dtype=f) / f(half)).astype(f)
        ang = (np.arange(SEQ, dtype=f)[:, None] * freq[None, :]).astype(f)
        r = np.arange(rows) % half
        return np.cos(ang).T[r], np.sin(ang).T[r]
    tabs_a = np.stack(table(A_DIM // 2, P), axis=1).astype(f)
    tabs_b = np.zeros((P, 2, SEQ), f)
    tabs_b[:B_NOPE, 0] = 1.0
    c, s = table(B_ROPE // 2, B_ROPE)
    tabs_b[B_NOPE:B_QK, 0], tabs_b[B_NOPE:B_QK, 1] = c, s
    return mats, masks_a, masks_c, tabs_a, tabs_b


def layout(i):
    f = np.float32
    a = {k: np.asarray(t) for k, t in i.items()}

    def chunks(w, tiles=None):
        k, n = w.shape
        return w.reshape(k // P, P, n // P, P).transpose(2, 1, 0, 3).reshape(n // P, P, k)
    w = a["ab_w_in"][0]
    aq, ak, av = w[:, 0:512], w[:, 512:1024], w[:, 1024:1536]
    kr = np.zeros((D, P), f)
    kr[:, B_NOPE:B_QK] = w[:, 1920:1952]
    rows = [chunks(w[:, 1536:1920]), chunks(kr)]
    rows.append(np.stack([chunks(aq), chunks(ak), chunks(av)], axis=1).reshape(-1, P, W_IN))
    rows.append(chunks(a["ab_w_out"][0]))
    down = []

    def network(l):
        gate, up = chunks(a["ffn_w_gate"][l]), chunks(a["ffn_w_up"][l])
        rows.append(np.stack([gate, up], axis=1).reshape(-1, P, W_IN))
        for s in range(2):
            down.append(chunks(a["ffn_w_down"][l][s * HALF_F * P:(s + 1) * HALF_F * P]))
    network(0)
    c = a["c_w_in"][0]
    rows.append(np.stack([chunks(c[:, t * D:(t + 1) * D]) for t in range(3)], axis=1).reshape(-1, P, W_IN))
    rows.append(chunks(a["c_w_out"][0]))
    network(1)
    w_in, w_down = np.concatenate(rows), np.concatenate(down)

    qb = a["b_w_q_b"][0].reshape(2, P, B_HEADS, B_QK).transpose(2, 1, 0, 3).reshape(B_HEADS, P, 2 * B_QK)
    kvb = a["b_w_kv_b"][0].reshape(P, B_HEADS, P).transpose(1, 0, 2)
    w_b = np.concatenate([qb, kvb], axis=2)

    vecs = np.zeros((P, V_N), f)
    gains = [a["norm_mix"][0], a["norm_ffn"][0], a["norm_mix"][1], a["norm_ffn"][1]]
    vecs[:, V_GAIN:V_GAIN + 4 * KT] = np.stack(gains).reshape(4 * KT, P).T
    vecs[:, V_AQ] = np.concatenate([a["a_q_norm"][0]] * 2)
    vecs[:, V_AK] = np.concatenate([a["a_k_norm"][0]] * 2)
    vecs[:, V_AO] = a["a_out_norm"][0]
    vecs[:, V_BQL:V_BQL + 2] = a["b_q_a_norm"][0].reshape(2, P).T
    vecs[:, V_BKVL] = a["b_kv_a_norm"][0]
    vecs[:B_NOPE, V_BQ], vecs[B_NOPE:B_QK, V_BQ] = a["b_q_nope_norm"][0], a["b_q_rope_norm"][0]
    vecs[:B_NOPE, V_BK] = a["b_k_nope_norm"][0]
    vecs[B_NOPE:B_QK, V_BKR] = a["b_k_rope_norm"][0]
    vecs[:A_DIM, V_LAM:V_LAM + 4] = a["a_lambda"][0].T
    vecs[:, V_EPS] = EPS
    xt = a["x"][0].T.reshape(KT, P, SEQ)
    return dict(xt=xt, w_in=w_in, w_b=w_b, w_down=w_down, vecs=vecs)


def kernel(**inputs):
    import concourse.bacc as bacc
    from concourse.bass_utils import run_bass_kernel_spmd

    arrays = layout(inputs)
    for name, value in zip(("mats", "masks_a", "masks_c", "tabs_a", "tabs_b"), constants()):
        arrays[name] = value
    arrays = {n: np.ascontiguousarray(t) for n, t in arrays.items()}
    nc = bacc.Bacc("TRN2", target_bir_lowering=False, num_devices=1)
    aps = {n: nc.dram_tensor(f"in_{n}", t.shape, mybir.dt.from_np(t.dtype), kind="ExternalInput").ap()
           for n, t in arrays.items()}
    out = nc.dram_tensor("out", (KT, P, SEQ), F32, kind="ExternalOutput").ap()
    trunk(nc, out=out, **aps)
    r = run_bass_kernel_spmd(nc, [{f"in_{n}": t for n, t in arrays.items()}], core_ids=[0])
    return r.results[0]["out"].reshape(D, SEQ).T.reshape(1, SEQ, D)
```

```python
import math

import numpy as np

import concourse.bass as bass
from concourse import mybir

F32 = mybir.dt.float32
F32R = mybir.dt.float32r
ALU = mybir.AluOpType
ACT = mybir.ActivationFunctionType
AX = mybir.AxisListType.X

P = 128
D = 1024
SEQ = 512
KT = D // P
NB = SEQ // P
CHUNK = 64
EPS = 1e-6
THETA = 10000.0
BIG = -1e30

A_HEADS, A_DIM = 4, 64
B_HEADS, B_NOPE, B_ROPE, B_V = 8, 64, 32, 64
B_QK = B_NOPE + B_ROPE
B_QRANK, B_KVRANK = 256, 128
C_HEADS, C_DIM = 16, 64
C_PAIRS = C_HEADS // 2
D_FF = 2816
HALF_F = D_FF // P // 2
LAM0 = 0.8 - 0.6 * math.exp(-0.3 * 0)

WSLOTS = 3
W_IN = KT * P
W_DOWN = HALF_F * P
WB = 2 * B_QK + P

G_LAT = 0
G_A = G_LAT + 4
G_OUT0 = G_A + 3 * A_HEADS
G_FFN0 = G_OUT0 + KT
FFN_HALF = 2 * HALF_F + KT
G_C = G_FFN0 + 2 * FFN_HALF
G_OUT1 = G_C + 3 * C_PAIRS
G_FFN1 = G_OUT1 + KT
N_CHUNKS = G_FFN1 + 2 * FFN_HALF

SW = [max(256, (b + 1) * P) for b in range(NB)]
TQ = [min(b * P, SEQ - 256) for b in range(NB)]
TW = [SEQ - q for q in TQ]
TO = [sum(TW[:b]) for b in range(NB)]
TWS = sum(TW)

MATS = ["ident", "rot_a", "rot_b", "blk64", "blk_b", "ones"]
V_GAIN = 0
V_AQ, V_AK, V_AO, V_BQL, V_BKVL, V_BQ, V_BK, V_BKR, V_LAM, V_EPS = 32, 33, 34, 35, 37, 38, 39, 40, 41, 45
V_N = 46


def width_of(g):
    for first in (G_FFN0, G_FFN1):
        if first <= g < first + 2 * FFN_HALF and (g - first) % FFN_HALF >= 2 * HALF_F:
            return W_DOWN
    return W_IN


def trunk(nc, xt, w_in, w_b, w_down, mats, masks_a, masks_c, tabs_a, tabs_b, vecs, out, upto="all"):
    cursor = [nc.sbuf_base]
    count = [0]

    def place(name, shape, dt, at=None):
        size = 4 * int(np.prod(shape[1:]))
        off = cursor[0] if at is None else at
        off = (off + 31) // 32 * 32
        t = nc.alloc_sbuf_tensor_at(name, list(shape), dt, offset=off)
        if at is None:
            cursor[0] = off + size
        return t, off + size

    def pair(name, shape, at=None):
        a, end = place(name + "_hi", shape, F32R, at)
        b, end = place(name + "_lo", shape, F32R, None if at is None else end)
        return (a, b), end

    x, _ = place("x", [P, KT, SEQ], F32)
    wraw, _ = place("wraw", [P, WSLOTS, W_DOWN], F32)
    (whi, wlo), _ = pair("w", [P, WSLOTS, W_DOWN])
    mat, _ = place("mat", [P, len(MATS), P], F32)
    ident_r, _ = place("ident_r", [P, P], F32R)
    cmask, _ = place("cmask", [P, 2, 256], F32R)
    vec, _ = place("vec", [P, V_N], F32)
    tiny, _ = place("tiny", [P, 112], F32)
    rstd, _ = place("rstd", [P, SEQ], F32)
    h0 = cursor[0]
    (hhi, hlo), _ = pair("h", [P, KT, SEQ])
    phase0 = cursor[0]

    (mhi, mlo), _ = pair("mixed", [P, KT, SEQ])
    (qlhi, qllo), _ = pair("ql", [P, 2, SEQ])
    (kvhi, kvlo), _ = pair("kvl", [P, SEQ])
    tabb, _ = place("tabb", [P, 2, SEQ], F32)
    (qhi, qlo), _ = pair("q", [P, 2, SEQ])
    (khi, klo), _ = pair("k", [P, SEQ])
    (vhi, vlo), _ = pair("v", [P, NB, P])
    e1, _ = place("e1", [P, 2, SEQ], F32)
    pn0 = cursor[0]
    pn, _ = place("pn", [P, NB, SEQ], F32)
    (pthi, ptlo), _ = pair("pt", [P, TWS])
    yq, _ = place("yq", [P, SEQ], F32)
    yk, _ = place("yk", [P, SEQ], F32)
    yv, _ = place("yv", [P, SEQ], F32)
    on, _ = place("on", [P, SEQ], F32)
    sqb, _ = place("sqb", [P, SEQ], F32)
    tb, _ = place("tb", [P, SEQ], F32)
    assert cursor[0] <= nc.sbuf_usable_end, cursor[0]
    taba, end = place("taba", [P, 2, SEQ], F32, at=phase0 + 4 * 4 * SEQ)
    rope_keep, end = place("rope_keep", [P, SEQ], F32, at=end)
    assert end <= phase0 + 4 * KT * SEQ
    bwraw, end = place("bwraw", [P, 2, WB], F32, at=h0)
    (bwhi, bwlo), end = pair("bw", [P, 2, WB], at=end)
    rawm, _ = place("rawm", [P, 2, 256], F32, at=pn0 + 12 * SEQ)
    sqn, end = place("sqn", [P, 2, SEQ], F32, at=pn0)
    ssum, _ = place("ssum", [P, SEQ], F32, at=end)

    (fhi, flo), end = pair("f", [P, HALF_F, SEQ], at=phase0)
    fy, end = place("fy", [P, SEQ], F32, at=end)
    fs, end = place("fs", [P, SEQ], F32, at=end)
    fu, end = place("fu", [P, SEQ], F32, at=end)
    fa, end = place("fa", [P, SEQ], F32, at=end)
    assert end <= pn0, (end, pn0)

    c0 = phase0 + 2 * 4 * KT * SEQ
    (cqhi, cqlo), end = pair("cq", [P, 2, SEQ], at=c0)
    (ckhi, cklo), end = pair("ck", [P, SEQ], at=end)
    (cvhi, cvlo), end = pair("cv", [P, NB, P], at=end)
    cyq, end = place("cyq", [P, SEQ], F32, at=end)
    cyk, end = place("cyk", [P, SEQ], F32, at=end)
    cyv, end = place("cyv", [P, SEQ], F32, at=end)
    cmats, end = place("cmats", [P, 2, P], F32R, at=end)
    csmask, end = place("csmask", [P, 2, 256], F32R, at=end)
    (cz0, cz0lo), end = pair("cs0", [P, TWS], at=end)
    (cz1, cz1lo), end = pair("cs1", [P, TWS], at=end)
    cshi, cslo = (cz0, cz1), (cz0lo, cz1lo)
    ca0, end = place("ca0", [P, TWS], F32, at=end)
    ca1, end = place("ca1", [P, TWS], F32, at=end)
    ca = (ca0, ca1)
    cs, end = place("cs", [P, TWS], F32, at=end)
    crawm, end = place("crawm", [P, 768], F32, at=end - 4 * TWS)
    assert end <= nc.sbuf_usable_end and end <= nc.sbuf_usable_end, end

    bank = [nc.alloc_psum_tensor(f"bank{i}", [P, SEQ], F32) for i in range(8)]

    sems = {}

    def S(name):
        if name not in sems:
            sems[name] = nc.alloc_semaphore(name)
        return sems[name]

    def wait(eng, name, value):
        if not isinstance(value, int) or value > 0:
            eng.wait_ge(S(name), value)

    M = {n: mat[:, i, :] for i, n in enumerate(MATS)}

    def v(col, n=1, rows=P):
        return vec[0:rows, col:col + n]

    def tile_at(t, k, rows=slice(0, P)):
        return t[rows, k, :] if isinstance(k, int) else t[rows, bass.ds(k, 1), :]

    def as3(ap, k):
        return ap if isinstance(k, int) else ap.rearrange("p (o n) -> p o n", o=1)

    def at_norm(n, what, value):
        return S("norm_" + what), value + n * {"sq": KT, "hi": KT, "lo": KT, "sum": KT - 1}.get(what, 1)

    def at_net(L, what, value):
        return S("net_" + what), value + L * 2 * (KT if what == "x" else HALF_F)

    def at_head(ph, what, value):
        a_only = {"e": 2 * NB, "mx": 2 * NB, "qlo": 2, "qhi": 2, "whi": 0, "wlo": 0, "q": 0, "kv": 0}
        of_a = A_HEADS * (NB if what in ("s", "nm", "r", "p", "tr", "phi", "plo") else a_only.get(what, 1))
        of_r = 1 if what in ("qsq", "qss", "qln", "qrs", "qt", "qrot", "qc", "qs", "qy2") else 0
        return S("head_" + what), value + (0 if ph == "r" else of_r) + (of_a if ph == "b" else 0)

    def slot(g_static):
        return g_static % WSLOTS

    def load_chunk(sp, g, s, n, src, width):
        wait(sp, "w_lo", g - (WSLOTS - 1))
        sp.dma_start(wraw[:, s, 0:width], src).then_inc(S(f"w_in{s}"), 16)

    def split_hi(act, g, s, use, width=W_IN):
        act.wait_ge(S(f"w_in{s}"), 16 * use)
        wait(act, "chunk_done", g - (WSLOTS - 1))
        nc.scalar.activation(whi[:, s, 0:width], wraw[:, s, 0:width], ACT.Copy).then_inc(S("w_hi"), 1)

    def hi_static(act, g):
        if g < N_CHUNKS:
            split_hi(act, g, slot(g), g // WSLOTS + 1, width_of(g))

    def hi_at(act, g0, i, step):
        split_hi(act, g0 + i * step, slot(g0), g0 // WSLOTS + 1 + i * (step // WSLOTS))

    def split_lo(pool, g, s, width):
        pool.wait_ge(S("w_hi"), g + 1)
        nc.gpsimd.tensor_tensor(wlo[:, s, 0:width], wraw[:, s, 0:width], whi[:, s, 0:width],
                                ALU.subtract).then_inc(S("w_lo"), 1)

    def project(pe, g, s, out_bank, src_hi, src_lo, first=None):
        n = len(src_hi)
        pe.wait_ge(S("w_hi"), g + 1)
        for kt in range(n):
            if first is not None:
                first(kt)
            w = whi[:, s, kt * P:(kt + 1) * P]
            nc.tensor.matmul(out_bank, w, src_hi[kt], start=(kt == 0), stop=False)
            nc.tensor.matmul(out_bank, w, src_lo[kt], start=False, stop=False)
        pe.wait_ge(S("w_lo"), g + 1)
        for kt in range(n):
            last = nc.tensor.matmul(out_bank, wlo[:, s, kt * P:(kt + 1) * P], src_hi[kt],
                                    start=False, stop=(kt == n - 1))
        last.then_inc(S("chunk_done"), 1)

    def project_early(pe, g, out_bank, src_hi, src_lo, tiles):
        pe.wait_ge(S("w_lo"), g + 1)
        for kt in range(tiles):
            w = slice(kt * P, (kt + 1) * P)
            for n, (a, o) in enumerate(((whi, src_hi), (whi, src_lo), (wlo, src_hi))):
                nc.tensor.matmul(out_bank, a[:, slot(g), w], o[kt], start=(kt == 0 and n == 0), stop=False)

    def project_rest(pe, g, out_bank, src_hi, src_lo, tiles):
        for kt in range(tiles, len(src_hi)):
            w = slice(kt * P, (kt + 1) * P)
            for n, (a, o) in enumerate(((whi, src_hi), (whi, src_lo), (wlo, src_hi))):
                last = nc.tensor.matmul(out_bank, a[:, slot(g), w], o[kt], start=False,
                                        stop=(kt == len(src_hi) - 1 and n == 2))
        last.then_inc(S("chunk_done"), 1)

    h_hi = [hhi[:, k, :] for k in range(KT)]
    h_lo = [hlo[:, k, :] for k in range(KT)]
    m_hi = [mhi[:, k, :] for k in range(KT)]
    m_lo = [mlo[:, k, :] for k in range(KT)]

    RS_NORM = (0, 24, 25, 26)
    RS_QL, RS_KVL, RS_ROPE = 1, 2, 3
    T_M, T_Y, T_A, T_Z = 44, 56, 68, (80, 92)

    def rs_a(u, what):
        if what == "out":
            return 16 if isinstance(u, int) and u == A_HEADS - 1 else u * 3 + 8
        first = RS_ROPE + 1 if isinstance(u, int) and u == 0 else u * 3 + 3
        return first + (1 if what == "k" else 0)

    def rs_b(u):
        return 15 if isinstance(u, int) and u == 0 else u + 16

    def rs_sum_pe(r, sources, cols, nh, b):
        for i in range(NB):
            for n, (src, rows) in enumerate(sources):
                last = nc.tensor.matmul(bank[b][:, i * nh:(i + 1) * nh], src[0:rows, i * P:(i + 1) * P],
                                        cols[0:rows, :], start=(n == 0), stop=(n == len(sources) - 1))
        last.then_inc(S("rs_sum"), 1)

    def rs_mean_dve(dve, r, scale, nh, b):
        dve.wait_ge(S("rs_sum"), r + 1)
        nc.vector.tensor_scalar(tiny[:, T_M:T_M + NB * nh], bank[b][:, 0:NB * nh], scale, EPS, ALU.mult,
                                ALU.add).then_inc(S("rs_mean"), 1)

    def rs_act(act, r, nh):
        m, y = tiny[:, T_M:T_M + NB * nh], tiny[:, T_Y:T_Y + NB * nh]
        act.wait_ge(S("rs_mean"), r + 1)
        nc.scalar.activation(y, m, ACT.Ln).then_inc(S("rs_ln"), 1)
        act.wait_ge(S("rs_ln"), r + 1)
        nc.scalar.activation(y, y, ACT.Exp, scale=-0.5).then_inc(S("rs_exp"), 1)

    def rs_newton_dve(dve, r, nh, slot=0):
        m, y, a, z = (tiny[:, t:t + NB * nh] for t in (T_M, T_Y, T_A, T_Z[slot]))
        dve.wait_ge(S("rs_exp"), r + 1)
        nc.vector.tensor_tensor(a, m, y, ALU.mult).then_inc(S("rs_my"), 1)
        dve.wait_ge(S("rs_my"), r + 1)
        nc.vector.tensor_tensor(a, a, y, ALU.mult).then_inc(S("rs_myy"), 1)
        dve.wait_ge(S("rs_myy"), r + 1)
        nc.vector.tensor_scalar(a, a, -0.5, 1.5, ALU.mult, ALU.add).then_inc(S("rs_step"), 1)
        dve.wait_ge(S("rs_step"), r + 1)
        nc.vector.tensor_tensor(z, a, y, ALU.mult).then_inc(S("rs_root"), 1)

    def rs_spread_pe(pe, r, nh, b, slot=0, step=None):
        pe.wait_ge(S("rs_root"), r + 1)
        for i in range(NB):
            for j in range(nh):
                col = T_Z[slot] + i * (step or nh) + j
                z = tiny[:, col:col + 1]
                rows = slice(j * P // nh, (j + 1) * P // nh)
                last = nc.tensor.matmul(bank[b][rows, i * P:(i + 1) * P], z.broadcast_to([P, P // nh]),
                                        M["ident"], start=True, stop=True)
        last.then_inc(S("rs_spread"), 1)

    def norm_act(act, n, d):
        if d >= 2:
            act.wait_ge(*at_norm(n, "sum", max(1, d - 2)))
        nc.scalar.activation(sqn[:, d % 2, :], x[:, d, :], ACT.Square).then_inc(S("norm_sq"), 1)
        nc.scalar.activation(hhi[:, d, :], x[:, d, :], ACT.Copy,
                             scale=v(V_GAIN + KT * n + d)).then_inc(S("norm_hi"), 1)

    def norm_dve(dve, n, d):
        dve.wait_ge(*at_norm(n, "hi", d + 1))
        nc.vector.scalar_tensor_tensor(hlo[:, d, :], x[:, d, :], v(V_GAIN + KT * n + d), hhi[:, d, :],
                                       ALU.mult, ALU.subtract).then_inc(S("norm_lo"), 1)

    def norm_pool(pool, n, d):
        if d == 0:
            return
        pool.wait_ge(*at_norm(n, "sq", d + 1))
        if d > 1:
            pool.wait_ge(*at_norm(n, "sum", d - 1))
        nc.gpsimd.tensor_tensor(ssum[:], sqn[:, 0, :] if d == 1 else ssum[:], sqn[:, d % 2, :],
                                ALU.add).then_inc(S("norm_sum"), 1)

    def norm_pe(pe, n, b):
        pe.wait_ge(*at_norm(n, "sum", KT - 1))
        rs_sum_pe(RS_NORM[n], [(ssum, P)], M["ones"][:, 0:1], 1, b)

    def norm_rstd_dve(dve, n, b, meanwhile=None):
        r = RS_NORM[n]
        rs_mean_dve(dve, r, 1.0 / D, 1, b)
        rs_newton_dve(dve, r, 1)
        if meanwhile is not None:
            meanwhile()
        dve.wait_ge(S("rs_spread"), r + 1)
        nc.vector.tensor_copy(rstd[:], bank[b][:]).then_inc(S("norm_rstd"), 1)
        dve.wait_ge(*at_norm(n, "rstd", 1))

    def need_h(pe, n):
        def first(kt):
            pe.wait_ge(*at_norm(n, "lo", kt + 1))
        return first

    OUT_BANKS = ((2, 3), (6, 2))
    OUT_EARLY = (2, 2)

    def out_early_pe(pe, g0, L, d):
        project_early(pe, g0 + d, bank[OUT_BANKS[L][d % 2]][:], m_hi, m_lo, KT - 1)

    def out_pe(pe, g0, L, heads_done):
        pe.wait_ge(*heads_done)
        for d in range(KT):
            b = bank[OUT_BANKS[L][d % 2]][:]
            if d < OUT_EARLY[L]:
                project_rest(pe, g0 + d, b, m_hi, m_lo, KT - 1)
                continue
            if d >= 2:
                pe.wait_ge(S("out_x"), L * KT + d - 1)
            project(pe, g0 + d, slot(g0 + d), b, m_hi, m_lo)

    def out_act(act, g0, L, n):
        for d in range(KT):
            act.wait_ge(S("out_x"), L * KT + d + 1)
            hi_static(act, g0 + d + 3)
            norm_act(act, n, d)

    def out_dve(dve, g0, L, n):
        for d in range(KT):
            dve.wait_ge(S("chunk_done"), g0 + d + 1)
            nc.vector.tensor_tensor(x[:, d, :], bank[OUT_BANKS[L][d % 2]][:], x[:, d, :], ALU.add).then_inc(S("out_x"), 1)
            norm_dve(dve, n, d)

    GU_LOOP = HALF_F // 3 * 3

    def ffn_each(eng, body):
        with eng.Fori(0, GU_LOOP // 3) as i:
            for j in range(3):
                body(i * 3 + j, j)
        for f in range(GU_LOOP, HALF_F):
            body(f, f % 3)

    def ffn_pe(pe, L, n):
        g_first = (G_FFN0, G_FFN1)[L]
        for s in range(2):
            g0 = g_first + s * FFN_HALF

            def gate_up(f, j):
                for c in range(2):
                    g = f * 2 + (g0 + c)
                    sl = slot(g0 + 2 * j + c)
                    if isinstance(f, int):
                        if s or f >= 3:
                            pe.wait_ge(*at_net(L, "yu"[c], s * HALF_F + f - 2 if f >= 3 else HALF_F))
                    elif s:
                        pe.wait_ge(*at_net(L, "yu"[c], f + (HALF_F - 2)))
                    project(pe, g, sl, bank[2 * j + c][:], h_hi, h_lo)
            if s == 0:
                for f in range(3):
                    for c in range(2):
                        g = g0 + 2 * f + c
                        project(pe, g, slot(g), bank[2 * f + c][:], h_hi, h_lo,
                                need_h(pe, n) if f == 0 and c == 0 else None)
                        if f == 0:
                            if c == 0:
                                norm_pe(pe, n, 7)
                            else:
                                rs_spread_pe(pe, RS_NORM[n], 1, 7)
                with pe.Fori(1, GU_LOOP // 3) as i:
                    for j in range(3):
                        for c in range(2):
                            pe.wait_ge(*at_net(L, "yu"[c], i * 3 + (j - 2)))
                            project(pe, i * 6 + (g0 + 2 * j + c), slot(g0 + 2 * j + c),
                                    bank[2 * j + c][:], h_hi, h_lo)
                for f in range(GU_LOOP, HALF_F):
                    gate_up(f, f % 3)
            else:
                pe.wait_ge(*at_net(L, "x", 6))
                with pe.Fori(0, GU_LOOP // 3) as i:
                    for j in range(3):
                        for c in range(2):
                            pe.wait_ge(*at_net(L, "yu"[c], i * 3 + (j - 2 + HALF_F)))
                            project(pe, i * 6 + (g0 + 2 * j + c), slot(g0 + 2 * j + c),
                                    bank[2 * j + c][:], h_hi, h_lo)
                for f in range(GU_LOOP, HALF_F):
                    gate_up(f, f % 3)
            gd = g0 + 2 * HALF_F
            f_hi = [fhi[:, k, :] for k in range(HALF_F)]
            f_lo = [flo[:, k, :] for k in range(HALF_F)]

            def need_f(kt):
                pe.wait_ge(*at_net(L, "lo", s * HALF_F + kt + 1))
            down_banks = (6, 7, 0)
            for d in range(3):
                if s:
                    pe.wait_ge(*at_net(L, "x", KT))
                project(pe, gd + d, slot(gd + d), bank[down_banks[d]][:], f_hi, f_lo,
                        need_f if d == 0 else None)
            for d in range(3, KT):
                pe.wait_ge(*at_net(L, "x", s * KT + d - 2))
                project(pe, gd + d, slot(gd + d), bank[down_banks[d % 3]][:], f_hi, f_lo)

    def ffn_act(act, L, n_next):
        g_first = (G_FFN0, G_FFN1)[L]
        for s in range(2):
            g0 = g_first + s * FFN_HALF

            def tile(i, j):
                f = i * 3 + j

                def split_ahead(c):
                    g = g0 + 2 * j + c
                    split_hi(act, i * 6 + g, slot(g), i * 2 + (g // WSLOTS + 1),
                             width_of(i * 6 + g) if isinstance(i, int) else W_IN)
                act.wait_ge(*at_net(L, "y", f + (s * HALF_F + 1)))
                nc.scalar.activation(fs[:], fy[:], ACT.Silu).then_inc(S("net_s"), 1)
                split_ahead(3)
                act.wait_ge(*at_net(L, "a", f + (s * HALF_F + 1)))
                nc.scalar.activation(tile_at(fhi, f), as3(fa[:], f), ACT.Copy).then_inc(S("net_hi"), 1)
                split_ahead(4)
            with act.Fori(0, GU_LOOP // 3) as i:
                for j in range(3):
                    tile(i, j)
            for f in range(GU_LOOP, HALF_F):
                tile(GU_LOOP // 3, f - GU_LOOP)
            for d in range(KT):
                act.wait_ge(*at_net(L, "x", s * KT + d + 1))
                hi_static(act, g0 + 2 * HALF_F + d + 3)
                if s and n_next is not None:
                    norm_act(act, n_next, d)

    def ffn_dve(dve, L, n, n_next):
        g_first = (G_FFN0, G_FFN1)[L]
        norm_rstd_dve(dve, n, 7)
        for s in range(2):
            g0 = g_first + s * FFN_HALF

            def tile(f, j):
                dve.wait_ge(S("chunk_done"), f * 2 + (g0 + 1))
                nc.vector.tensor_tensor(fy[:], bank[2 * j][:], rstd[:], ALU.mult).then_inc(S("net_y"), 1)
                dve.wait_ge(S("chunk_done"), f * 2 + (g0 + 2))
                nc.vector.tensor_tensor(fu[:], bank[2 * j + 1][:], rstd[:], ALU.mult).then_inc(S("net_u"), 1)
                dve.wait_ge(*at_net(L, "u", f + (s * HALF_F + 1)))
                dve.wait_ge(*at_net(L, "s", f + (s * HALF_F + 1)))
                nc.vector.tensor_tensor(fa[:], fu[:], fs[:], ALU.mult).then_inc(S("net_a"), 1)
                dve.wait_ge(*at_net(L, "hi", f + (s * HALF_F + 1)))
                nc.vector.tensor_tensor(tile_at(flo, f), as3(fa[:], f), tile_at(fhi, f),
                                        ALU.subtract).then_inc(S("net_lo"), 1)
            ffn_each(dve, tile)
            gd = g0 + 2 * HALF_F
            for d in range(KT):
                dve.wait_ge(S("chunk_done"), gd + d + 1)
                if s:
                    dve.wait_ge(*at_net(L, "x", KT))
                b = bank[(6, 7, 0)[d % 3]]
                nc.vector.tensor_tensor(x[:, d, :], b[:], x[:, d, :], ALU.add).then_inc(S("net_x"), 1)
                if s and n_next is not None:
                    norm_dve(dve, n_next, d)

    PJ = (2, 3)
    MMB = 4
    TRB = (5, 6)
    OB = 7
    VTB = 0
    QMB = 5
    KSB, KMB = 0, 1
    def score_bank(sub, b, j):
        return bank[((0, 1), TRB)[b % 2][j] if sub == 2 else (0, 1, *TRB)[b]]

    def scores_pe(pe, ph, u, b):
        sub = 2 if ph == "a" else 1
        if b == 0:
            pe.wait_ge(*at_head(ph, "qlo", u * sub + sub))
            pe.wait_ge(*at_head(ph, "klo", u + 1))
        if b == (1 if ph == "a" else 0):
            pe.wait_ge(*at_head(ph, "vlo", u + 1))
        if sub == 2 and b >= 2:
            pe.wait_ge(*at_head(ph, "e", u * (NB * sub) + sub * (b - 1)))
        w = SW[b]
        rows = P if ph == "a" else B_QK
        for j in range(sub):
            o = score_bank(sub, b, j)
            for n, (a, c) in enumerate(((qhi, khi), (qhi, klo), (qlo, khi))):
                nc.tensor.matmul(o[:, 0:w], a[0:rows, j, b * P:(b + 1) * P], c[0:rows, 0:w],
                                 start=(n == 0), stop=False)
            last = nc.tensor.matmul(o[:, w - 256:w], ident_r[:], cmask[:, 0 if b == 0 else 1, :],
                                    start=False, stop=True)
        last.then_inc(S("head_s"), 1)

    T_MX, T_NM, T_L, T_R, T_RL = 0, 8, 16, 24, 32
    T_LAM, T_OG = 42, 43

    def tc(t, b, j, n=1):
        return tiny[:, t + 2 * b + j:t + 2 * b + j + n]

    def softmax_dve(dve, ph, u, b, scale):
        sub = 2 if ph == "a" else 1
        w = SW[b]
        n = u * NB + (b + 1)
        dve.wait_ge(*at_head(ph, "s", n))
        for j in range(sub):
            o = score_bank(sub, b, j)
            nc.vector.reduce_max(tc(T_MX, b, j), o[:, 0:w], AX).then_inc(S("head_mx"), 1)
        dve.wait_ge(*at_head(ph, "mx", n * sub))
        nc.vector.tensor_scalar(tc(T_NM, b, 0, sub), tc(T_MX, b, 0, sub), -scale, None,
                                ALU.mult).then_inc(S("head_nm"), 1)

    def softmax_act(act, ph, u, b, scale):
        sub = 2 if ph == "a" else 1
        w = SW[b]
        act.wait_ge(*at_head(ph, "nm", u * NB + (b + 1)))
        for j in range(sub):
            o = score_bank(sub, b, j)
            dst = pn[:, b, 0:w] if j == 0 else e1[:, b % 2, 0:w]
            nc.scalar.activation(dst, o[:, 0:w], ACT.Exp, bias=tc(T_NM, b, j),
                                 scale=scale, accum_out=tc(T_L, b, j)).then_inc(S("head_e"), 1)

    def probs_dve(dve, ph, u, b):
        sub = 2 if ph == "a" else 1
        w = SW[b]
        n = u * NB + (b + 1)
        dve.wait_ge(*at_head(ph, "e", n * sub))
        nc.vector.reciprocal(tc(T_R, b, 0, sub), tc(T_L, b, 0, sub)).then_inc(S("head_r"), 1)
        dve.wait_ge(*at_head(ph, "r", n))
        if sub == 2:
            nc.vector.tensor_tensor(tc(T_RL, b, 0), tc(T_R, b, 1),
                                    tiny[:, T_LAM:T_LAM + 1], ALU.mult).then_inc(S("head_rl"), 1)
            dve.wait_ge(*at_head(ph, "rl", n))
            nc.vector.tensor_scalar(e1[:, b % 2, 0:w], e1[:, b % 2, 0:w], tc(T_RL, b, 0), None,
                                    ALU.mult).then_inc(S("head_e1"), 1)
            dve.wait_ge(*at_head(ph, "e1", n))
            nc.vector.scalar_tensor_tensor(pn[:, b, 0:w], pn[:, b, 0:w], tc(T_R, b, 0), e1[:, b % 2, 0:w],
                                           ALU.mult, ALU.subtract).then_inc(S("head_p"), 1)
        else:
            nc.vector.tensor_scalar(pn[:, b, 0:w], pn[:, b, 0:w], tc(T_R, b, 0), None,
                                    ALU.mult).then_inc(S("head_p"), 1)

    def ptrans_pe(pe, ph, u, kb):
        if kb == 0:
            pe.wait_ge(*at_head(ph, "p", u * NB + NB))
        if kb >= 2:
            pe.wait_ge(*at_head(ph, "plo", u * NB + (kb - 1)))
        for b in range(kb, NB):
            last = nc.tensor.transpose(bank[TRB[kb % 2]][:, b * P:(b + 1) * P], pn[:, b, kb * P:(kb + 1) * P],
                                       M["ident"])
        last.then_inc(S("head_tr"), 1)

    def pt_slice(t, kb):
        return t[:, TO[kb] + TW[kb] - (SEQ - kb * P):TO[kb] + TW[kb]]

    def ptrans_act(act, ph, u, kb):
        act.wait_ge(*at_head(ph, "tr", u * NB + (kb + 1)))
        nc.scalar.activation(pt_slice(pthi, kb), bank[TRB[kb % 2]][:, kb * P:SEQ], ACT.Copy).then_inc(S("head_phi"), 1)

    def ptrans_dve(dve, ph, u, kb):
        dve.wait_ge(*at_head(ph, "phi", u * NB + (kb + 1)))
        nc.vector.tensor_tensor(pt_slice(ptlo, kb), bank[TRB[kb % 2]][:, kb * P:SEQ], pt_slice(pthi, kb),
                                ALU.subtract).then_inc(S("head_plo"), 1)

    def values_pe(pe, ph, u, kb, s=0):
        pe.wait_ge(*at_head(ph, "plo", u * NB + (kb + 1)))
        if ph == "b" and kb == 0:
            pe.wait_ge(*at_head("b", "mlo", u))
        dv = P if ph == "a" else B_V
        for n, (a, c) in enumerate(((vhi, pthi), (vhi, ptlo), (vlo, pthi))):
            last = nc.tensor.matmul(bank[OB][0:dv, TQ[kb]:SEQ], a[:, kb, s * dv:(s + 1) * dv], c[:, TO[kb]:TO[kb] + TW[kb]],
                                    start=(kb == 0 and n == 0), stop=(kb == NB - 1 and n == 2))
        if kb == NB - 1:
            last.then_inc(S("head_o"), 1)

    def vtrans_pe(pe, ph, u, vb=TRB[0]):
        pe.wait_ge(*at_head(ph, "vy", u + 1))
        for b in range(NB):
            last = nc.tensor.transpose(bank[vb][:, b * P:(b + 1) * P], yv[:, b * P:(b + 1) * P], M["ident"])
        last.then_inc(S("head_vt"), 1)

    def v_parts(ph, t, s, vb):
        dv, at = (P, 0) if ph == "a" else (B_V, P - B_V)
        src = bank[vb][:].rearrange("p (b n) -> p b n", n=P)[:, :, at:at + dv]
        return t[:, :, s * dv:(s + 1) * dv], src

    def v_act(act, ph, u, s=0, vb=TRB[0]):
        act.wait_ge(*at_head(ph, "vt", u + 1))
        o, i = v_parts(ph, vhi, s, vb)
        nc.scalar.activation(o, i, ACT.Copy).then_inc(S("head_vhi"), 1)

    def v_dve(dve, ph, u, s=0, vb=TRB[0]):
        dve.wait_ge(*at_head(ph, "vhi", u + 1))
        o, i = v_parts(ph, vlo, s, vb)
        nc.vector.tensor_tensor(o, i, v_parts(ph, vhi, s, vb)[0], ALU.subtract).then_inc(S("head_vlo"), 1)

    def a_osum_pe(pe, u):
        pe.wait_ge(*at_head("a", "osq", u + 1))
        rs_sum_pe(rs_a(u, "out"), [(sqb, P)], M["ones"][:, 0:1], 1, KSB)

    def a_osq_act(act, u):
        act.wait_ge(*at_head("a", "o", u + 1))
        nc.scalar.activation(sqb[:], bank[OB][:], ACT.Square).then_inc(S("head_osq"), 1)

    def a_mhi_act(act, u):
        act.wait_ge(*at_head("a", "on", u + 1))
        nc.scalar.activation(tile_at(mhi, u), as3(on[:], u), ACT.Copy).then_inc(S("head_mhi"), 1)

    def a_out_dve(dve, u):
        nc.vector.tensor_scalar(on[:], bank[OB][:], tiny[:, T_OG:T_OG + 1], None, ALU.mult).then_inc(S("head_og2"), 1)
        rs_newton_dve(dve, rs_a(u, "out"), 1)
        dve.wait_ge(*at_head("a", "og2", u + 1))
        dve.wait_ge(S("rs_spread"), rs_a(u, "out") + 1)
        nc.vector.tensor_tensor(on[:], on[:], bank[MMB][:], ALU.mult).then_inc(S("head_on"), 1)

    def a_mlo_dve(dve, u):
        dve.wait_ge(*at_head("a", "mhi", u + 1))
        nc.vector.tensor_tensor(tile_at(mlo, u), as3(on[:], u), tile_at(mhi, u),
                                ALU.subtract).then_inc(S("head_mlo"), 1)
        dve.wait_ge(*at_head("a", "mlo", u + 1))

    def qk_sum_pe(pe, ph, t, u, r, rows, m, nh, b):
        pe.wait_ge(*at_head(ph, t + "sq", u + 1))
        rs_sum_pe(r, [(sqb, rows)], M[m][:, 0:64 * nh:64], nh, b)

    def qk_rot_pe(pe, ph, t, u, rows, m):
        pe.wait_ge(*at_head(ph, t + "t", u + 1))
        nc.tensor.matmul(bank[MMB][0:rows, :], M[m][0:rows, 0:rows], tb[0:rows, :], start=True,
                         stop=True).then_inc(S(f"head_{t}rot"), 1)

    def qk_t_dve(dve, ph, t, u, r, rows, y, gain, b, out):
        dve.wait_ge(S("rs_spread"), r + 1)
        nc.vector.scalar_tensor_tensor(out[0:rows, :], y[0:rows, :], gain, bank[b][0:rows, :], ALU.mult,
                                       ALU.mult).then_inc(S(f"head_{t}t"), 1)

    def qk_cos_pool(pool, ph, t, u, rows, y, tab):
        pool.wait_ge(*at_head(ph, t + "t", u + 1))
        nc.gpsimd.tensor_tensor(y[0:rows, :], tb[0:rows, :], tab[0:rows, 0, :], ALU.mult).then_inc(S(f"head_{t}c"), 1)

    def qk_rope_dve(dve, ph, t, u, rows, y, tab):
        dve.wait_ge(*at_head(ph, t + "rot", u + 1))
        dve.wait_ge(*at_head(ph, t + "c", u + 1))
        nc.vector.tensor_tensor(tb[0:rows, :], bank[MMB][0:rows, :], tab[0:rows, 1, :], ALU.mult).then_inc(S(f"head_{t}s"), 1)
        dve.wait_ge(*at_head(ph, t + "s", u + 1))
        nc.vector.tensor_tensor(y[0:rows, :], y[0:rows, :], tb[0:rows, :], ALU.add).then_inc(S(f"head_{t}y2"), 1)
        dve.wait_ge(*at_head(ph, t + "y2", u + 1))


    def a_proj_pe(pe, u, t):
        c = "qkv".index(t)
        g = u * 3 + (G_A + c)
        if t == "q" and not (isinstance(u, int) and u == 0):
            pe.wait_ge(*at_head("a", "vy", u))
        if t == "v":
            pe.wait_ge(*at_head("a", "qy", u + 1))
        project(pe, g, slot(G_A + c), bank[PJ[c % 2]][:], h_hi, h_lo)

    def a_y_dve(dve, u, t):
        c = "qkv".index(t)
        dve.wait_ge(S("chunk_done"), u * 3 + (G_A + c + 1))
        y = (yq, yk, yv)[c]
        if t == "k" and not (isinstance(u, int) and u == 0):
            dve.wait_ge(*at_head("a", "klo", u))
        nc.vector.tensor_tensor(y[:], bank[PJ[c % 2]][:], rstd[:], ALU.mult).then_inc(S(f"head_{t}y"), 1)

    def a_sq_act(act, u, t):
        act.wait_ge(*at_head("a", t + "y", u + 1))
        nc.scalar.activation(sqb[:], (yq, yk)["qk".index(t)][:], ACT.Square).then_inc(S(f"head_{t}sq"), 1)

    def a_qslot_act(act, u):
        act.wait_ge(*at_head("a", "qy2", u + 1))
        if not (isinstance(u, int) and u == 0):
            act.wait_ge(*at_head("a", "s", u * NB))
        for j in range(2):
            r = slice(64 * j, 64 * j + 64)
            nc.scalar.activation(qhi[r, j, :], yq[r, :], ACT.Copy).then_inc(S("head_qhi"), 1)

    def a_kslot_act(act, u):
        act.wait_ge(*at_head("a", "ky2", u + 1))
        nc.scalar.activation(khi[:], yk[:], ACT.Copy).then_inc(S("head_khi"), 1)

    def a_qslot_dve(dve, u):
        dve.wait_ge(*at_head("a", "qhi", u * 2 + 2))
        for j in range(2):
            r = slice(64 * j, 64 * j + 64)
            nc.vector.tensor_tensor(qlo[r, j, :], yq[r, :], qhi[r, j, :], ALU.subtract).then_inc(S("head_qlo"), 1)

    def a_kslot_pool(pool, u):
        pool.wait_ge(*at_head("a", "khi", u + 1))
        nc.gpsimd.tensor_tensor(klo[:], yk[:], khi[:], ALU.subtract).then_inc(S("head_klo"), 1)

    B_LOOP = (B_HEADS - 3) // 2
    A_SCALE = A_DIM ** -0.5
    B_SCALE = B_QK ** -0.5

    def b_load(sp, u, s):
        src = w_b[u, :, :] if isinstance(u, int) else w_b[bass.ds(u, 1), :, :].rearrange("o p n -> p (o n)")
        sp.dma_start(bwraw[:, s, :], src).then_inc(S(f"b_in{s}"), 16)

    def b_hi_act(act, s, use):
        act.wait_ge(S(f"b_in{s}"), use * 16)
        nc.scalar.activation(bwhi[:, s, :], bwraw[:, s, :], ACT.Copy).then_inc(S("head_whi"), 1)

    def b_lo_pool(pool, u, s):
        pool.wait_ge(*at_head("b", "whi", u + 1))
        nc.gpsimd.tensor_tensor(bwlo[:, s, :], bwraw[:, s, :], bwhi[:, s, :], ALU.subtract).then_inc(S("head_wlo"), 1)

    def b_proj_pe(pe, u, s):
        pe.wait_ge(*at_head("b", "wlo", u + 1))
        if not (isinstance(u, int) and u == 0):
            pe.wait_ge(*at_head("b", "vy", u))
        n = 0
        for kt in range(2):
            c = slice(kt * B_QK, (kt + 1) * B_QK)
            for a, o in ((bwhi, qlhi), (bwhi, qllo), (bwlo, qlhi)):
                last = nc.tensor.matmul(bank[PJ[0]][0:B_QK, :], a[:, s, c], o[:, kt, :], start=(n == 0), stop=(n == 5))
                n += 1
        last.then_inc(S("head_q"), 1)

    def b_proj_kv_pe(pe, s):
        for n, (a, o) in enumerate(((bwhi, kvhi), (bwhi, kvlo), (bwlo, kvhi))):
            last = nc.tensor.matmul(bank[PJ[1]][:], a[:, s, 2 * B_QK:], o[:], start=(n == 0), stop=(n == 2))
        last.then_inc(S("head_kv"), 1)

    def b_squares(u):
        return (sqb, yk) if isinstance(u, int) and u == 0 else (e1[:, 0, :], e1[:, 1, :])

    def b_squares_act(act, u):
        q2, k2 = b_squares(u)
        act.wait_ge(*at_head("b", "q", u + 1))
        nc.scalar.activation(q2[0:B_QK, :], bank[PJ[0]][0:B_QK, :], ACT.Square).then_inc(S("head_qsq"), 1)
        act.wait_ge(*at_head("b", "kv", u + 1))
        nc.scalar.activation(k2[0:B_NOPE, :], bank[PJ[1]][0:B_NOPE, :], ACT.Square).then_inc(S("head_ksq"), 1)

    def b_copies_act(act, u):
        act.wait_ge(*at_head("b", "qlo", u))
        nc.scalar.activation(yq[0:B_QK, :], bank[PJ[0]][0:B_QK, :], ACT.Copy).then_inc(S("head_qy"), 1)
        nc.scalar.activation(yv[:], bank[PJ[1]][:], ACT.Copy).then_inc(S("head_vy"), 1)

    def b_sums_pe(pe, u):
        pe.wait_ge(*at_head("b", "qsq", u + 1))
        pe.wait_ge(*at_head("b", "ksq", u + 1))
        q2, k2 = b_squares(u)
        for i in range(NB):
            c = slice(i * P, (i + 1) * P)
            nc.tensor.matmul(bank[MMB][:, 3 * i:3 * i + 2], q2[0:B_QK, c], M["blk_b"][0:B_QK, 0:128:64],
                             start=True, stop=True)
            last = nc.tensor.matmul(bank[MMB][:, 3 * i + 2:3 * i + 3], k2[0:B_NOPE, c],
                                    M["blk_b"][0:B_NOPE, 0:1], start=True, stop=True)
        last.then_inc(S("rs_sum"), 1)

    def b_spread_k_pe(pe, u):
        for i in range(NB):
            col = T_Z[0] + 3 * i + 2
            last = nc.tensor.matmul(bank[KMB][0:B_NOPE, i * P:(i + 1) * P],
                                    tiny[:, col:col + 1].broadcast_to([P, B_NOPE]), M["ident"],
                                    start=True, stop=True)
        last.then_inc(S("rs_k_spread"), 1)

    def b_q_dve(dve, u):
        dve.wait_ge(*at_head("b", "qy", u + 1))
        qk_t_dve(dve, "b", "q", u, rs_b(u), B_QK, yq, v(V_BQ, rows=B_QK), MMB, tb)

    def b_k_dve(dve, u):
        dve.wait_ge(*at_head("b", "vy", u + 1))
        dve.wait_ge(S("rs_k_spread"), u + 1)
        dve.wait_ge(*at_head("b", "klo", u))
        nc.vector.scalar_tensor_tensor(yk[0:B_NOPE, :], yv[0:B_NOPE, :], v(V_BK, rows=B_NOPE),
                                       bank[KMB][0:B_NOPE, :], ALU.mult, ALU.mult).then_inc(S("head_kt"), 1)

    def b_qslot_act(act, u):
        act.wait_ge(*at_head("b", "qy2", u + 1))
        act.wait_ge(*at_head("b", "s", u * NB))
        nc.scalar.activation(qhi[0:B_QK, 0, :], yq[0:B_QK, :], ACT.Copy).then_inc(S("head_qhi"), 1)

    def b_kslot_act(act, u):
        act.wait_ge(*at_head("b", "kt", u + 1))
        nc.scalar.activation(khi[0:B_NOPE, :], yk[0:B_NOPE, :], ACT.Copy).then_inc(S("head_khi"), 1)

    def b_qslot_pool(pool, u):
        pool.wait_ge(*at_head("b", "qhi", u + 1))
        nc.gpsimd.tensor_tensor(qlo[0:B_QK, 0, :], yq[0:B_QK, :], qhi[0:B_QK, 0, :], ALU.subtract).then_inc(S("head_qlo"), 1)

    def b_kslot_pool(pool, u):
        pool.wait_ge(*at_head("b", "khi", u + 1))
        nc.gpsimd.tensor_tensor(klo[0:B_NOPE, :], yk[0:B_NOPE, :], khi[0:B_NOPE, :], ALU.subtract).then_inc(S("head_klo"), 1)

    def head_out_act(act, ph, u, j, k):
        act.wait_ge(*at_head(ph, "o", u + 1))
        nc.scalar.activation(tile_at(mhi, k, slice(64 * j, 64 * j + 64)), as3(bank[OB][0:64, :], k),
                             ACT.Copy).then_inc(S("head_mhi"), 1)

    def head_out_dve(dve, ph, u, j, k):
        dve.wait_ge(*at_head(ph, "mhi", u + 1))
        r = slice(64 * j, 64 * j + 64)
        nc.vector.tensor_tensor(tile_at(mlo, k, r), as3(bank[OB][0:64, :], k), tile_at(mhi, k, r),
                                ALU.subtract).then_inc(S("head_mlo"), 1)

    ZB = ((0, 1, 2), (3, 4, 5))
    CP, CO = 6, 7
    ZAT = ((0, 0), (1, 0), (2, 0), (2, 256))
    BW = (512, 384, 512)
    BO = (0, 512, 896)

    def c_proj_bank(u, c):
        return bank[(CP, *ZB[0])[c]] if isinstance(u, int) and u == 0 else bank[CP]

    def c_proj_pe(pe, u, t, n=None):
        c = "qkv".index(t)
        if not (isinstance(u, int) and u == 0):
            if t == "q":
                pe.wait_ge(S("c_vy"), u)
            else:
                pe.wait_ge(S("c_qy" if t == "k" else "c_ky"), u + 1)
        project(pe, u * 3 + (G_C + c), slot(G_C + c), c_proj_bank(u, c)[:], h_hi, h_lo, n)

    def c_scores_pe(pe, u, j):
        if j == 0:
            pe.wait_ge(S("c_qlo"), u * 2 + 2)
            pe.wait_ge(S("c_klo"), u + 1)
        for kb in range(NB):
            b, o = ZAT[kb]
            z = bank[ZB[j][b]][:, o:o + TW[kb]]
            for n, (a, c) in enumerate(((ckhi, cqhi), (ckhi, cqlo), (cklo, cqhi))):
                nc.tensor.matmul(z, a[:, kb * P:(kb + 1) * P], c[:, j, TQ[kb]:SEQ],
                                 start=(n == 0 and kb < 3), stop=False, skip_group_check=True)
            last = nc.tensor.matmul(z[:, 0:256], ident_r[:], csmask[:, 1 if kb == 3 else 0, :], start=False,
                                    stop=True, skip_group_check=True)
            if kb != 2:
                last.then_inc(S(f"c_z{j}"), 1)

    def c_chain_act(act, u, j, b):
        z, a = bank[ZB[j][b]][:, 0:BW[b]], ca[j][:, BO[b]:BO[b] + BW[b]]
        n = u * 3 + (b + 1)
        act.wait_ge(S(f"c_z{j}"), n)
        nc.scalar.activation(a, z, ACT.Abs).then_inc(S(f"c_abs{j}"), 1)
        act.wait_ge(S(f"c_abs{j}"), n)
        nc.scalar.activation(a, a, ACT.Exp, scale=-1.0).then_inc(S(f"c_ex{j}"), 1)
        act.wait_ge(S(f"c_ex{j}"), n)
        nc.scalar.activation(a, a, ACT.Ln, bias=1.0).then_inc(S(f"c_ln{j}"), 1)

    def c_chain_dve(dve, u, j, b):
        z = bank[ZB[j][b]][:, 0:BW[b]]
        r = slice(BO[b], BO[b] + BW[b])
        n = u * 3 + (b + 1)
        dve.wait_ge(S(f"c_ln{j}"), n)
        nc.vector.scalar_tensor_tensor(cs[:, r], z, 0.0, ca[j][:, r], ALU.max, ALU.add).then_inc(S(f"c_sp{j}"), 1)
        dve.wait_ge(S(f"c_sp{j}"), n)
        nc.vector.tensor_copy(cshi[j][:, r], cs[:, r]).then_inc(S(f"c_shi{j}"), 1)
        dve.wait_ge(S(f"c_shi{j}"), n)
        nc.vector.tensor_tensor(cslo[j][:, r], cs[:, r], cshi[j][:, r], ALU.subtract).then_inc(S(f"c_slo{j}"), 1)

    def c_tail_pe(pe, u, j):
        pe.wait_ge(S(f"c_slo{j}"), u * 3 + 3)
        for kb in range(NB):
            b, o = ZAT[kb]
            for src in range(kb, NB):
                w = TW[src]
                z = bank[ZB[j][b]][:, o + TW[kb] - w:o + TW[kb]]
                for t in (cshi, cslo):
                    last = nc.tensor.matmul(z, cmats[:, 0 if src == kb else 1, :], t[j][:, TO[src]:TO[src] + w],
                                            start=False, stop=True, skip_group_check=True)
            if kb != 2:
                last.then_inc(S(f"c_tail{j}"), 1)

    def c_w_act(act, u, j, b):
        act.wait_ge(S(f"c_tail{j}"), u * 3 + (b + 1))
        a = ca[j][:, BO[b]:BO[b] + BW[b]]
        nc.scalar.activation(a, bank[ZB[j][b]][:, 0:BW[b]], ACT.Exp).then_inc(S(f"c_w{j}"), 1)

    def c_w_dve(dve, u, j, b):
        r = slice(BO[b], BO[b] + BW[b])
        n = u * 3 + (b + 1)
        dve.wait_ge(S(f"c_w{j}"), n)
        if b == 0:
            dve.wait_ge(S(f"c_tail{j}"), u * 3 + 3)
        nc.vector.tensor_copy(cshi[j][:, r], ca[j][:, r]).then_inc(S(f"c_whi{j}"), 1)
        dve.wait_ge(S(f"c_whi{j}"), n)
        nc.vector.tensor_tensor(cslo[j][:, r], ca[j][:, r], cshi[j][:, r], ALU.subtract).then_inc(S(f"c_wlo{j}"), 1)

    def c_values_pe(pe, u, j):
        if j == 0:
            pe.wait_ge(S("c_vlo"), u + 1)
        else:
            pe.wait_ge(S("c_mlo"), u * 2 + 1)
        for kb in range(NB):
            if kb < 3:
                pe.wait_ge(S(f"c_wlo{j}"), u * 3 + (kb + 1))
            for n, (a, c) in enumerate(((cvhi, cshi), (cvhi, cslo), (cvlo, cshi))):
                last = nc.tensor.matmul(bank[CO][0:64, TQ[kb]:SEQ], a[:, kb, 64 * j:64 * j + 64],
                                        c[j][:, TO[kb]:TO[kb] + TW[kb]], start=(kb == 0 and n == 0),
                                        stop=(kb == NB - 1 and n == 2))
        last.then_inc(S("c_o"), 1)

    def c_y_dve(dve, u, t):
        c = "qkv".index(t)
        dve.wait_ge(S("chunk_done"), u * 3 + (G_C + c + 1))
        y = (cyq, cyk, cyv)[c]
        if t == "q":
            nc.vector.scalar_tensor_tensor(y[:], c_proj_bank(u, c)[:], C_DIM ** -0.5, rstd[:], ALU.mult,
                                           ALU.mult).then_inc(S("c_qy"), 1)
        else:
            nc.vector.tensor_tensor(y[:], c_proj_bank(u, c)[:], rstd[:], ALU.mult).then_inc(S(f"c_{t}y"), 1)

    def c_slot_act(act, u, t):
        act.wait_ge(S(f"c_{t}y"), u + 1)
        if t == "k":
            nc.scalar.activation(ckhi[:], cyk[:], ACT.Copy).then_inc(S("c_khi"), 1)
        else:
            for j in range(2):
                r = slice(64 * j, 64 * j + 64)
                nc.scalar.activation(cqhi[r, j, :], cyq[r, :], ACT.Copy).then_inc(S("c_qhi"), 1)

    def c_slot_dve(dve, u, t):
        if t == "k":
            dve.wait_ge(S("c_khi"), u + 1)
            nc.vector.tensor_tensor(cklo[:], cyk[:], ckhi[:], ALU.subtract).then_inc(S("c_klo"), 1)
        else:
            dve.wait_ge(S("c_qhi"), u * 2 + 2)
            for j in range(2):
                r = slice(64 * j, 64 * j + 64)
                nc.vector.tensor_tensor(cqlo[r, j, :], cyq[r, :], cqhi[r, j, :], ALU.subtract).then_inc(S("c_qlo"), 1)

    def c_vt_pe(pe, u):
        pe.wait_ge(S("c_vy"), u + 1)
        for b in range(NB):
            last = nc.tensor.transpose(bank[CO][:, b * P:(b + 1) * P], cyv[:, b * P:(b + 1) * P], M["ident"])
        last.then_inc(S("c_vt"), 1)

    def c_v_act(act, u):
        act.wait_ge(S("c_vt"), u + 1)
        nc.scalar.activation(cvhi[:], bank[CO][:].rearrange("p (b n) -> p b n", n=P), ACT.Copy).then_inc(S("c_vhi"), 1)

    def c_v_dve(dve, u):
        dve.wait_ge(S("c_vhi"), u + 1)
        nc.vector.tensor_tensor(cvlo[:], bank[CO][:].rearrange("p (b n) -> p b n", n=P), cvhi[:],
                                ALU.subtract).then_inc(S("c_vlo"), 1)

    with nc.Block() as block:

        @block.sync
        def _(sp):
            for d in range(KT):
                sp.dma_start(x[:, d, :], xt[d, :, :]).then_inc(S(f"x_in{d}"), 16)
                if d == 0:
                    load_chunk(sp, 0, 0, 1, w_in[0, :, :], W_IN)
            sp.dma_start(mat[:], mats[:, :, :]).then_inc(S("mat_in"), 16)
            for g in (1, 2):
                load_chunk(sp, g, g, 1, w_in[g, :, :], W_IN)
            sp.dma_start(tabb[:], tabs_b[:, :, :]).then_inc(S("tabb_in"), 16)
            sp.dma_start(taba[:], tabs_a[:, :, :]).then_inc(S("taba_in"), 16)
            sp.dma_start(rawm[:], masks_a[:, :, :]).then_inc(S("masks_in"), 16)

            def run(g0, n, src, first, width):
                loops = n // WSLOTS
                if loops > 1:
                    with sp.Fori(0, loops) as i:
                        for j in range(WSLOTS):
                            load_chunk(sp, i * WSLOTS + (g0 + j), slot(g0 + j), None,
                                       src[bass.ds(i * WSLOTS + (first + j), 1), :, :].rearrange("o p n -> p (o n)"),
                                       width)
                else:
                    loops = 0
                for k in range(loops * WSLOTS, n):
                    load_chunk(sp, g0 + k, slot(g0 + k), None, src[first + k, :, :], width)

            run(3, G_OUT0, w_in, 3, W_IN)
            sp.wait_ge(S("chunk_done"), G_OUT0)
            for u in range(2):
                b_load(sp, u, u)
            with sp.Fori(1, B_HEADS // 2) as i:
                for s in range(2):
                    sp.wait_ge(*at_head("b", "wlo", i * 2 + (s - 1)))
                    b_load(sp, i * 2 + s, s)
            run(G_OUT0 + 3, KT - 3, w_in, G_OUT0 + 3, W_IN)
            sp.wait_ge(S("chunk_done"), G_OUT0 + 1)
            sp.dma_start(crawm[:], masks_c[:, :]).then_inc(S("crawm_in"), 16)
            row, down = G_OUT0 + KT, 0
            for s in range(2):
                run(G_FFN0 + s * FFN_HALF, 2 * HALF_F, w_in, row, W_IN)
                row += 2 * HALF_F
                run(G_FFN0 + s * FFN_HALF + 2 * HALF_F, KT, w_down, down, W_DOWN)
                down += KT
            run(G_C, 3 * C_PAIRS, w_in, row, W_IN)
            row += 3 * C_PAIRS
            run(G_OUT1, KT, w_in, row, W_IN)
            row += KT
            for s in range(2):
                run(G_FFN1 + s * FFN_HALF, 2 * HALF_F, w_in, row, W_IN)
                row += 2 * HALF_F
                run(G_FFN1 + s * FFN_HALF + 2 * HALF_F, KT, w_down, down, W_DOWN)
                down += KT
            for d in range(KT):
                sp.wait_ge(*at_net(1, "x", KT + d + 1))
                sp.dma_start(out[d, :, :], x[:, d, :]).then_inc(S("out"), 16)
            sp.wait_ge(S("out"), 16 * KT)

        @block.gpsimd
        def _(pool):
            def run(g0, n, width):
                loops = n // WSLOTS
                if loops > 1:
                    with pool.Fori(0, loops) as i:
                        for j in range(WSLOTS):
                            split_lo(pool, i * WSLOTS + (g0 + j), slot(g0 + j), width)
                else:
                    loops = 0
                for k in range(loops * WSLOTS, n):
                    split_lo(pool, g0 + k, slot(g0 + k), width)

            split_lo(pool, 0, 0, W_IN)
            for d in range(1, KT):
                norm_pool(pool, 0, d)
            for g in (1, 2):
                split_lo(pool, g, g, W_IN)
            for g in range(3, G_A + 3):
                split_lo(pool, g, slot(g), W_IN)
            pool.wait_ge(S("tabb_in"), 16)
            qk_cos_pool(pool, "r", "q", 0, B_QK, on, tabb)
            pool.wait_ge(S("taba_in"), 16)

            def a_pool(nxt, g):
                split_lo(pool, g, slot(G_A), W_IN)
                qk_cos_pool(pool, "a", "q", nxt, P, yq, taba)
                split_lo(pool, g + 1, slot(G_A + 1), W_IN)
                qk_cos_pool(pool, "a", "k", nxt, P, yk, taba)
                split_lo(pool, g + 2, slot(G_A + 2), W_IN)
                a_kslot_pool(pool, nxt)

            a_pool(0, G_A + 3)
            with pool.Fori(1, A_HEADS) as i:
                a_pool(i, i * 3 + (G_A + 3))

            def b_pool(nxt):
                qk_cos_pool(pool, "b", "q", nxt, B_QK, yq, tabb)
                b_kslot_pool(pool, nxt)
                b_qslot_pool(pool, nxt)

            for u in range(2):
                b_lo_pool(pool, u, u)
            b_pool(0)
            b_lo_pool(pool, 2, 0)
            with pool.Fori(0, B_LOOP) as i:
                for s in range(2):
                    b_pool(i * 2 + (s + 1))
                    b_lo_pool(pool, i * 2 + (s + 3), 1 - s)
            for u in range(2 * B_LOOP, B_HEADS - 1):
                b_pool(u + 1)
                if u + 3 < B_HEADS:
                    b_lo_pool(pool, u + 3, (u + 3) % 2)
            for d in range(KT):
                split_lo(pool, G_OUT0 + d + 3, slot(G_OUT0 + d + 3), width_of(G_OUT0 + d + 3))
                norm_pool(pool, 1, d)
            for L, g_first in ((0, G_FFN0), (1, G_FFN1)):
                run(g_first + 3, 2 * HALF_F - 3, W_IN)
                run(g_first + 2 * HALF_F, KT, W_DOWN)
                run(g_first + FFN_HALF, 2 * HALF_F, W_IN)
                gd = g_first + FFN_HALF + 2 * HALF_F
                run(gd, 3, W_DOWN)
                for d in range(KT):
                    if gd + d + 3 < N_CHUNKS:
                        split_lo(pool, gd + d + 3, slot(gd + d + 3), width_of(gd + d + 3))
                    if L == 0:
                        norm_pool(pool, 2, d)
                if L == 0:
                    run(G_C + 3, 3 * C_PAIRS - 3, W_IN)
                    run(G_OUT1, 3, W_IN)
                    for d in range(KT):
                        split_lo(pool, G_OUT1 + d + 3, slot(G_OUT1 + d + 3), width_of(G_OUT1 + d + 3))
                        norm_pool(pool, 3, d)

        @block.scalar
        def _(act):
            act.preload_act_table_set("natural_log_exp_and_others")
            act.dma_start(vec[:], vecs[:, :]).then_inc(S("vec_in"), 16)
            act.wait_ge(S("vec_in"), 16)
            for d in range(KT):
                act.wait_ge(S(f"x_in{d}"), 16)
                norm_act(act, 0, d)
                if d in (0, 6, 7):
                    hi_static(act, (0, 6, 7).index(d))
            act.wait_ge(S("lam_sum"), 1)
            nc.scalar.activation(tiny[:, 102:104], bank[5][:, 0:2], ACT.Exp).then_inc(S("lam_exp"), 1)
            rs_act(act, RS_NORM[0], 1)
            hi_static(act, 3)
            act.wait_ge(S("l_y"), 1)
            nc.scalar.activation(sqb[:], yq[:], ACT.Square).then_inc(S("l_sq"), 1)
            hi_static(act, 4)
            act.wait_ge(S("l_y"), 2)
            nc.scalar.activation(tb[:], yk[:], ACT.Square).then_inc(S("l_sq"), 1)
            rs_act(act, RS_QL, 1)
            hi_static(act, 5)
            act.wait_ge(S("l_y"), 3)
            nc.scalar.activation(sqb[:], yv[:], ACT.Square).then_inc(S("l_sq"), 1)
            for k in range(2):
                act.wait_ge(S("l_n"), k + 1)
                nc.scalar.activation(qlhi[:, k, :], (yq, yk)[k][:], ACT.Copy).then_inc(S("l_hi"), 1)
            hi_static(act, 6)
            rs_act(act, RS_KVL, 1)
            act.wait_ge(S("l_y"), 4)
            nc.scalar.activation(sqb[0:B_QK, :], on[0:B_QK, :], ACT.Square).then_inc(S("head_qsq"), 1)
            act.wait_ge(S("l_n"), 3)
            nc.scalar.activation(kvhi[:], yv[:], ACT.Copy).then_inc(S("l_hi"), 1)
            hi_static(act, G_A + 3)
            rs_act(act, RS_ROPE, 2)
            a_sq_act(act, 0, "q")
            hi_static(act, G_A + 4)
            rs_act(act, rs_a(0, "q"), 2)
            a_sq_act(act, 0, "k")
            hi_static(act, G_A + 5)
            rs_act(act, rs_a(0, "k"), 2)
            a_qslot_act(act, 0)
            a_kslot_act(act, 0)
            v_act(act, "a", 0)

            def a_act(u, nxt, hi):
                softmax_act(act, "a", u, 0, A_SCALE)
                softmax_act(act, "a", u, 1, A_SCALE)
                a_sq_act(act, nxt, "q")
                hi(0)
                softmax_act(act, "a", u, 2, A_SCALE)
                softmax_act(act, "a", u, 3, A_SCALE)
                rs_act(act, rs_a(nxt, "q"), 2)
                hi(1)
                a_sq_act(act, nxt, "k")
                ptrans_act(act, "a", u, 0)
                ptrans_act(act, "a", u, 1)
                rs_act(act, rs_a(nxt, "k"), 2)
                hi(2)
                ptrans_act(act, "a", u, 2)
                ptrans_act(act, "a", u, 3)
                a_qslot_act(act, nxt)
                a_kslot_act(act, nxt)
                a_osq_act(act, u)
                rs_act(act, rs_a(u, "out"), 1)
                v_act(act, "a", nxt)
                a_mhi_act(act, u)

            with act.Fori(0, A_HEADS - 1) as i:
                a_act(i, i + 1, lambda c: hi_at(act, G_A + 6 + c, i, 3))

            u = A_HEADS - 1
            for h in range(2):
                b_hi_act(act, h, 1)
            softmax_act(act, "a", u, 0, A_SCALE)
            softmax_act(act, "a", u, 1, A_SCALE)
            act.wait_ge(*at_head("a", "klo", A_HEADS))
            b_squares_act(act, 0)
            softmax_act(act, "a", u, 2, A_SCALE)
            softmax_act(act, "a", u, 3, A_SCALE)
            b_copies_act(act, 0)
            act.wait_ge(*at_head("r", "kept", 1))
            nc.scalar.activation(khi[64:96, :], rope_keep[64:96, :], ACT.Copy).then_inc(S("kr_hi"), 1)
            rs_act(act, rs_b(0), 3)
            ptrans_act(act, "a", u, 0)
            b_hi_act(act, 0, 2)
            ptrans_act(act, "a", u, 1)
            b_kslot_act(act, 0)
            ptrans_act(act, "a", u, 2)
            b_qslot_act(act, 0)
            ptrans_act(act, "a", u, 3)
            act.wait_ge(*at_head("a", "p", A_HEADS * NB))
            b_squares_act(act, 1)
            a_osq_act(act, u)
            rs_act(act, rs_a(u, "out"), 1)
            v_act(act, "b", 0)
            a_mhi_act(act, u)

            def b_act(u, n, s, k, hi):
                if n:
                    rs_act(act, rs_b(u + 1), 3)
                softmax_act(act, "b", u, 0, B_SCALE)
                softmax_act(act, "b", u, 1, B_SCALE)
                if n:
                    b_copies_act(act, u + 1)
                softmax_act(act, "b", u, 2, B_SCALE)
                softmax_act(act, "b", u, 3, B_SCALE)
                ptrans_act(act, "b", u, 0)
                if hi is not None:
                    b_hi_act(act, 1 - s, hi)
                ptrans_act(act, "b", u, 1)
                ptrans_act(act, "b", u, 2)
                if n:
                    b_kslot_act(act, u + 1)
                    v_act(act, "b", u + 1, 1 - s, VTB)
                ptrans_act(act, "b", u, 3)
                if n:
                    b_qslot_act(act, u + 1)
                if n > 1:
                    b_squares_act(act, u + 2)
                head_out_act(act, "b", u, s, k)

            with act.Fori(0, B_LOOP) as i:
                for s in range(2):
                    b_act(i * 2 + s, 2, s, i + 4, i + (2 + s))
            for u in range(2 * B_LOOP, B_HEADS):
                b_act(u, min(2, B_HEADS - 1 - u), u % 2, A_HEADS + u // 2,
                      (u + 3) // 2 + 1 if u + 3 < B_HEADS else None)
            out_act(act, G_OUT0, 0, 1)
            rs_act(act, RS_NORM[1], 1)
            ffn_act(act, 0, 2)

            act.preload_act_table_set("natural_log_exp_and_others")
            rs_act(act, RS_NORM[2], 1)

            def c_act(u, nxt, hi):
                if u is not None:
                    for b in range(3):
                        c_chain_act(act, u, 0, b)
                    for b in range(3):
                        c_chain_act(act, u, 1, b)
                if nxt is not None:
                    c_slot_act(act, nxt, "q")
                    hi(0)
                if u is not None:
                    for b in range(3):
                        c_w_act(act, u, 0, b)
                    c_v_act(act, u)
                if nxt is not None:
                    c_slot_act(act, nxt, "k")
                    hi(1)
                if u is not None:
                    for b in range(3):
                        c_w_act(act, u, 1, b)
                    act.wait_ge(S("c_o"), u * 2 + 1)
                    cout_act(u, 0)
                if nxt is not None:
                    act.wait_ge(S("c_vy"), nxt + 1)
                    hi(2)
                if u is not None:
                    act.wait_ge(S("c_o"), u * 2 + 2)
                    cout_act(u, 1)

            def cout_act(u, j):
                nc.scalar.activation(tile_at(mhi, u, slice(64 * j, 64 * j + 64)), as3(bank[CO][0:64, :], u),
                                     ACT.Copy).then_inc(S("c_mhi"), 1)

            c_act(None, 0, lambda c: hi_static(act, G_C + 3 + c))
            with act.Fori(0, C_PAIRS - 1) as i:
                c_act(i, i + 1, lambda c: hi_at(act, G_C + 6 + c, i, 3))
            c_act(C_PAIRS - 1, None, None)
            out_act(act, G_OUT1, 1, 3)
            rs_act(act, RS_NORM[3], 1)
            ffn_act(act, 1, None)

        @block.vector
        def _(dve):
            nc.vector.memset(qhi[64:128, 0, :].bitcast(F32), 0.0)
            nc.vector.memset(qhi[0:64, 1, :].bitcast(F32), 0.0)
            nc.vector.memset(qlo[64:128, 0, :].bitcast(F32), 0.0)
            nc.vector.memset(qlo[0:64, 1, :].bitcast(F32), 0.0)
            nc.vector.memset(pthi[:, TO[3]:TO[3] + P].bitcast(F32), 0.0)
            nc.vector.memset(ptlo[:, TO[3]:TO[3] + P].bitcast(F32), 0.0)
            dve.wait_ge(S("vec_in"), 16)
            nc.vector.tensor_tensor(tiny[:, 100:101], v(V_LAM), v(V_LAM + 1), ALU.mult).then_inc(S("lam_prod"), 1)
            nc.vector.tensor_tensor(tiny[:, 101:102], v(V_LAM + 2), v(V_LAM + 3), ALU.mult).then_inc(S("lam_prod"), 1)
            nc.vector.tensor_scalar(tiny[:, T_OG:T_OG + 1], v(V_AO), 1.0 - LAM0, None, ALU.mult).then_inc(S("head_og"), 1)
            for d in range(KT):
                norm_dve(dve, 0, d)
            dve.wait_ge(S("mat_in"), 16)
            nc.vector.tensor_copy(ident_r[:], M["ident"])
            dve.wait_ge(S("lam_exp"), 1)
            nc.vector.tensor_tensor(tiny[:, 104:105], tiny[:, 102:103], tiny[:, 103:104], ALU.subtract).then_inc(S("lam_dif"), 1)
            dve.wait_ge(S("lam_dif"), 1)
            nc.vector.tensor_scalar(tiny[:, T_LAM:T_LAM + 1], tiny[:, 104:105], LAM0, None, ALU.add).then_inc(S("lam"), 1)
            dve.wait_ge(S("lam"), 1)
            norm_rstd_dve(dve, 0, MMB)
            for c in range(3):
                dve.wait_ge(S("chunk_done"), c + 1)
                nc.vector.tensor_tensor((yq, yk, yv)[c][:], bank[(2, 3, 0)[c]][:], rstd[:], ALU.mult).then_inc(S("l_y"), 1)
            rs_mean_dve(dve, RS_QL, 1.0 / B_QRANK, 1, MMB)
            rs_newton_dve(dve, RS_QL, 1)
            dve.wait_ge(S("rs_spread"), RS_QL + 1)
            for k in range(2):
                y = (yq, yk)[k]
                nc.vector.scalar_tensor_tensor(y[:], y[:], v(V_BQL + k), bank[MMB][:], ALU.mult, ALU.mult).then_inc(S("l_n"), 1)
                dve.wait_ge(S("l_hi"), k + 1)
                nc.vector.tensor_tensor(qllo[:, k, :], y[:], qlhi[:, k, :], ALU.subtract).then_inc(S("l_lo"), 1)
            dve.wait_ge(S("chunk_done"), 4)
            nc.vector.tensor_tensor(on[:], bank[1][:], rstd[:], ALU.mult).then_inc(S("l_y"), 1)
            rs_mean_dve(dve, RS_KVL, 1.0 / B_KVRANK, 1, 5)
            rs_newton_dve(dve, RS_KVL, 1)
            a_y_dve(dve, 0, "q")
            dve.wait_ge(S("rs_spread"), RS_KVL + 1)
            nc.vector.scalar_tensor_tensor(yv[:], yv[:], v(V_BKVL), bank[6][:], ALU.mult, ALU.mult).then_inc(S("l_n"), 1)
            dve.wait_ge(S("l_hi"), 3)
            nc.vector.tensor_tensor(kvlo[:], yv[:], kvhi[:], ALU.subtract).then_inc(S("l_lo"), 1)
            rs_mean_dve(dve, RS_ROPE, 1.0, 2, OB)
            rs_newton_dve(dve, RS_ROPE, 2)
            dve.wait_ge(S("masks_in"), 16)
            nc.vector.tensor_copy(cmask[:], rawm[:])
            a_y_dve(dve, 0, "k")
            dve.wait_ge(S("tabb_in"), 16)
            qk_t_dve(dve, "r", "q", 0, RS_ROPE, B_QK, on, v(V_BKR, rows=B_QK), MMB, tb)
            rs_mean_dve(dve, rs_a(0, "q"), 1.0 / A_DIM, 2, OB)
            rs_newton_dve(dve, rs_a(0, "q"), 2)
            qk_rope_dve(dve, "r", "q", 0, B_QK, on, tabb)
            nc.vector.tensor_copy(rope_keep[64:96, :], on[64:96, :]).then_inc(S("head_kept"), 1)
            dve.wait_ge(*at_head("r", "kept", 1))
            dve.wait_ge(S("taba_in"), 16)
            qk_t_dve(dve, "a", "q", 0, rs_a(0, "q"), P, yq, v(V_AQ), QMB, tb)
            rs_mean_dve(dve, rs_a(0, "k"), 1.0 / A_DIM, 2, KSB)
            rs_newton_dve(dve, rs_a(0, "k"), 2, 1)
            a_y_dve(dve, 0, "v")
            qk_rope_dve(dve, "a", "q", 0, P, yq, taba)
            qk_t_dve(dve, "a", "k", 0, rs_a(0, "k"), P, yk, v(V_AK), KMB, tb)
            a_qslot_dve(dve, 0)
            qk_rope_dve(dve, "a", "k", 0, P, yk, taba)
            v_dve(dve, "a", 0)

            def a_dve(u, nxt):
                softmax_dve(dve, "a", u, 0, A_SCALE)
                softmax_dve(dve, "a", u, 1, A_SCALE)
                probs_dve(dve, "a", u, 0)
                probs_dve(dve, "a", u, 1)
                a_y_dve(dve, nxt, "q")
                softmax_dve(dve, "a", u, 2, A_SCALE)
                softmax_dve(dve, "a", u, 3, A_SCALE)
                probs_dve(dve, "a", u, 2)
                rs_mean_dve(dve, rs_a(nxt, "q"), 1.0 / A_DIM, 2, OB)
                probs_dve(dve, "a", u, 3)
                rs_newton_dve(dve, rs_a(nxt, "q"), 2)
                a_y_dve(dve, nxt, "k")
                qk_t_dve(dve, "a", "q", nxt, rs_a(nxt, "q"), P, yq, v(V_AQ), MMB, tb)
                ptrans_dve(dve, "a", u, 0)
                rs_mean_dve(dve, rs_a(nxt, "k"), 1.0 / A_DIM, 2, KSB)
                ptrans_dve(dve, "a", u, 1)
                qk_rope_dve(dve, "a", "q", nxt, P, yq, taba)
                rs_newton_dve(dve, rs_a(nxt, "k"), 2, 1)
                a_y_dve(dve, nxt, "v")
                qk_t_dve(dve, "a", "k", nxt, rs_a(nxt, "k"), P, yk, v(V_AK), KMB, tb)
                ptrans_dve(dve, "a", u, 2)
                qk_rope_dve(dve, "a", "k", nxt, P, yk, taba)
                ptrans_dve(dve, "a", u, 3)
                a_qslot_dve(dve, nxt)
                rs_mean_dve(dve, rs_a(u, "out"), 1.0 / (2 * A_DIM), 1, KSB)
                a_out_dve(dve, u)
                v_dve(dve, "a", nxt)
                a_mlo_dve(dve, u)

            with dve.Fori(0, A_HEADS - 1) as i:
                a_dve(i, i + 1)

            u = A_HEADS - 1
            softmax_dve(dve, "a", u, 0, A_SCALE)
            softmax_dve(dve, "a", u, 1, A_SCALE)
            probs_dve(dve, "a", u, 0)
            probs_dve(dve, "a", u, 1)
            softmax_dve(dve, "a", u, 2, A_SCALE)
            softmax_dve(dve, "a", u, 3, A_SCALE)
            probs_dve(dve, "a", u, 2)
            rs_mean_dve(dve, rs_b(0), 1.0, 3, MMB)
            probs_dve(dve, "a", u, 3)
            rs_newton_dve(dve, rs_b(0), 3)
            dve.wait_ge(S("kr_hi"), 1)
            nc.vector.tensor_tensor(klo[64:96, :], rope_keep[64:96, :], khi[64:96, :], ALU.subtract).then_inc(S("kr_lo"), 1)
            ptrans_dve(dve, "a", u, 0)
            b_q_dve(dve, 0)
            b_k_dve(dve, 0)
            ptrans_dve(dve, "a", u, 1)
            qk_rope_dve(dve, "b", "q", 0, B_QK, yq, tabb)
            ptrans_dve(dve, "a", u, 2)
            ptrans_dve(dve, "a", u, 3)
            rs_mean_dve(dve, rs_a(u, "out"), 1.0 / (2 * A_DIM), 1, KSB)
            a_out_dve(dve, u)
            v_dve(dve, "b", 0)
            a_mlo_dve(dve, u)

            def b_dve(u, n, s, k):
                if n:
                    rs_mean_dve(dve, rs_b(u + 1), 1.0, 3, MMB)
                softmax_dve(dve, "b", u, 0, B_SCALE)
                if n:
                    rs_newton_dve(dve, rs_b(u + 1), 3)
                softmax_dve(dve, "b", u, 1, B_SCALE)
                probs_dve(dve, "b", u, 0)
                softmax_dve(dve, "b", u, 2, B_SCALE)
                probs_dve(dve, "b", u, 1)
                softmax_dve(dve, "b", u, 3, B_SCALE)
                probs_dve(dve, "b", u, 2)
                probs_dve(dve, "b", u, 3)
                if n:
                    b_q_dve(dve, u + 1)
                ptrans_dve(dve, "b", u, 0)
                if n:
                    b_k_dve(dve, u + 1)
                ptrans_dve(dve, "b", u, 1)
                ptrans_dve(dve, "b", u, 2)
                if n:
                    qk_rope_dve(dve, "b", "q", u + 1, B_QK, yq, tabb)
                    v_dve(dve, "b", u + 1, 1 - s, VTB)
                ptrans_dve(dve, "b", u, 3)
                head_out_dve(dve, "b", u, s, k)

            with dve.Fori(0, B_LOOP) as i:
                for s in range(2):
                    b_dve(i * 2 + s, 2, s, i + 4)
            for u in range(2 * B_LOOP, B_HEADS):
                b_dve(u, min(2, B_HEADS - 1 - u), u % 2, A_HEADS + u // 2)
            out_dve(dve, G_OUT0, 0, 1)
            ffn_dve(dve, 0, 1, 2)

            def c_prepare():
                for t in (cqhi, cqlo):
                    nc.vector.memset(t[64:128, 0, :].bitcast(F32), 0.0)
                    nc.vector.memset(t[0:64, 1, :].bitcast(F32), 0.0)
                dve.wait_ge(S("crawm_in"), 16)
                nc.vector.tensor_copy(cmats[:].rearrange("p m n -> p (m n)"), crawm[:, 0:256])
                nc.vector.tensor_copy(csmask[:].rearrange("p m n -> p (m n)"), crawm[:, 256:768])
            norm_rstd_dve(dve, 2, CO, c_prepare)

            def c_out(u, j):
                dve.wait_ge(S("c_mhi"), u * 2 + (j + 1))
                r = slice(64 * j, 64 * j + 64)
                nc.vector.tensor_tensor(tile_at(mlo, u, r), as3(bank[CO][0:64, :], u), tile_at(mhi, u, r),
                                        ALU.subtract).then_inc(S("c_mlo"), 1)

            def c_dve(u, nxt):
                if u is not None:
                    for b in range(3):
                        c_chain_dve(dve, u, 0, b)
                    for b in range(2):
                        c_chain_dve(dve, u, 1, b)
                if nxt is not None:
                    c_y_dve(dve, nxt, "q")
                if u is not None:
                    c_chain_dve(dve, u, 1, 2)
                if nxt is not None:
                    c_slot_dve(dve, nxt, "q")
                if u is not None:
                    for b in range(3):
                        c_w_dve(dve, u, 0, b)
                    c_v_dve(dve, u)
                if nxt is not None:
                    c_y_dve(dve, nxt, "k")
                    c_slot_dve(dve, nxt, "k")
                if u is not None:
                    for b in range(3):
                        c_w_dve(dve, u, 1, b)
                    c_out(u, 0)
                if nxt is not None:
                    c_y_dve(dve, nxt, "v")
                if u is not None:
                    c_out(u, 1)

            c_dve(None, 0)
            with dve.Fori(0, C_PAIRS - 1) as i:
                c_dve(i, i + 1)
            c_dve(C_PAIRS - 1, None)
            out_dve(dve, G_OUT1, 1, 3)
            ffn_dve(dve, 1, 3, None)

        @block.tensor
        def _(pe):
            project(pe, 0, 0, bank[2][:], h_hi, h_lo, need_h(pe, 0))
            pe.wait_ge(S("mat_in"), 16)
            pe.wait_ge(S("lam_prod"), 2)
            nc.tensor.matmul(bank[5][:, 0:2], M["ones"], tiny[:, 100:102], start=True, stop=True).then_inc(S("lam_sum"), 1)
            norm_pe(pe, 0, MMB)
            project(pe, 1, 1, bank[3][:], h_hi, h_lo)
            rs_spread_pe(pe, RS_NORM[0], 1, MMB)
            project(pe, 2, 2, bank[0][:], h_hi, h_lo)
            pe.wait_ge(S("l_sq"), 2)
            rs_sum_pe(RS_QL, [(sqb, P), (tb, P)], M["ones"][:, 0:1], 1, MMB)
            project(pe, 3, 0, bank[1][:], h_hi, h_lo)
            rs_spread_pe(pe, RS_QL, 1, MMB)
            pe.wait_ge(S("lam_exp"), 1)
            pe.wait_ge(S("l_sq"), 3)
            rs_sum_pe(RS_KVL, [(sqb, P)], M["ones"][:, 0:1], 1, 5)

            a_proj_pe(pe, 0, "q")
            rs_spread_pe(pe, RS_KVL, 1, 6)
            qk_sum_pe(pe, "r", "q", 0, RS_ROPE, B_QK, "blk_b", 2, OB)
            a_proj_pe(pe, 0, "k")
            rs_spread_pe(pe, RS_ROPE, 2, MMB)
            qk_sum_pe(pe, "a", "q", 0, rs_a(0, "q"), P, "blk64", 2, OB)
            qk_rot_pe(pe, "r", "q", 0, B_QK, "rot_b")
            a_proj_pe(pe, 0, "v")
            rs_spread_pe(pe, rs_a(0, "q"), 2, QMB)
            qk_sum_pe(pe, "a", "k", 0, rs_a(0, "k"), P, "blk64", 2, KSB)
            pe.wait_ge(*at_head("r", "qs", 1))
            qk_rot_pe(pe, "a", "q", 0, P, "rot_a")
            rs_spread_pe(pe, rs_a(0, "k"), 2, KMB, 1)
            pe.wait_ge(*at_head("a", "qs", 1))
            qk_rot_pe(pe, "a", "k", 0, P, "rot_a")
            vtrans_pe(pe, "a", 0)

            def a_pe(u, nxt):
                scores_pe(pe, "a", u, 0)
                scores_pe(pe, "a", u, 1)
                a_proj_pe(pe, nxt, "q")
                scores_pe(pe, "a", u, 2)
                scores_pe(pe, "a", u, 3)
                qk_sum_pe(pe, "a", "q", nxt, rs_a(nxt, "q"), P, "blk64", 2, OB)
                a_proj_pe(pe, nxt, "k")
                rs_spread_pe(pe, rs_a(nxt, "q"), 2, MMB)
                ptrans_pe(pe, "a", u, 0)
                qk_sum_pe(pe, "a", "k", nxt, rs_a(nxt, "k"), P, "blk64", 2, KSB)
                ptrans_pe(pe, "a", u, 1)
                qk_rot_pe(pe, "a", "q", nxt, P, "rot_a")
                a_proj_pe(pe, nxt, "v")
                rs_spread_pe(pe, rs_a(nxt, "k"), 2, KMB, 1)
                values_pe(pe, "a", u, 0)
                ptrans_pe(pe, "a", u, 2)
                pe.wait_ge(*at_head("a", "qs", nxt + 1))
                qk_rot_pe(pe, "a", "k", nxt, P, "rot_a")
                values_pe(pe, "a", u, 1)
                ptrans_pe(pe, "a", u, 3)
                values_pe(pe, "a", u, 2)
                values_pe(pe, "a", u, 3)
                vtrans_pe(pe, "a", nxt)
                a_osum_pe(pe, u)
                pe.wait_ge(*at_head("a", "ks", nxt + 1))
                rs_spread_pe(pe, rs_a(u, "out"), 1, MMB)

            with pe.Fori(0, A_HEADS - 1) as i:
                a_pe(i, i + 1)

            u = A_HEADS - 1
            scores_pe(pe, "a", u, 0)
            scores_pe(pe, "a", u, 1)
            pe.wait_ge(*at_head("a", "vy", A_HEADS))
            b_proj_pe(pe, 0, 0)
            b_proj_kv_pe(pe, 0)
            scores_pe(pe, "a", u, 2)
            scores_pe(pe, "a", u, 3)
            pe.wait_ge(*at_head("a", "on", A_HEADS - 1))
            b_sums_pe(pe, 0)
            b_proj_pe(pe, 1, 1)
            b_proj_kv_pe(pe, 1)
            ptrans_pe(pe, "a", u, 0)
            rs_spread_pe(pe, rs_b(0), 2, MMB, step=3)
            b_spread_k_pe(pe, 0)
            ptrans_pe(pe, "a", u, 1)
            values_pe(pe, "a", u, 0)
            qk_rot_pe(pe, "b", "q", 0, B_QK, "rot_b")
            ptrans_pe(pe, "a", u, 2)
            values_pe(pe, "a", u, 1)
            ptrans_pe(pe, "a", u, 3)
            values_pe(pe, "a", u, 2)
            values_pe(pe, "a", u, 3)
            vtrans_pe(pe, "b", 0)
            a_osum_pe(pe, u)
            pe.wait_ge(*at_head("b", "qs", 1))
            rs_spread_pe(pe, rs_a(u, "out"), 1, MMB)
            pe.wait_ge(S("kr_lo"), 1)
            pe.wait_ge(*at_head("a", "on", A_HEADS))

            def b_pe(u, n, s):
                if n:
                    pe.wait_ge(*at_head("b", "qs", u + 1))
                    b_sums_pe(pe, u + 1)
                for b in range(NB):
                    scores_pe(pe, "b", u, b)
                if n:
                    rs_spread_pe(pe, rs_b(u + 1), 2, MMB, step=3)
                    pe.wait_ge(*at_head("b", "e", u * NB + 2))
                    b_spread_k_pe(pe, u + 1)
                else:
                    out_early_pe(pe, G_OUT0, 0, 0)
                if n:
                    vtrans_pe(pe, "b", u + 1, VTB)
                ptrans_pe(pe, "b", u, 0)
                ptrans_pe(pe, "b", u, 1)
                ptrans_pe(pe, "b", u, 2)
                values_pe(pe, "b", u, 0, s)
                if n:
                    qk_rot_pe(pe, "b", "q", u + 1, B_QK, "rot_b")
                values_pe(pe, "b", u, 1, s)
                ptrans_pe(pe, "b", u, 3)
                if n == 0:
                    out_early_pe(pe, G_OUT0, 0, 1)
                if n > 1:
                    b_proj_pe(pe, u + 2, s)
                    b_proj_kv_pe(pe, s)
                values_pe(pe, "b", u, 2, s)
                values_pe(pe, "b", u, 3, s)

            with pe.Fori(0, B_LOOP) as i:
                for s in range(2):
                    b_pe(i * 2 + s, 2, s)
            for u in range(2 * B_LOOP, B_HEADS):
                b_pe(u, min(2, B_HEADS - 1 - u), u % 2)
            out_pe(pe, G_OUT0, 0, at_head("b", "mlo", B_HEADS))
            ffn_pe(pe, 0, 1)

            def c_pe(u, nxt):
                if u is not None:
                    c_scores_pe(pe, u, 0)
                    c_scores_pe(pe, u, 1)
                if u is None:
                    pe.wait_ge(*at_net(0, "x", KT + 7))
                if nxt is not None:
                    c_proj_pe(pe, nxt, "q", need_h(pe, 2) if u is None else None)
                if u is not None:
                    if nxt is None:
                        pe.wait_ge(S("c_vy"), C_PAIRS)
                        pe.wait_ge(S("c_mlo"), C_HEADS - 2)
                        out_early_pe(pe, G_OUT1, 1, 0)
                    c_tail_pe(pe, u, 0)
                    c_vt_pe(pe, u)
                else:
                    norm_pe(pe, 2, CO)
                if nxt is not None:
                    c_proj_pe(pe, nxt, "k")
                if u is None:
                    rs_spread_pe(pe, RS_NORM[2], 1, CO)
                if u is not None:
                    c_tail_pe(pe, u, 1)
                    c_values_pe(pe, u, 0)
                    if nxt is None:
                        out_early_pe(pe, G_OUT1, 1, 1)
                if nxt is not None:
                    c_proj_pe(pe, nxt, "v")
                if u is not None:
                    c_values_pe(pe, u, 1)

            c_pe(None, 0)
            pe.wait_ge(S("c_vy"), 1)
            with pe.Fori(0, C_PAIRS - 1) as i:
                c_pe(i, i + 1)
            c_pe(C_PAIRS - 1, None)
            out_pe(pe, G_OUT1, 1, (S("c_mlo"), C_HEADS))
            ffn_pe(pe, 1, 3)


def constants():
    f = np.float32
    i = np.arange(P)

    def rot(first, rows, half):
        m = np.zeros((P, P), f)
        for r in range(first, first + rows):
            up = (r - first) % (2 * half) < half
            m[r + half if up else r - half, r] = -1.0 if up else 1.0
        return m
    blk64 = (i[:, None] // 64 == i[None, :] // 64).astype(f)
    blk_b = np.zeros((P, P), f)
    blk_b[:B_NOPE, :B_NOPE] = 1.0 / B_NOPE
    blk_b[B_NOPE:B_QK, B_NOPE:B_QK] = 1.0 / B_ROPE
    mats = np.stack([np.eye(P, dtype=f), rot(0, P, A_DIM // 2), rot(B_NOPE, B_ROPE, B_ROPE // 2), blk64,
                     blk_b, np.ones((P, P), f)], axis=1)
    hidden = np.where(i[:, None] // CHUNK < i[None, :] // CHUNK, f(BIG), f(0))
    masks_a = np.zeros((P, 2, 256), f)
    masks_a[:, 0, :P], masks_a[:, 0, P:], masks_a[:, 1, P:] = hidden, BIG, hidden
    later = np.where(i[None, :] <= i[:, None], f(BIG), f(0))
    masks_c = np.zeros((P, 768), f)
    masks_c[:, 0:P] = -(i[:, None] >= i[None, :]).astype(f)
    masks_c[:, P:2 * P] = -1.0
    masks_c[:, 256:384] = later
    masks_c[:, 512:640] = BIG
    masks_c[:, 640:768] = later

    def table(half, rows):
        freq = np.power(f(THETA), -np.arange(half, dtype=f) / f(half)).astype(f)
        ang = (np.arange(SEQ, dtype=f)[:, None] * freq[None, :]).astype(f)
        r = np.arange(rows) % half
        return np.cos(ang).T[r], np.sin(ang).T[r]
    tabs_a = np.stack(table(A_DIM // 2, P), axis=1).astype(f)
    tabs_b = np.zeros((P, 2, SEQ), f)
    tabs_b[:B_NOPE, 0] = 1.0
    c, s = table(B_ROPE // 2, B_ROPE)
    tabs_b[B_NOPE:B_QK, 0], tabs_b[B_NOPE:B_QK, 1] = c, s
    return mats, masks_a, masks_c, tabs_a, tabs_b


def layout(i):
    f = np.float32
    a = {k: np.asarray(t) for k, t in i.items()}

    def chunks(w, tiles=None):
        k, n = w.shape
        return w.reshape(k // P, P, n // P, P).transpose(2, 1, 0, 3).reshape(n // P, P, k)
    w = a["ab_w_in"][0]
    aq, ak, av = w[:, 0:512], w[:, 512:1024], w[:, 1024:1536]
    kr = np.zeros((D, P), f)
    kr[:, B_NOPE:B_QK] = w[:, 1920:1952]
    rows = [chunks(w[:, 1536:1920]), chunks(kr)]
    rows.append(np.stack([chunks(aq), chunks(ak), chunks(av)], axis=1).reshape(-1, P, W_IN))
    rows.append(chunks(a["ab_w_out"][0]))
    down = []

    def network(l):
        gate, up = chunks(a["ffn_w_gate"][l]), chunks(a["ffn_w_up"][l])
        rows.append(np.stack([gate, up], axis=1).reshape(-1, P, W_IN))
        for s in range(2):
            down.append(chunks(a["ffn_w_down"][l][s * HALF_F * P:(s + 1) * HALF_F * P]))
    network(0)
    c = a["c_w_in"][0]
    rows.append(np.stack([chunks(c[:, t * D:(t + 1) * D]) for t in range(3)], axis=1).reshape(-1, P, W_IN))
    rows.append(chunks(a["c_w_out"][0]))
    network(1)
    w_in, w_down = np.concatenate(rows), np.concatenate(down)

    qb = a["b_w_q_b"][0].reshape(2, P, B_HEADS, B_QK).transpose(2, 1, 0, 3).reshape(B_HEADS, P, 2 * B_QK)
    kvb = a["b_w_kv_b"][0].reshape(P, B_HEADS, P).transpose(1, 0, 2)
    w_b = np.concatenate([qb, kvb], axis=2)

    vecs = np.zeros((P, V_N), f)
    gains = [a["norm_mix"][0], a["norm_ffn"][0], a["norm_mix"][1], a["norm_ffn"][1]]
    vecs[:, V_GAIN:V_GAIN + 4 * KT] = np.stack(gains).reshape(4 * KT, P).T
    vecs[:, V_AQ] = np.concatenate([a["a_q_norm"][0]] * 2)
    vecs[:, V_AK] = np.concatenate([a["a_k_norm"][0]] * 2)
    vecs[:, V_AO] = a["a_out_norm"][0]
    vecs[:, V_BQL:V_BQL + 2] = a["b_q_a_norm"][0].reshape(2, P).T
    vecs[:, V_BKVL] = a["b_kv_a_norm"][0]
    vecs[:B_NOPE, V_BQ], vecs[B_NOPE:B_QK, V_BQ] = a["b_q_nope_norm"][0], a["b_q_rope_norm"][0]
    vecs[:B_NOPE, V_BK] = a["b_k_nope_norm"][0]
    vecs[B_NOPE:B_QK, V_BKR] = a["b_k_rope_norm"][0]
    vecs[:A_DIM, V_LAM:V_LAM + 4] = a["a_lambda"][0].T
    vecs[:, V_EPS] = EPS
    xt = a["x"][0].T.reshape(KT, P, SEQ)
    return dict(xt=xt, w_in=w_in, w_b=w_b, w_down=w_down, vecs=vecs)


def kernel(**inputs):
    import concourse.bacc as bacc
    from concourse.bass_utils import run_bass_kernel_spmd

    arrays = layout(inputs)
    for name, value in zip(("mats", "masks_a", "masks_c", "tabs_a", "tabs_b"), constants()):
        arrays[name] = value
    arrays = {n: np.ascontiguousarray(t) for n, t in arrays.items()}
    nc = bacc.Bacc("TRN2", target_bir_lowering=False, num_devices=1)
    aps = {n: nc.dram_tensor(f"in_{n}", t.shape, mybir.dt.from_np(t.dtype), kind="ExternalInput").ap()
           for n, t in arrays.items()}
    out = nc.dram_tensor("out", (KT, P, SEQ), F32, kind="ExternalOutput").ap()
    trunk(nc, out=out, **aps)
    r = run_bass_kernel_spmd(nc, [{f"in_{n}": t for n, t in arrays.items()}], core_ids=[0])
    return r.results[0]["out"].reshape(D, SEQ).T.reshape(1, SEQ, D)
```

```python
import math

import numpy as np

import concourse.bass as bass
from concourse import mybir

F32 = mybir.dt.float32
F32R = mybir.dt.float32r
ALU = mybir.AluOpType
ACT = mybir.ActivationFunctionType
AX = mybir.AxisListType.X

P = 128
D = 1024
SEQ = 512
KT = D // P
NB = SEQ // P
CHUNK = 64
EPS = 1e-6
THETA = 10000.0
BIG = -1e30

A_HEADS, A_DIM = 4, 64
B_HEADS, B_NOPE, B_ROPE, B_V = 8, 64, 32, 64
B_QK = B_NOPE + B_ROPE
B_QRANK, B_KVRANK = 256, 128
C_HEADS, C_DIM = 16, 64
C_PAIRS = C_HEADS // 2
D_FF = 2816
HALF_F = D_FF // P // 2
LAM0 = 0.8 - 0.6 * math.exp(-0.3 * 0)

WSLOTS = 3
W_IN = KT * P
W_DOWN = HALF_F * P
WB = 2 * B_QK + P
OUT_AHEAD = B_HEADS - 2
W_AHEAD = A_HEADS * P

G_LAT = 0
G_A = G_LAT + 4
G_OUT0 = G_A + 3 * A_HEADS
G_FFN0 = G_OUT0 + KT
FFN_HALF = 2 * HALF_F + KT
G_C = G_FFN0 + 2 * FFN_HALF
G_OUT1 = G_C + 3 * C_PAIRS
G_FFN1 = G_OUT1 + KT
N_CHUNKS = G_FFN1 + 2 * FFN_HALF

SW = [max(256, (b + 1) * P) for b in range(NB)]
TQ = [min(b * P, SEQ - 256) for b in range(NB)]
TW = [SEQ - q for q in TQ]
TO = [sum(TW[:b]) for b in range(NB)]
TWS = sum(TW)

MATS = ["ident", "rot_a", "rot_b", "blk64", "blk_b", "ones"]
V_GAIN = 0
V_AQ, V_AK, V_AO, V_BQL, V_BKVL, V_BQ, V_BK, V_BKR, V_LAM = 32, 33, 34, 35, 37, 38, 39, 40, 41
V_N = 45


def width_of(g):
    if G_OUT0 + 3 <= g < G_OUT0 + OUT_AHEAD:
        return W_IN - W_AHEAD
    for first in (G_FFN0, G_FFN1):
        if first <= g < first + 2 * FFN_HALF and (g - first) % FFN_HALF >= 2 * HALF_F:
            return W_DOWN
    return W_IN


def trunk(nc, xt, w_in, w_b, w_down, mats, masks_a, masks_c, tabs_a, tabs_b, vecs, out):
    cursor = [nc.sbuf_base]

    def place(name, shape, dt, at=None):
        size = 4 * int(np.prod(shape[1:]))
        off = cursor[0] if at is None else at
        off = (off + 31) // 32 * 32
        t = nc.alloc_sbuf_tensor_at(name, list(shape), dt, offset=off)
        if at is None:
            cursor[0] = off + size
        return t, off + size

    def pair(name, shape, at=None):
        a, end = place(name + "_hi", shape, F32R, at)
        b, end = place(name + "_lo", shape, F32R, None if at is None else end)
        return (a, b), end

    x, _ = place("x", [P, KT, SEQ], F32)
    wraw, _ = place("wraw", [P, WSLOTS, W_DOWN], F32)
    (whi, wlo), _ = pair("w", [P, WSLOTS, W_DOWN])
    mat, _ = place("mat", [P, len(MATS), P], F32)
    ident_r, _ = place("ident_r", [P, P], F32R)
    cmask, _ = place("cmask", [P, 2, 256], F32R)
    vec, _ = place("vec", [P, V_N], F32)
    tiny, _ = place("tiny", [P, 112], F32)
    rstd, _ = place("rstd", [P, SEQ], F32)
    h0 = cursor[0]
    (hhi, hlo), _ = pair("h", [P, KT, SEQ])
    phase0 = cursor[0]

    (mhi, mlo), _ = pair("mixed", [P, KT, SEQ])
    (qlhi, qllo), _ = pair("ql", [P, 2, SEQ])
    (kvhi, kvlo), _ = pair("kvl", [P, SEQ])
    tabb, _ = place("tabb", [P, 2, SEQ], F32)
    (qhi, qlo), _ = pair("q", [P, 2, SEQ])
    (khi, klo), _ = pair("k", [P, SEQ])
    (vhi, vlo), _ = pair("v", [P, NB, P])
    e1, _ = place("e1", [P, 2, SEQ], F32)
    pn0 = cursor[0]
    pn, _ = place("pn", [P, NB, SEQ], F32)
    (pthi, ptlo), _ = pair("pt", [P, TWS])
    yq, _ = place("yq", [P, SEQ], F32)
    yk, _ = place("yk", [P, SEQ], F32)
    yv, _ = place("yv", [P, SEQ], F32)
    on, _ = place("on", [P, SEQ], F32)
    sqb, _ = place("sqb", [P, SEQ], F32)
    tb, _ = place("tb", [P, SEQ], F32)
    assert cursor[0] <= nc.sbuf_usable_end, cursor[0]
    taba, end = place("taba", [P, 2, SEQ], F32, at=phase0 + 4 * 4 * SEQ)
    rope_keep, end = place("rope_keep", [P, SEQ], F32, at=end)
    assert end <= phase0 + 4 * KT * SEQ
    bwraw, end = place("bwraw", [P, 2, WB + W_AHEAD], F32, at=h0)
    (bwhi, bwlo), end = pair("bw", [P, 2, WB + W_AHEAD], at=end)
    assert end <= phase0
    rawm, _ = place("rawm", [P, 2, 256], F32, at=pn0 + 12 * SEQ)
    sqn, end = place("sqn", [P, 2, SEQ], F32, at=pn0)
    ssum, _ = place("ssum", [P, SEQ], F32, at=end)

    (fhi, flo), end = pair("f", [P, HALF_F, SEQ], at=phase0)
    fy, end = place("fy", [P, SEQ], F32, at=end)
    fs, end = place("fs", [P, SEQ], F32, at=end)
    fu, end = place("fu", [P, SEQ], F32, at=end)
    fa, end = place("fa", [P, SEQ], F32, at=end)
    assert end <= pn0, (end, pn0)

    c0 = phase0 + 2 * 4 * KT * SEQ
    (cqhi, cqlo), end = pair("cq", [P, 2, SEQ], at=c0)
    ck, end = place("ck", [P, 2, SEQ], F32R, at=end)
    cv, end = place("cv", [P, NB, 2, P], F32R, at=end)
    cyq, end = place("cyq", [P, SEQ], F32, at=end)
    cyk, end = place("cyk", [P, SEQ], F32, at=end)
    cyv, end = place("cyv", [P, SEQ], F32, at=end)
    cmats, end = place("cmats", [P, 2, P], F32R, at=end)
    csmask, end = place("csmask", [P, 2, 256], F32R, at=end)
    (cz0, cz0lo), end = pair("cs0", [P, TWS], at=end)
    (cz1, cz1lo), end = pair("cs1", [P, TWS], at=end)
    cshi, cslo = (cz0, cz1), (cz0lo, cz1lo)
    ca0, end = place("ca0", [P, TWS], F32, at=end)
    ca1, end = place("ca1", [P, TWS], F32, at=end)
    ca = (ca0, ca1)
    cs, end = place("cs", [P, TWS], F32, at=end)
    co, _ = place("co", [P, SEQ], F32, at=end)
    assert end + 4 * SEQ <= nc.sbuf_usable_end, end
    crawm, end = place("crawm", [P, 768], F32, at=end - 4 * TWS)

    bank = [nc.alloc_psum_tensor(f"bank{i}", [P, SEQ], F32) for i in range(8)]

    sems = {}

    def S(name):
        if name not in sems:
            sems[name] = nc.alloc_semaphore(name)
        return sems[name]

    def wait(eng, name, value):
        if not isinstance(value, int) or value > 0:
            eng.wait_ge(S(name), value)

    M = {n: mat[:, i, :] for i, n in enumerate(MATS)}

    def v(col, n=1, rows=P):
        return vec[0:rows, col:col + n]

    def tile_at(t, k, rows=slice(0, P)):
        return t[rows, k, :] if isinstance(k, int) else t[rows, bass.ds(k, 1), :]

    def is_first(u):
        return isinstance(u, int) and u == 0

    def as3(ap, k):
        return ap if isinstance(k, int) else ap.rearrange("p (o n) -> p o n", o=1)

    def at_norm(n, what, value):
        return S("norm_" + what), value + n * {"sq": KT, "hi": KT, "lo": KT, "sum": KT - 1}.get(what, 1)

    def at_net(L, what, value):
        return S("net_" + what), value + L * 2 * (KT if what == "x" else HALF_F)

    def at_head(ph, what, value):
        a_only = {"e": 2 * NB, "mx": 2 * NB, "qlo": 2, "qhi": 2, "whi": 0, "wlo": 0, "q": 0, "kv": 0}
        of_a = A_HEADS * (NB if what in ("s", "nm", "r", "p", "tr", "phi", "plo") else a_only.get(what, 1))
        of_r = 1 if what in ("qsq", "qt", "qrot", "qc", "qs", "qy2") else 0
        return S("head_" + what), value + (0 if ph == "r" else of_r) + (of_a if ph == "b" else 0)

    def slot(g_static):
        return g_static % WSLOTS

    def load_chunk(sp, g, s, src, width):
        wait(sp, "w_lo", g - (WSLOTS - 1))
        sp.dma_start(wraw[:, s, 0:width], src).then_inc(S(f"w_in{s}"), 16)

    def split_hi(act, g, s, use, width=W_IN):
        act.wait_ge(S(f"w_in{s}"), 16 * use)
        wait(act, "chunk_done", g - (WSLOTS - 1))
        nc.scalar.activation(whi[:, s, 0:width], wraw[:, s, 0:width], ACT.Copy).then_inc(S("w_hi"), 1)

    def hi_static(act, g):
        if g < N_CHUNKS:
            split_hi(act, g, slot(g), g // WSLOTS + 1, width_of(g))

    def hi_at(act, g0, i, step):
        split_hi(act, g0 + i * step, slot(g0), g0 // WSLOTS + 1 + i * (step // WSLOTS))

    def split_lo(pool, g, s, width):
        pool.wait_ge(S("w_hi"), g + 1)
        nc.gpsimd.tensor_tensor(wlo[:, s, 0:width], wraw[:, s, 0:width], whi[:, s, 0:width],
                                ALU.subtract).then_inc(S("w_lo"), 1)

    def project(pe, g, s, out_bank, src_hi, src_lo, first=None):
        n = len(src_hi)
        pe.wait_ge(S("w_hi"), g + 1)
        for kt in range(n):
            if first is not None:
                first(kt)
            w = whi[:, s, kt * P:(kt + 1) * P]
            nc.tensor.matmul(out_bank, w, src_hi[kt], start=(kt == 0), stop=False)
            nc.tensor.matmul(out_bank, w, src_lo[kt], start=False, stop=False)
        pe.wait_ge(S("w_lo"), g + 1)
        for kt in range(n):
            last = nc.tensor.matmul(out_bank, wlo[:, s, kt * P:(kt + 1) * P], src_hi[kt],
                                    start=False, stop=(kt == n - 1))
        last.then_inc(S("chunk_done"), 1)

    def project_tiles(pe, g, out_bank, src_hi, src_lo, tiles):
        pe.wait_ge(S("w_lo"), g + 1)
        for kt in tiles:
            w = slice(kt * P, (kt + 1) * P)
            for n, (a, o) in enumerate(((whi, src_hi), (whi, src_lo), (wlo, src_hi))):
                last = nc.tensor.matmul(out_bank, a[:, slot(g), w], o[kt], start=(kt == 0 and n == 0),
                                        stop=(kt == len(src_hi) - 1 and n == 2))
        if kt == len(src_hi) - 1:
            last.then_inc(S("chunk_done"), 1)

    h_hi = [hhi[:, k, :] for k in range(KT)]
    h_lo = [hlo[:, k, :] for k in range(KT)]
    m_hi = [mhi[:, k, :] for k in range(KT)]
    m_lo = [mlo[:, k, :] for k in range(KT)]

    RS_NORM = (0, 24, 25, 26)
    RS_QL, RS_KVL, RS_ROPE = 1, 2, 3
    T_M, T_Y, T_A, T_Z = 44, 56, 68, (80, 92)

    def rs_a(u, what):
        if what == "out":
            return 16 if isinstance(u, int) and u == A_HEADS - 1 else u * 3 + 8
        first = RS_ROPE + 1 if is_first(u) else u * 3 + 3
        return first + (1 if what == "k" else 0)

    def rs_b(u):
        return 15 if is_first(u) else u + 16

    def rs_sum_pe(r, sources, cols, nh, b):
        for i in range(NB):
            for n, (src, rows) in enumerate(sources):
                last = nc.tensor.matmul(bank[b][:, i * nh:(i + 1) * nh], src[0:rows, i * P:(i + 1) * P],
                                        cols[0:rows, :], start=(n == 0), stop=(n == len(sources) - 1))
        last.then_inc(S("rs_sum"), 1)

    def rs_mean_dve(dve, r, scale, nh, b):
        dve.wait_ge(S("rs_sum"), r + 1)
        nc.vector.tensor_scalar(tiny[:, T_M:T_M + NB * nh], bank[b][:, 0:NB * nh], scale, EPS, ALU.mult,
                                ALU.add).then_inc(S("rs_mean"), 1)

    def rs_act(act, r, nh):
        m, y = tiny[:, T_M:T_M + NB * nh], tiny[:, T_Y:T_Y + NB * nh]
        act.wait_ge(S("rs_mean"), r + 1)
        nc.scalar.activation(y, m, ACT.Ln).then_inc(S("rs_ln"), 1)
        act.wait_ge(S("rs_ln"), r + 1)
        nc.scalar.activation(y, y, ACT.Exp, scale=-0.5).then_inc(S("rs_exp"), 1)

    def rs_newton_dve(dve, r, nh, slot=0):
        m, y, a, z = (tiny[:, t:t + NB * nh] for t in (T_M, T_Y, T_A, T_Z[slot]))
        dve.wait_ge(S("rs_exp"), r + 1)
        nc.vector.tensor_tensor(a, m, y, ALU.mult).then_inc(S("rs_my"), 1)
        dve.wait_ge(S("rs_my"), r + 1)
        nc.vector.tensor_tensor(a, a, y, ALU.mult).then_inc(S("rs_myy"), 1)
        dve.wait_ge(S("rs_myy"), r + 1)
        nc.vector.tensor_scalar(a, a, -0.5, 1.5, ALU.mult, ALU.add).then_inc(S("rs_step"), 1)
        dve.wait_ge(S("rs_step"), r + 1)
        nc.vector.tensor_tensor(z, a, y, ALU.mult).then_inc(S("rs_root"), 1)

    def rs_spread_pe(pe, r, nh, b, slot=0, step=None):
        pe.wait_ge(S("rs_root"), r + 1)
        for i in range(NB):
            for j in range(nh):
                col = T_Z[slot] + i * (step or nh) + j
                z = tiny[:, col:col + 1]
                rows = slice(j * P // nh, (j + 1) * P // nh)
                last = nc.tensor.matmul(bank[b][rows, i * P:(i + 1) * P], z.broadcast_to([P, P // nh]),
                                        M["ident"], start=True, stop=True)
        last.then_inc(S("rs_spread"), 1)

    def norm_act(act, n, d):
        if d >= 2:
            act.wait_ge(*at_norm(n, "sum", max(1, d - 2)))
        nc.scalar.activation(sqn[:, d % 2, :], x[:, d, :], ACT.Square).then_inc(S("norm_sq"), 1)
        nc.scalar.activation(hhi[:, d, :], x[:, d, :], ACT.Copy,
                             scale=v(V_GAIN + KT * n + d)).then_inc(S("norm_hi"), 1)

    def norm_dve(dve, n, d):
        dve.wait_ge(*at_norm(n, "hi", d + 1))
        nc.vector.scalar_tensor_tensor(hlo[:, d, :], x[:, d, :], v(V_GAIN + KT * n + d), hhi[:, d, :],
                                       ALU.mult, ALU.subtract).then_inc(S("norm_lo"), 1)

    def norm_pool(pool, n, d):
        if d == 0:
            return
        pool.wait_ge(*at_norm(n, "sq", d + 1))
        if d > 1:
            pool.wait_ge(*at_norm(n, "sum", d - 1))
        nc.gpsimd.tensor_tensor(ssum[:], sqn[:, 0, :] if d == 1 else ssum[:], sqn[:, d % 2, :],
                                ALU.add).then_inc(S("norm_sum"), 1)

    def norm_pe(pe, n, b):
        pe.wait_ge(*at_norm(n, "sum", KT - 1))
        rs_sum_pe(RS_NORM[n], [(ssum, P)], M["ones"][:, 0:1], 1, b)

    def norm_rstd_dve(dve, n, b, meanwhile=None):
        r = RS_NORM[n]
        rs_mean_dve(dve, r, 1.0 / D, 1, b)
        rs_newton_dve(dve, r, 1)
        if meanwhile is not None:
            meanwhile()
        dve.wait_ge(S("rs_spread"), r + 1)
        nc.vector.tensor_copy(rstd[:], bank[b][:]).then_inc(S("norm_rstd"), 1)
        dve.wait_ge(*at_norm(n, "rstd", 1))

    def need_h(pe, n):
        def first(kt):
            pe.wait_ge(*at_norm(n, "lo", kt + 1))
        return first

    OUT_BANKS = ((2, 3), (6, 2))
    OUT_EARLY = 2

    def out_sources(L, d):
        first = A_HEADS if L == 0 and d < OUT_AHEAD else 0
        return m_hi[first:], m_lo[first:]

    def out_ahead_pe(pe, u, s, tiles):
        pe.wait_ge(*at_head("b", "wlo", u + 3))
        for kt in tiles:
            w = slice(WB + kt * P, WB + (kt + 1) * P)
            for n, (a, o) in enumerate(((bwhi, m_hi), (bwhi, m_lo), (bwlo, m_hi))):
                last = nc.tensor.matmul(bank[AHB][:], a[:, s, w], o[kt], start=(kt == 0 and n == 0),
                                        stop=(kt == A_HEADS - 1 and n == 2))
        if kt == A_HEADS - 1:
            last.then_inc(S("out_ahead"), 1)

    AHEAD_FIRST = 2

    def out_ahead_dve(dve, u):
        dve.wait_ge(S("out_ahead"), u + 1)
        nc.vector.tensor_tensor(tile_at(x, u), as3(bank[AHB][:], u), tile_at(x, u), ALU.add).then_inc(S("ahead_x"), 1)

    def out_early_pe(pe, g0, L, d, tiles):
        project_tiles(pe, g0 + d, bank[OUT_BANKS[L][d % 2]][:], *out_sources(L, d), tiles)

    def out_pe(pe, g0, L, heads_done):
        pe.wait_ge(*heads_done)
        for d in range(KT):
            b = bank[OUT_BANKS[L][d % 2]][:]
            hi, lo = out_sources(L, d)
            if d < OUT_EARLY:
                project_tiles(pe, g0 + d, b, hi, lo, (len(hi) - 1,))
                continue
            if d >= 2:
                pe.wait_ge(S("out_x"), L * KT + d - 1)
            project(pe, g0 + d, slot(g0 + d), b, hi, lo)

    def out_act(act, g0, L, n):
        for d in range(KT):
            act.wait_ge(S("out_x"), L * KT + d + 1)
            hi_static(act, g0 + d + 3)
            norm_act(act, n, d)

    def out_dve(dve, g0, L, n):
        if L == 0:
            dve.wait_ge(S("ahead_x"), OUT_AHEAD)
        for d in range(KT):
            dve.wait_ge(S("chunk_done"), g0 + d + 1)
            nc.vector.tensor_tensor(x[:, d, :], bank[OUT_BANKS[L][d % 2]][:], x[:, d, :],
                                    ALU.add).then_inc(S("out_x"), 1)
            if d:
                norm_dve(dve, n, d - 1)
        norm_dve(dve, n, KT - 1)

    GU_LOOP = HALF_F // 3 * 3

    def ffn_each(eng, body):
        with eng.Fori(0, GU_LOOP // 3) as i:
            for j in range(3):
                body(i * 3 + j, j)
        for f in range(GU_LOOP, HALF_F):
            body(f, f % 3)

    def ffn_pe(pe, L, n):
        g_first = (G_FFN0, G_FFN1)[L]
        for s in range(2):
            g0 = g_first + s * FFN_HALF

            def gate_up(f, j):
                for c in range(2):
                    g = f * 2 + (g0 + c)
                    sl = slot(g0 + 2 * j + c)
                    if isinstance(f, int):
                        if s or f >= 3:
                            pe.wait_ge(*at_net(L, "yu"[c], s * HALF_F + f - 2 if f >= 3 else HALF_F))
                    elif s:
                        pe.wait_ge(*at_net(L, "yu"[c], f + (HALF_F - 2)))
                    project(pe, g, sl, bank[2 * j + c][:], h_hi, h_lo)
            if s == 0:
                for f in range(3):
                    for c in range(2):
                        g = g0 + 2 * f + c
                        project(pe, g, slot(g), bank[2 * f + c][:], h_hi, h_lo,
                                need_h(pe, n) if f == 0 and c == 0 else None)
                        if f == 0:
                            if c == 0:
                                norm_pe(pe, n, 7)
                            else:
                                rs_spread_pe(pe, RS_NORM[n], 1, 7)
                with pe.Fori(1, GU_LOOP // 3) as i:
                    for j in range(3):
                        for c in range(2):
                            pe.wait_ge(*at_net(L, "yu"[c], i * 3 + (j - 2)))
                            project(pe, i * 6 + (g0 + 2 * j + c), slot(g0 + 2 * j + c),
                                    bank[2 * j + c][:], h_hi, h_lo)
                for f in range(GU_LOOP, HALF_F):
                    gate_up(f, f % 3)
            else:
                pe.wait_ge(*at_net(L, "x", 6))
                with pe.Fori(0, GU_LOOP // 3) as i:
                    for j in range(3):
                        for c in range(2):
                            pe.wait_ge(*at_net(L, "yu"[c], i * 3 + (j - 2 + HALF_F)))
                            project(pe, i * 6 + (g0 + 2 * j + c), slot(g0 + 2 * j + c),
                                    bank[2 * j + c][:], h_hi, h_lo)
                for f in range(GU_LOOP, HALF_F):
                    gate_up(f, f % 3)
            gd = g0 + 2 * HALF_F
            f_hi = [fhi[:, k, :] for k in range(HALF_F)]
            f_lo = [flo[:, k, :] for k in range(HALF_F)]

            def need_f(kt):
                pe.wait_ge(*at_net(L, "lo", s * HALF_F + kt + 1))
            down_banks = (6, 7, 0)
            for d in range(3):
                if s:
                    pe.wait_ge(*at_net(L, "x", KT))
                project(pe, gd + d, slot(gd + d), bank[down_banks[d]][:], f_hi, f_lo,
                        need_f if d == 0 else None)
            for d in range(3, KT):
                pe.wait_ge(*at_net(L, "x", s * KT + d - 2))
                project(pe, gd + d, slot(gd + d), bank[down_banks[d % 3]][:], f_hi, f_lo)

    def ffn_act(act, L, n_next):
        g_first = (G_FFN0, G_FFN1)[L]
        for s in range(2):
            g0 = g_first + s * FFN_HALF

            def tile(i, j):
                f = i * 3 + j

                def split_ahead(c):
                    g = g0 + 2 * j + c
                    split_hi(act, i * 6 + g, slot(g), i * 2 + (g // WSLOTS + 1),
                             width_of(i * 6 + g) if isinstance(i, int) else W_IN)
                act.wait_ge(*at_net(L, "y", f + (s * HALF_F + 1)))
                nc.scalar.activation(fs[:], fy[:], ACT.Silu).then_inc(S("net_s"), 1)
                split_ahead(3)
                act.wait_ge(*at_net(L, "a", f + (s * HALF_F + 1)))
                nc.scalar.activation(tile_at(fhi, f), as3(fa[:], f), ACT.Copy).then_inc(S("net_hi"), 1)
                split_ahead(4)
            with act.Fori(0, GU_LOOP // 3) as i:
                for j in range(3):
                    tile(i, j)
            for f in range(GU_LOOP, HALF_F):
                tile(GU_LOOP // 3, f - GU_LOOP)
            for d in range(KT):
                act.wait_ge(*at_net(L, "x", s * KT + d + 1))
                hi_static(act, g0 + 2 * HALF_F + d + 3)
                if s and n_next is not None:
                    norm_act(act, n_next, d)

    def ffn_dve(dve, L, n, n_next):
        g_first = (G_FFN0, G_FFN1)[L]
        norm_rstd_dve(dve, n, 7)
        for s in range(2):
            g0 = g_first + s * FFN_HALF

            def tile(f, j):
                dve.wait_ge(S("chunk_done"), f * 2 + (g0 + 1))
                nc.vector.tensor_tensor(fy[:], bank[2 * j][:], rstd[:], ALU.mult).then_inc(S("net_y"), 1)
                dve.wait_ge(S("chunk_done"), f * 2 + (g0 + 2))
                nc.vector.tensor_tensor(fu[:], bank[2 * j + 1][:], rstd[:], ALU.mult).then_inc(S("net_u"), 1)
                dve.wait_ge(*at_net(L, "u", f + (s * HALF_F + 1)))
                dve.wait_ge(*at_net(L, "s", f + (s * HALF_F + 1)))
                nc.vector.tensor_tensor(fa[:], fu[:], fs[:], ALU.mult).then_inc(S("net_a"), 1)
                dve.wait_ge(*at_net(L, "hi", f + (s * HALF_F + 1)))
                nc.vector.tensor_tensor(tile_at(flo, f), as3(fa[:], f), tile_at(fhi, f),
                                        ALU.subtract).then_inc(S("net_lo"), 1)
            ffn_each(dve, tile)
            gd = g0 + 2 * HALF_F
            for d in range(KT):
                dve.wait_ge(S("chunk_done"), gd + d + 1)
                if s:
                    dve.wait_ge(*at_net(L, "x", KT))
                b = bank[(6, 7, 0)[d % 3]]
                nc.vector.tensor_tensor(x[:, d, :], b[:], x[:, d, :], ALU.add).then_inc(S("net_x"), 1)
                if s and n_next is not None:
                    norm_dve(dve, n_next, d)

    PJ = (2, 3)
    MMB = 4
    TRB = (5, 6)
    OB = 7
    QMB = 5
    VTA = 3
    VTB = AHB = 0
    KSB, KMB = 0, 1
    def score_bank(sub, b, j):
        return bank[((0, 1), TRB)[b % 2][j] if sub == 2 else (0, 1, *TRB)[b]]

    def scores_pe(pe, ph, u, b):
        sub = 2 if ph == "a" else 1
        if b == 0:
            pe.wait_ge(*at_head(ph, "qlo", u * sub + sub))
            pe.wait_ge(*at_head(ph, "klo", u + 1))
        if b == 0 and ph == "b":
            pe.wait_ge(*at_head(ph, "vlo", u + 1))
        if sub == 2 and b >= 2:
            pe.wait_ge(*at_head(ph, "e", u * (NB * sub) + sub * (b - 1)))
        w = SW[b]
        rows = P if ph == "a" else B_QK
        for j in range(sub):
            o = score_bank(sub, b, j)
            for n, (a, c) in enumerate(((qhi, khi), (qhi, klo), (qlo, khi))):
                nc.tensor.matmul(o[:, 0:w], a[0:rows, j, b * P:(b + 1) * P], c[0:rows, 0:w],
                                 start=(n == 0), stop=False)
            last = nc.tensor.matmul(o[:, w - 256:w], ident_r[:], cmask[:, 0 if b == 0 else 1, :],
                                    start=False, stop=True)
        last.then_inc(S("head_s"), 1)

    T_MX, T_NM, T_L, T_R, T_RL = 0, 8, 16, 24, 32
    T_LAM, T_OG = 42, 43
    T_LP, T_LE, T_LD = 100, 102, 104

    def tc(t, b, j, n=1):
        return tiny[:, t + 2 * b + j:t + 2 * b + j + n]

    def softmax_dve(dve, ph, u, b, scale):
        sub = 2 if ph == "a" else 1
        w = SW[b]
        n = u * NB + (b + 1)
        dve.wait_ge(*at_head(ph, "s", n))
        for j in range(sub):
            o = score_bank(sub, b, j)
            nc.vector.reduce_max(tc(T_MX, b, j), o[:, 0:w], AX).then_inc(S("head_mx"), 1)
        dve.wait_ge(*at_head(ph, "mx", n * sub))
        nc.vector.tensor_scalar(tc(T_NM, b, 0, sub), tc(T_MX, b, 0, sub), -scale, None,
                                ALU.mult).then_inc(S("head_nm"), 1)

    def softmax_act(act, ph, u, b, scale):
        sub = 2 if ph == "a" else 1
        w = SW[b]
        act.wait_ge(*at_head(ph, "nm", u * NB + (b + 1)))
        for j in range(sub):
            o = score_bank(sub, b, j)
            dst = pn[:, b, 0:w] if j == 0 else e1[:, b % 2, 0:w]
            nc.scalar.activation(dst, o[:, 0:w], ACT.Exp, bias=tc(T_NM, b, j),
                                 scale=scale, accum_out=tc(T_L, b, j)).then_inc(S("head_e"), 1)

    def probs_dve(dve, ph, u, b):
        sub = 2 if ph == "a" else 1
        w = SW[b]
        n = u * NB + (b + 1)
        dve.wait_ge(*at_head(ph, "e", n * sub))
        nc.vector.reciprocal(tc(T_R, b, 0, sub), tc(T_L, b, 0, sub)).then_inc(S("head_r"), 1)
        dve.wait_ge(*at_head(ph, "r", n))
        if sub == 2:
            nc.vector.tensor_tensor(tc(T_RL, b, 0), tc(T_R, b, 1),
                                    tiny[:, T_LAM:T_LAM + 1], ALU.mult).then_inc(S("head_rl"), 1)
            dve.wait_ge(*at_head(ph, "rl", n))
            nc.vector.tensor_scalar(e1[:, b % 2, 0:w], e1[:, b % 2, 0:w], tc(T_RL, b, 0), None,
                                    ALU.mult).then_inc(S("head_e1"), 1)
            dve.wait_ge(*at_head(ph, "e1", n))
            nc.vector.scalar_tensor_tensor(pn[:, b, 0:w], pn[:, b, 0:w], tc(T_R, b, 0), e1[:, b % 2, 0:w],
                                           ALU.mult, ALU.subtract).then_inc(S("head_p"), 1)
        else:
            nc.vector.tensor_scalar(pn[:, b, 0:w], pn[:, b, 0:w], tc(T_R, b, 0), None,
                                    ALU.mult).then_inc(S("head_p"), 1)

    def ptrans_pe(pe, ph, u, kb):
        if kb == 0:
            pe.wait_ge(*at_head(ph, "p", u * NB + NB))
        if kb >= 2:
            pe.wait_ge(*at_head(ph, "plo", u * NB + (kb - 1)))
        for b in range(kb, NB):
            last = nc.tensor.transpose(bank[TRB[kb % 2]][:, b * P:(b + 1) * P], pn[:, b, kb * P:(kb + 1) * P],
                                       M["ident"])
        last.then_inc(S("head_tr"), 1)

    def pt_slice(t, kb):
        return t[:, TO[kb] + TW[kb] - (SEQ - kb * P):TO[kb] + TW[kb]]

    def ptrans_act(act, ph, u, kb):
        act.wait_ge(*at_head(ph, "tr", u * NB + (kb + 1)))
        nc.scalar.activation(pt_slice(pthi, kb), bank[TRB[kb % 2]][:, kb * P:SEQ], ACT.Copy).then_inc(S("head_phi"), 1)

    def ptrans_dve(dve, ph, u, kb):
        dve.wait_ge(*at_head(ph, "phi", u * NB + (kb + 1)))
        nc.vector.tensor_tensor(pt_slice(ptlo, kb), bank[TRB[kb % 2]][:, kb * P:SEQ], pt_slice(pthi, kb),
                                ALU.subtract).then_inc(S("head_plo"), 1)

    def values_pe(pe, ph, u, kb, s=0):
        pe.wait_ge(*at_head(ph, "plo", u * NB + (kb + 1)))
        if ph == "b" and kb == 0:
            pe.wait_ge(*at_head("b", "mlo", u))
        dv = P if ph == "a" else B_V
        for n, (a, c) in enumerate(((vhi, pthi), (vhi, ptlo), (vlo, pthi))):
            last = nc.tensor.matmul(bank[OB][0:dv, TQ[kb]:SEQ], a[:, kb, s * dv:(s + 1) * dv],
                                    c[:, TO[kb]:TO[kb] + TW[kb]],
                                    start=(kb == 0 and n == 0), stop=(kb == NB - 1 and n == 2))
        if kb == NB - 1:
            last.then_inc(S("head_o"), 1)

    def vtrans_pe(pe, ph, u, vb=TRB[0]):
        pe.wait_ge(*at_head(ph, "vy", u + 1))
        for b in range(NB):
            last = nc.tensor.transpose(bank[vb][:, b * P:(b + 1) * P], yv[:, b * P:(b + 1) * P], M["ident"])
        last.then_inc(S("head_vt"), 1)

    def v_parts(ph, t, s, vb):
        dv, at = (P, 0) if ph == "a" else (B_V, P - B_V)
        src = bank[vb][:].rearrange("p (b n) -> p b n", n=P)[:, :, at:at + dv]
        return t[:, :, s * dv:(s + 1) * dv], src

    def v_act(act, ph, u, s=0, vb=TRB[0]):
        act.wait_ge(*at_head(ph, "vt", u + 1))
        o, i = v_parts(ph, vhi, s, vb)
        nc.scalar.activation(o, i, ACT.Copy).then_inc(S("head_vhi"), 1)

    def v_dve(dve, ph, u, s=0, vb=TRB[0]):
        dve.wait_ge(*at_head(ph, "vhi", u + 1))
        o, i = v_parts(ph, vlo, s, vb)
        nc.vector.tensor_tensor(o, i, v_parts(ph, vhi, s, vb)[0], ALU.subtract).then_inc(S("head_vlo"), 1)

    def a_osum_pe(pe, u):
        last_head = isinstance(u, int) and u == A_HEADS - 1
        pe.wait_ge(*(at_head("b", "qs", 1) if last_head else at_head("a", "ks", u + 2)))
        pe.wait_ge(*at_head("a", "osq", u + 1))
        rs_sum_pe(rs_a(u, "out"), [(sqb, P)], M["ones"][:, 0:1], 1, MMB)

    def a_osq_act(act, u):
        act.wait_ge(*at_head("a", "o", u + 1))
        nc.scalar.activation(sqb[:], bank[OB][:], ACT.Square).then_inc(S("head_osq"), 1)

    def a_mhi_act(act, u):
        act.wait_ge(*at_head("a", "on", u + 1))
        nc.scalar.activation(tile_at(mhi, u), as3(on[:], u), ACT.Copy).then_inc(S("head_mhi"), 1)

    def a_osum_dve(dve, u):
        rs_mean_dve(dve, rs_a(u, "out"), 1.0 / (2 * A_DIM), 1, MMB)
        nc.vector.tensor_scalar(on[:], bank[OB][:], tiny[:, T_OG:T_OG + 1], None, ALU.mult).then_inc(S("head_og2"), 1)
        rs_newton_dve(dve, rs_a(u, "out"), 1)

    def a_on_dve(dve, u):
        dve.wait_ge(*at_head("a", "og2", u + 1))
        dve.wait_ge(S("rs_spread"), rs_a(u, "out") + 1)
        nc.vector.tensor_tensor(on[:], on[:], bank[MMB][:], ALU.mult).then_inc(S("head_on"), 1)

    def a_mlo_dve(dve, u):
        dve.wait_ge(*at_head("a", "mhi", u + 1))
        nc.vector.tensor_tensor(tile_at(mlo, u), as3(on[:], u), tile_at(mhi, u),
                                ALU.subtract).then_inc(S("head_mlo"), 1)
        dve.wait_ge(*at_head("a", "mlo", u + 1))

    def qk_sum_pe(pe, ph, t, u, r, rows, m, nh, b):
        pe.wait_ge(*at_head(ph, t + "sq", u + 1))
        rs_sum_pe(r, [(sqb, rows)], M[m][:, 0:64 * nh:64], nh, b)

    def qk_rot_pe(pe, ph, t, u, rows, m):
        pe.wait_ge(*at_head(ph, t + "t", u + 1))
        nc.tensor.matmul(bank[MMB][0:rows, :], M[m][0:rows, 0:rows], tb[0:rows, :], start=True,
                         stop=True).then_inc(S(f"head_{t}rot"), 1)

    def qk_t_dve(dve, ph, t, u, r, rows, y, gain, b, out):
        dve.wait_ge(S("rs_spread"), r + 1)
        nc.vector.scalar_tensor_tensor(out[0:rows, :], y[0:rows, :], gain, bank[b][0:rows, :], ALU.mult,
                                       ALU.mult).then_inc(S(f"head_{t}t"), 1)

    def qk_cos_pool(pool, ph, t, u, rows, y, tab):
        pool.wait_ge(*at_head(ph, t + "t", u + 1))
        nc.gpsimd.tensor_tensor(y[0:rows, :], tb[0:rows, :], tab[0:rows, 0, :], ALU.mult).then_inc(S(f"head_{t}c"), 1)

    def qk_rope_dve(dve, ph, t, u, rows, y, tab):
        dve.wait_ge(*at_head(ph, t + "rot", u + 1))
        dve.wait_ge(*at_head(ph, t + "c", u + 1))
        nc.vector.tensor_tensor(tb[0:rows, :], bank[MMB][0:rows, :], tab[0:rows, 1, :],
                                ALU.mult).then_inc(S(f"head_{t}s"), 1)
        dve.wait_ge(*at_head(ph, t + "s", u + 1))
        nc.vector.tensor_tensor(y[0:rows, :], y[0:rows, :], tb[0:rows, :], ALU.add).then_inc(S(f"head_{t}y2"), 1)
        dve.wait_ge(*at_head(ph, t + "y2", u + 1))


    def a_proj_pe(pe, u, t):
        c = "qkv".index(t)
        g = u * 3 + (G_A + c)
        if t == "q" and not (is_first(u)):
            pe.wait_ge(*at_head("a", "vy", u))
        if t == "k" and not is_first(u):
            pe.wait_ge(*at_head("a", "vlo", u))
        if t == "v":
            pe.wait_ge(*at_head("a", "qy", u + 1))
        project(pe, g, slot(G_A + c), bank[PJ[c % 2]][:], h_hi, h_lo)

    def a_y_dve(dve, u, t):
        c = "qkv".index(t)
        dve.wait_ge(S("chunk_done"), u * 3 + (G_A + c + 1))
        y = (yq, yk, yv)[c]
        nc.vector.tensor_tensor(y[:], bank[PJ[c % 2]][:], rstd[:], ALU.mult).then_inc(S(f"head_{t}y"), 1)

    def a_sq_act(act, u, t):
        act.wait_ge(*at_head("a", t + "y", u + 1))
        nc.scalar.activation(sqb[:], (yq, yk)["qk".index(t)][:], ACT.Square).then_inc(S(f"head_{t}sq"), 1)

    def a_qslot_act(act, u):
        act.wait_ge(*at_head("a", "qy2", u + 1))
        if not (is_first(u)):
            act.wait_ge(*at_head("a", "s", u * NB))
        for j in range(2):
            r = slice(64 * j, 64 * j + 64)
            nc.scalar.activation(qhi[r, j, :], yq[r, :], ACT.Copy).then_inc(S("head_qhi"), 1)

    def a_kslot_act(act, u):
        act.wait_ge(*at_head("a", "ky2", u + 1))
        nc.scalar.activation(khi[:], yk[:], ACT.Copy).then_inc(S("head_khi"), 1)

    def a_qslot_dve(dve, u):
        dve.wait_ge(*at_head("a", "qhi", u * 2 + 2))
        for j in range(2):
            r = slice(64 * j, 64 * j + 64)
            nc.vector.tensor_tensor(qlo[r, j, :], yq[r, :], qhi[r, j, :], ALU.subtract).then_inc(S("head_qlo"), 1)

    def a_kslot_dve(dve, u):
        dve.wait_ge(*at_head("a", "khi", u + 1))
        nc.vector.tensor_tensor(klo[:], yk[:], khi[:], ALU.subtract).then_inc(S("head_klo"), 1)

    B_LOOP = (B_HEADS - 3) // 2
    A_SCALE = A_DIM ** -0.5
    B_SCALE = B_QK ** -0.5

    def b_width(u):
        return WB if isinstance(u, int) and u < 2 else WB + W_AHEAD

    def b_load(sp, u, s):
        n = b_width(u)
        src = w_b[u, :, 0:n] if isinstance(u, int) else w_b[bass.ds(u, 1), :, :].rearrange("o p n -> p (o n)")
        sp.dma_start(bwraw[:, s, 0:n], src).then_inc(S(f"b_in{s}"), 16)

    def b_hi_act(act, s, use, n=WB + W_AHEAD):
        act.wait_ge(S(f"b_in{s}"), use * 16)
        nc.scalar.activation(bwhi[:, s, 0:n], bwraw[:, s, 0:n], ACT.Copy).then_inc(S("head_whi"), 1)

    def b_lo_pool(pool, u, s):
        pool.wait_ge(*at_head("b", "whi", u + 1))
        n = b_width(u)
        nc.gpsimd.tensor_tensor(bwlo[:, s, 0:n], bwraw[:, s, 0:n], bwhi[:, s, 0:n],
                                ALU.subtract).then_inc(S("head_wlo"), 1)

    def b_proj_pe(pe, u, s):
        pe.wait_ge(*at_head("b", "wlo", u + 1))
        if not (is_first(u)):
            pe.wait_ge(*at_head("b", "vy", u))
        n = 0
        for kt in range(2):
            c = slice(kt * B_QK, (kt + 1) * B_QK)
            for a, o in ((bwhi, qlhi), (bwhi, qllo), (bwlo, qlhi)):
                last = nc.tensor.matmul(bank[PJ[0]][0:B_QK, :], a[:, s, c], o[:, kt, :], start=(n == 0), stop=(n == 5))
                n += 1
        last.then_inc(S("head_q"), 1)

    def b_proj_kv_pe(pe, s):
        for n, (a, o) in enumerate(((bwhi, kvhi), (bwhi, kvlo), (bwlo, kvhi))):
            last = nc.tensor.matmul(bank[PJ[1]][:], a[:, s, 2 * B_QK:WB], o[:], start=(n == 0), stop=(n == 2))
        last.then_inc(S("head_kv"), 1)

    def b_squares(u):
        return (sqb, yk) if is_first(u) else (e1[:, 0, :], e1[:, 1, :])

    def b_squares_act(act, u):
        q2, k2 = b_squares(u)
        act.wait_ge(*at_head("b", "q", u + 1))
        nc.scalar.activation(q2[0:B_QK, :], bank[PJ[0]][0:B_QK, :], ACT.Square).then_inc(S("head_qsq"), 1)
        act.wait_ge(*at_head("b", "kv", u + 1))
        nc.scalar.activation(k2[0:B_NOPE, :], bank[PJ[1]][0:B_NOPE, :], ACT.Square).then_inc(S("head_ksq"), 1)

    def b_copies_act(act, u):
        act.wait_ge(*at_head("b", "qlo", u))
        nc.scalar.activation(yq[0:B_QK, :], bank[PJ[0]][0:B_QK, :], ACT.Copy).then_inc(S("head_qy"), 1)
        nc.scalar.activation(yv[:], bank[PJ[1]][:], ACT.Copy).then_inc(S("head_vy"), 1)

    def b_sums_pe(pe, u):
        pe.wait_ge(*at_head("b", "qsq", u + 1))
        pe.wait_ge(*at_head("b", "ksq", u + 1))
        q2, k2 = b_squares(u)
        for i in range(NB):
            c = slice(i * P, (i + 1) * P)
            nc.tensor.matmul(bank[MMB][:, 3 * i:3 * i + 2], q2[0:B_QK, c], M["blk_b"][0:B_QK, 0:128:64],
                             start=True, stop=True)
            last = nc.tensor.matmul(bank[MMB][:, 3 * i + 2:3 * i + 3], k2[0:B_NOPE, c],
                                    M["blk_b"][0:B_NOPE, 0:1], start=True, stop=True)
        last.then_inc(S("rs_sum"), 1)

    def b_spread_k_pe(pe, u):
        for i in range(NB):
            col = T_Z[0] + 3 * i + 2
            last = nc.tensor.matmul(bank[KMB][0:B_NOPE, i * P:(i + 1) * P],
                                    tiny[:, col:col + 1].broadcast_to([P, B_NOPE]), M["ident"],
                                    start=True, stop=True)
        last.then_inc(S("rs_k_spread"), 1)

    def b_q_dve(dve, u):
        dve.wait_ge(*at_head("b", "qy", u + 1))
        qk_t_dve(dve, "b", "q", u, rs_b(u), B_QK, yq, v(V_BQ, rows=B_QK), MMB, tb)

    def b_k_dve(dve, u):
        dve.wait_ge(*at_head("b", "vy", u + 1))
        dve.wait_ge(S("rs_k_spread"), u + 1)
        dve.wait_ge(*at_head("b", "klo", u))
        nc.vector.scalar_tensor_tensor(yk[0:B_NOPE, :], yv[0:B_NOPE, :], v(V_BK, rows=B_NOPE),
                                       bank[KMB][0:B_NOPE, :], ALU.mult, ALU.mult).then_inc(S("head_kt"), 1)

    def b_qslot_act(act, u):
        act.wait_ge(*at_head("b", "qy2", u + 1))
        act.wait_ge(*at_head("b", "s", u * NB))
        nc.scalar.activation(qhi[0:B_QK, 0, :], yq[0:B_QK, :], ACT.Copy).then_inc(S("head_qhi"), 1)

    def b_kslot_act(act, u):
        act.wait_ge(*at_head("b", "kt", u + 1))
        nc.scalar.activation(khi[0:B_NOPE, :], yk[0:B_NOPE, :], ACT.Copy).then_inc(S("head_khi"), 1)

    def b_qslot_pool(pool, u):
        pool.wait_ge(*at_head("b", "qhi", u + 1))
        nc.gpsimd.tensor_tensor(qlo[0:B_QK, 0, :], yq[0:B_QK, :], qhi[0:B_QK, 0, :],
                                ALU.subtract).then_inc(S("head_qlo"), 1)

    def b_kslot_pool(pool, u):
        pool.wait_ge(*at_head("b", "khi", u + 1))
        nc.gpsimd.tensor_tensor(klo[0:B_NOPE, :], yk[0:B_NOPE, :], khi[0:B_NOPE, :],
                                ALU.subtract).then_inc(S("head_klo"), 1)

    def head_out_act(act, ph, u, j, k):
        act.wait_ge(*at_head(ph, "o", u + 1))
        nc.scalar.activation(tile_at(mhi, k, slice(64 * j, 64 * j + 64)), as3(bank[OB][0:64, :], k),
                             ACT.Copy).then_inc(S("head_mhi"), 1)

    def head_out_dve(dve, ph, u, j, k):
        dve.wait_ge(*at_head(ph, "mhi", u + 1))
        r = slice(64 * j, 64 * j + 64)
        nc.vector.tensor_tensor(tile_at(mlo, k, r), as3(bank[OB][0:64, :], k), tile_at(mhi, k, r),
                                ALU.subtract).then_inc(S("head_mlo"), 1)

    ZB = ((0, 1, 2), (3, 4, 5))
    CP, CO = 6, 7
    ZAT = ((0, 0), (1, 0), (2, 0), (2, 256))
    BW = (512, 384, 512)
    BO = (0, 512, 896)

    def c_proj_bank(u, c):
        return bank[(CP, *ZB[0])[c]] if is_first(u) else bank[CP]

    def c_proj_pe(pe, u, t, n=None):
        c = "qkv".index(t)
        if not (is_first(u)):
            if t == "q":
                pe.wait_ge(S("c_vy"), u)
            else:
                pe.wait_ge(S("c_qy" if t == "k" else "c_ky"), u + 1)
        project(pe, u * 3 + (G_C + c), slot(G_C + c), c_proj_bank(u, c)[:], h_hi, h_lo, n)

    def c_scores_pe(pe, u, j):
        if j == 0:
            pe.wait_ge(S("c_qhi"), u * 4 + 4)
            pe.wait_ge(S("c_qlo"), u * 2 + 2)
            pe.wait_ge(S("c_klo"), u * 2 + 2)
        for kb in range(NB):
            b, o = ZAT[kb]
            z = bank[ZB[j][b]][:, o:o + TW[kb]]
            for n, (rows, c) in enumerate(((P, cqhi), (C_DIM, cqlo))):
                nc.tensor.matmul(z, ck[0:rows, j, kb * P:(kb + 1) * P], c[0:rows, j, TQ[kb]:SEQ],
                                 start=(n == 0 and kb < 3), stop=False, skip_group_check=True)
            last = nc.tensor.matmul(z[:, 0:256], ident_r[:], csmask[:, 1 if kb == 3 else 0, :], start=False,
                                    stop=True, skip_group_check=True)
            if kb != 2:
                last.then_inc(S(f"c_z{j}"), 1)

    def c_chain_act(act, u, j, b):
        z, a = bank[ZB[j][b]][:, 0:BW[b]], ca[j][:, BO[b]:BO[b] + BW[b]]
        n = u * 3 + (b + 1)
        act.wait_ge(S(f"c_z{j}"), n)
        nc.scalar.activation(a, z, ACT.Abs).then_inc(S(f"c_abs{j}"), 1)
        act.wait_ge(S(f"c_abs{j}"), n)
        nc.scalar.activation(a, a, ACT.Exp, scale=-1.0).then_inc(S(f"c_ex{j}"), 1)
        act.wait_ge(S(f"c_ex{j}"), n)
        nc.scalar.activation(a, a, ACT.Ln, bias=1.0).then_inc(S(f"c_ln{j}"), 1)

    def c_chain_dve(dve, u, j, b):
        z = bank[ZB[j][b]][:, 0:BW[b]]
        r = slice(BO[b], BO[b] + BW[b])
        n = u * 3 + (b + 1)
        dve.wait_ge(S(f"c_ln{j}"), n)
        nc.vector.scalar_tensor_tensor(cs[:, r], z, 0.0, ca[j][:, r], ALU.max, ALU.add).then_inc(S(f"c_sp{j}"), 1)
        dve.wait_ge(S(f"c_sp{j}"), n)
        nc.vector.tensor_copy(cshi[j][:, r], cs[:, r]).then_inc(S(f"c_shi{j}"), 1)
        dve.wait_ge(S(f"c_shi{j}"), n)
        nc.vector.tensor_tensor(cslo[j][:, r], cs[:, r], cshi[j][:, r], ALU.subtract).then_inc(S(f"c_slo{j}"), 1)

    def c_tail_pe(pe, u, j):
        pe.wait_ge(S(f"c_slo{j}"), u * 3 + 3)
        for kb in range(NB):
            b, o = ZAT[kb]
            for src in range(kb, NB):
                w = TW[src]
                z = bank[ZB[j][b]][:, o + TW[kb] - w:o + TW[kb]]
                for t in (cshi, cslo):
                    last = nc.tensor.matmul(z, cmats[:, 0 if src == kb else 1, :], t[j][:, TO[src]:TO[src] + w],
                                            start=False, stop=True, skip_group_check=True)
            if kb != 2:
                last.then_inc(S(f"c_tail{j}"), 1)

    def c_w_act(act, u, j, b):
        act.wait_ge(S(f"c_tail{j}"), u * 3 + (b + 1))
        a = ca[j][:, BO[b]:BO[b] + BW[b]]
        nc.scalar.activation(a, bank[ZB[j][b]][:, 0:BW[b]], ACT.Exp).then_inc(S(f"c_w{j}"), 1)

    def c_w_dve(dve, u, j, b):
        r = slice(BO[b], BO[b] + BW[b])
        n = u * 3 + (b + 1)
        dve.wait_ge(S(f"c_w{j}"), n)
        if b == 0:
            dve.wait_ge(S(f"c_tail{j}"), u * 3 + 3)
        nc.vector.tensor_copy(cshi[j][:, r], ca[j][:, r]).then_inc(S(f"c_whi{j}"), 1)
        dve.wait_ge(S(f"c_whi{j}"), n)
        nc.vector.tensor_tensor(cslo[j][:, r], ca[j][:, r], cshi[j][:, r], ALU.subtract).then_inc(S(f"c_wlo{j}"), 1)

    def c_values_pe(pe, u, j):
        if j == 0:
            pe.wait_ge(S("c_vlo"), u + 1)
        else:
            pe.wait_ge(S("c_out"), u * 2 + 1)
        for kb in range(NB):
            if kb < 3:
                pe.wait_ge(S(f"c_wlo{j}"), u * 3 + (kb + 1))
            for n, (rows, c) in enumerate(((P, cshi), (C_DIM, cslo))):
                last = nc.tensor.matmul(bank[CO][0:rows, TQ[kb]:SEQ], cv[:, kb, j, 0:rows],
                                        c[j][:, TO[kb]:TO[kb] + TW[kb]], start=(kb == 0 and n == 0),
                                        stop=(kb == NB - 1), skip_group_check=True)
        last.then_inc(S("c_o"), 1)

    def c_y_dve(dve, u, t):
        c = "qkv".index(t)
        dve.wait_ge(S("chunk_done"), u * 3 + (G_C + c + 1))
        y = (cyq, cyk, cyv)[c]
        if t == "q":
            nc.vector.scalar_tensor_tensor(y[:], c_proj_bank(u, c)[:], C_DIM ** -0.5, rstd[:], ALU.mult,
                                           ALU.mult).then_inc(S("c_qy"), 1)
        else:
            nc.vector.tensor_tensor(y[:], c_proj_bank(u, c)[:], rstd[:], ALU.mult).then_inc(S(f"c_{t}y"), 1)

    def c_slot_act(act, u, t):
        act.wait_ge(S(f"c_{t}y"), u + 1)
        for j in range(2):
            r = slice(C_DIM * j, C_DIM * (j + 1))
            if t == "k":
                nc.scalar.activation(ck[0:C_DIM, j, :], cyk[r, :], ACT.Copy).then_inc(S("c_khi"), 1)
            else:
                for half in range(2):
                    nc.scalar.activation(cqhi[C_DIM * half:C_DIM * (half + 1), j, :], cyq[r, :],
                                         ACT.Copy).then_inc(S("c_qhi"), 1)

    def c_slot_dve(dve, u, t):
        for j in range(2):
            r = slice(C_DIM * j, C_DIM * (j + 1))
            if t == "k":
                dve.wait_ge(S("c_khi"), u * 2 + (j + 1))
                nc.vector.tensor_tensor(ck[C_DIM:P, j, :], cyk[r, :], ck[0:C_DIM, j, :],
                                        ALU.subtract).then_inc(S("c_klo"), 1)
            else:
                dve.wait_ge(S("c_qhi"), u * 4 + (2 * j + 1))
                nc.vector.tensor_tensor(cqlo[0:C_DIM, j, :], cyq[r, :], cqhi[0:C_DIM, j, :],
                                        ALU.subtract).then_inc(S("c_qlo"), 1)

    def c_vt_pe(pe, u):
        pe.wait_ge(S("c_vy"), u + 1)
        if not is_first(u):
            pe.wait_ge(S("c_out"), u * 2)
        for b in range(NB):
            last = nc.tensor.transpose(bank[CO][:, b * P:(b + 1) * P], cyv[:, b * P:(b + 1) * P], M["ident"])
        last.then_inc(S("c_vt"), 1)

    def c_v_parts():
        src = bank[CO][:].rearrange("p (b j n) -> p b j n", j=2, n=C_DIM)
        return src, cv[:, :, :, 0:C_DIM], cv[:, :, :, C_DIM:P]

    def c_v_act(act, u):
        act.wait_ge(S("c_vt"), u + 1)
        src, hi, _ = c_v_parts()
        nc.scalar.activation(hi, src, ACT.Copy).then_inc(S("c_vhi"), 1)

    def c_v_dve(dve, u):
        dve.wait_ge(S("c_vhi"), u + 1)
        src, hi, lo = c_v_parts()
        nc.vector.tensor_tensor(lo, src, hi, ALU.subtract).then_inc(S("c_vlo"), 1)

    with nc.Block() as block:

        @block.sync
        def _(sp):
            for d in range(KT):
                sp.dma_start(x[:, d, :], xt[d, :, :]).then_inc(S(f"x_in{d}"), 16)
                if d == 0:
                    load_chunk(sp, 0, 0, w_in[0, :, :], W_IN)
            sp.dma_start(mat[:], mats[:, :, :]).then_inc(S("mat_in"), 16)
            for g in (1, 2):
                load_chunk(sp, g, g, w_in[g, :, :], W_IN)
            sp.dma_start(tabb[:], tabs_b[:, :, :]).then_inc(S("tabb_in"), 16)
            sp.dma_start(taba[:], tabs_a[:, :, :]).then_inc(S("taba_in"), 16)
            sp.dma_start(rawm[:], masks_a[:, :, :]).then_inc(S("masks_in"), 16)

            def run(g0, n, src, first, width):
                loops = n // WSLOTS
                if loops > 1:
                    with sp.Fori(0, loops) as i:
                        for j in range(WSLOTS):
                            load_chunk(sp, i * WSLOTS + (g0 + j), slot(g0 + j),
                                       src[bass.ds(i * WSLOTS + (first + j), 1), :, :].rearrange("o p n -> p (o n)"),
                                       width)
                else:
                    loops = 0
                for k in range(loops * WSLOTS, n):
                    load_chunk(sp, g0 + k, slot(g0 + k), src[first + k, :, 0:width], width)

            run(3, G_OUT0, w_in, 3, W_IN)
            sp.wait_ge(S("chunk_done"), G_OUT0)
            for u in range(2):
                b_load(sp, u, u)
            with sp.Fori(1, B_HEADS // 2) as i:
                for s in range(2):
                    sp.wait_ge(*at_head("b", "wlo", i * 2 + (s - 1)))
                    b_load(sp, i * 2 + s, s)
            run(G_OUT0 + 3, OUT_AHEAD - 3, w_in, G_OUT0 + 3, W_IN - W_AHEAD)
            run(G_OUT0 + OUT_AHEAD, KT - OUT_AHEAD, w_in, G_OUT0 + OUT_AHEAD, W_IN)
            sp.wait_ge(S("chunk_done"), G_OUT0 + 1)
            sp.dma_start(crawm[:], masks_c[:, :]).then_inc(S("crawm_in"), 16)
            row, down = G_OUT0 + KT, 0
            for s in range(2):
                run(G_FFN0 + s * FFN_HALF, 2 * HALF_F, w_in, row, W_IN)
                row += 2 * HALF_F
                run(G_FFN0 + s * FFN_HALF + 2 * HALF_F, KT, w_down, down, W_DOWN)
                down += KT
            run(G_C, 3 * C_PAIRS, w_in, row, W_IN)
            row += 3 * C_PAIRS
            run(G_OUT1, KT, w_in, row, W_IN)
            row += KT
            for s in range(2):
                run(G_FFN1 + s * FFN_HALF, 2 * HALF_F, w_in, row, W_IN)
                row += 2 * HALF_F
                run(G_FFN1 + s * FFN_HALF + 2 * HALF_F, KT, w_down, down, W_DOWN)
                down += KT
            for d in range(KT):
                sp.wait_ge(*at_net(1, "x", KT + d + 1))
                sp.dma_start(out[d, :, :], x[:, d, :]).then_inc(S("out"), 16)
            sp.wait_ge(S("out"), 16 * KT)

        @block.gpsimd
        def _(pool):
            def run(g0, n, width):
                loops = n // WSLOTS
                if loops > 1:
                    with pool.Fori(0, loops) as i:
                        for j in range(WSLOTS):
                            split_lo(pool, i * WSLOTS + (g0 + j), slot(g0 + j), width)
                else:
                    loops = 0
                for k in range(loops * WSLOTS, n):
                    split_lo(pool, g0 + k, slot(g0 + k), width)

            split_lo(pool, 0, 0, W_IN)
            for d in range(1, KT):
                norm_pool(pool, 0, d)
            for g in (1, 2):
                split_lo(pool, g, g, W_IN)
            for g in range(3, G_A + 3):
                split_lo(pool, g, slot(g), W_IN)
            pool.wait_ge(S("tabb_in"), 16)
            qk_cos_pool(pool, "r", "q", 0, B_QK, on, tabb)
            pool.wait_ge(S("taba_in"), 16)

            def a_pool(nxt, g):
                split_lo(pool, g, slot(G_A), W_IN)
                qk_cos_pool(pool, "a", "q", nxt, P, yq, taba)
                split_lo(pool, g + 1, slot(G_A + 1), W_IN)
                qk_cos_pool(pool, "a", "k", nxt, P, yk, taba)
                split_lo(pool, g + 2, slot(G_A + 2), W_IN)

            a_pool(0, G_A + 3)
            with pool.Fori(1, A_HEADS) as i:
                a_pool(i, i * 3 + (G_A + 3))

            def b_pool(nxt):
                qk_cos_pool(pool, "b", "q", nxt, B_QK, yq, tabb)
                b_kslot_pool(pool, nxt)
                b_qslot_pool(pool, nxt)

            for u in range(2):
                b_lo_pool(pool, u, u)
            b_pool(0)
            b_lo_pool(pool, 2, 0)
            with pool.Fori(0, B_LOOP) as i:
                for s in range(2):
                    b_pool(i * 2 + (s + 1))
                    b_lo_pool(pool, i * 2 + (s + 3), 1 - s)
            for u in range(2 * B_LOOP, B_HEADS - 1):
                b_pool(u + 1)
                if u + 3 < B_HEADS:
                    b_lo_pool(pool, u + 3, (u + 3) % 2)
            for d in range(KT):
                split_lo(pool, G_OUT0 + d + 3, slot(G_OUT0 + d + 3), width_of(G_OUT0 + d + 3))
                norm_pool(pool, 1, d)
            for L, g_first in ((0, G_FFN0), (1, G_FFN1)):
                run(g_first + 3, 2 * HALF_F - 3, W_IN)
                run(g_first + 2 * HALF_F, KT, W_DOWN)
                run(g_first + FFN_HALF, 2 * HALF_F, W_IN)
                gd = g_first + FFN_HALF + 2 * HALF_F
                run(gd, 3, W_DOWN)
                for d in range(KT):
                    if gd + d + 3 < N_CHUNKS:
                        split_lo(pool, gd + d + 3, slot(gd + d + 3), width_of(gd + d + 3))
                    if L == 0:
                        norm_pool(pool, 2, d)
                if L == 0:
                    run(G_C + 3, 3 * C_PAIRS - 3, W_IN)
                    run(G_OUT1, 3, W_IN)
                    for d in range(KT):
                        split_lo(pool, G_OUT1 + d + 3, slot(G_OUT1 + d + 3), width_of(G_OUT1 + d + 3))
                        norm_pool(pool, 3, d)

        @block.scalar
        def _(act):
            act.preload_act_table_set("natural_log_exp_and_others")
            act.dma_start(vec[:], vecs[:, :]).then_inc(S("vec_in"), 16)
            act.wait_ge(S("vec_in"), 16)
            for d in range(KT):
                act.wait_ge(S(f"x_in{d}"), 16)
                norm_act(act, 0, d)
                if d in (0, 6, 7):
                    hi_static(act, (0, 6, 7).index(d))
            act.wait_ge(S("lam_sum"), 1)
            nc.scalar.activation(tiny[:, T_LE:T_LE + 2], bank[5][:, 0:2], ACT.Exp).then_inc(S("lam_exp"), 1)
            rs_act(act, RS_NORM[0], 1)
            hi_static(act, 3)
            act.wait_ge(S("l_y"), 1)
            nc.scalar.activation(sqb[:], yq[:], ACT.Square).then_inc(S("l_sq"), 1)
            hi_static(act, 4)
            act.wait_ge(S("l_y"), 2)
            nc.scalar.activation(tb[:], yk[:], ACT.Square).then_inc(S("l_sq"), 1)
            rs_act(act, RS_QL, 1)
            hi_static(act, 5)
            act.wait_ge(S("l_y"), 3)
            nc.scalar.activation(sqb[:], yv[:], ACT.Square).then_inc(S("l_sq"), 1)
            for k in range(2):
                act.wait_ge(S("l_n"), k + 1)
                nc.scalar.activation(qlhi[:, k, :], (yq, yk)[k][:], ACT.Copy).then_inc(S("l_hi"), 1)
            hi_static(act, 6)
            rs_act(act, RS_KVL, 1)
            act.wait_ge(S("l_y"), 4)
            nc.scalar.activation(sqb[0:B_QK, :], on[0:B_QK, :], ACT.Square).then_inc(S("head_qsq"), 1)
            act.wait_ge(S("l_n"), 3)
            nc.scalar.activation(kvhi[:], yv[:], ACT.Copy).then_inc(S("l_hi"), 1)
            hi_static(act, G_A + 3)
            rs_act(act, RS_ROPE, 2)
            a_sq_act(act, 0, "q")
            hi_static(act, G_A + 4)
            rs_act(act, rs_a(0, "q"), 2)
            a_sq_act(act, 0, "k")
            hi_static(act, G_A + 5)
            rs_act(act, rs_a(0, "k"), 2)
            a_qslot_act(act, 0)
            a_kslot_act(act, 0)
            v_act(act, "a", 0, 0, VTA)

            def a_act(u, nxt, hi):
                if not is_first(u):
                    rs_act(act, rs_a(u - 1, "out"), 1)
                softmax_act(act, "a", u, 0, A_SCALE)
                softmax_act(act, "a", u, 1, A_SCALE)
                a_sq_act(act, nxt, "q")
                hi(0)
                if not is_first(u):
                    a_mhi_act(act, u - 1)
                softmax_act(act, "a", u, 2, A_SCALE)
                softmax_act(act, "a", u, 3, A_SCALE)
                rs_act(act, rs_a(nxt, "q"), 2)
                hi(1)
                a_sq_act(act, nxt, "k")
                ptrans_act(act, "a", u, 0)
                ptrans_act(act, "a", u, 1)
                rs_act(act, rs_a(nxt, "k"), 2)
                a_qslot_act(act, nxt)
                hi(2)
                ptrans_act(act, "a", u, 2)
                ptrans_act(act, "a", u, 3)
                a_kslot_act(act, nxt)
                a_osq_act(act, u)
                v_act(act, "a", nxt, 0, VTA)

            a_act(0, 1, lambda c: hi_static(act, G_A + 6 + c))
            with act.Fori(1, A_HEADS - 1) as i:
                a_act(i, i + 1, lambda c: hi_at(act, G_A + 6 + c, i, 3))

            u = A_HEADS - 1
            for h in range(2):
                b_hi_act(act, h, 1, WB)
            rs_act(act, rs_a(u - 1, "out"), 1)
            softmax_act(act, "a", u, 0, A_SCALE)
            softmax_act(act, "a", u, 1, A_SCALE)
            a_mhi_act(act, u - 1)
            act.wait_ge(*at_head("a", "klo", A_HEADS))
            b_squares_act(act, 0)
            softmax_act(act, "a", u, 2, A_SCALE)
            b_copies_act(act, 0)
            softmax_act(act, "a", u, 3, A_SCALE)
            act.wait_ge(*at_head("r", "kept", 1))
            nc.scalar.activation(khi[64:96, :], rope_keep[64:96, :], ACT.Copy).then_inc(S("kr_hi"), 1)
            rs_act(act, rs_b(0), 3)
            ptrans_act(act, "a", u, 0)
            b_hi_act(act, 0, 2)
            for kb in range(1, NB):
                ptrans_act(act, "a", u, kb)
            b_kslot_act(act, 0)
            a_osq_act(act, u)
            b_qslot_act(act, 0)
            act.wait_ge(*at_head("a", "p", A_HEADS * NB))
            v_act(act, "b", 0)
            rs_act(act, rs_a(u, "out"), 1)
            b_squares_act(act, 1)
            a_mhi_act(act, u)

            def b_act(u, n, s, k, hi):
                if n:
                    rs_act(act, rs_b(u + 1), 3)
                softmax_act(act, "b", u, 0, B_SCALE)
                softmax_act(act, "b", u, 1, B_SCALE)
                if n:
                    b_copies_act(act, u + 1)
                softmax_act(act, "b", u, 2, B_SCALE)
                softmax_act(act, "b", u, 3, B_SCALE)
                ptrans_act(act, "b", u, 0)
                if hi is not None:
                    b_hi_act(act, 1 - s, hi)
                ptrans_act(act, "b", u, 1)
                ptrans_act(act, "b", u, 2)
                if n:
                    b_kslot_act(act, u + 1)
                    v_act(act, "b", u + 1, 1 - s, VTB)
                ptrans_act(act, "b", u, 3)
                if n:
                    b_qslot_act(act, u + 1)
                if n > 1:
                    b_squares_act(act, u + 2)
                head_out_act(act, "b", u, s, k)

            with act.Fori(0, B_LOOP) as i:
                for s in range(2):
                    b_act(i * 2 + s, 2, s, i + 4, i + (2 + s))
            for u in range(2 * B_LOOP, B_HEADS):
                b_act(u, min(2, B_HEADS - 1 - u), u % 2, A_HEADS + u // 2,
                      (u + 3) // 2 + 1 if u + 3 < B_HEADS else None)
            out_act(act, G_OUT0, 0, 1)
            rs_act(act, RS_NORM[1], 1)
            ffn_act(act, 0, 2)

            act.preload_act_table_set("natural_log_exp_and_others")
            rs_act(act, RS_NORM[2], 1)

            def c_act(u, nxt, hi):
                if u is not None:
                    for b in range(3):
                        c_chain_act(act, u, 0, b)
                    if not is_first(u):
                        c_lower_act(u - 1, 1)
                    c_chain_act(act, u, 1, 0)
                    if not is_first(u):
                        cout_act(u - 1, 1)
                    c_chain_act(act, u, 1, 1)
                    c_chain_act(act, u, 1, 2)
                if nxt is not None:
                    c_slot_act(act, nxt, "q")
                    hi(0)
                if u is not None:
                    c_w_act(act, u, 0, 0)
                    c_v_act(act, u)
                    for b in range(1, 3):
                        c_w_act(act, u, 0, b)
                if nxt is not None:
                    c_slot_act(act, nxt, "k")
                if u is not None:
                    c_lower_act(u, 0)
                if nxt is not None:
                    hi(1)
                if u is not None:
                    for b in range(3):
                        c_w_act(act, u, 1, b)
                    cout_act(u, 0)
                if nxt is not None:
                    act.wait_ge(S("c_vy"), nxt + 1)
                    hi(2)
                if nxt is None:
                    c_lower_act(u, 1)
                    cout_act(u, 1)

            def c_lower_act(u, j):
                act.wait_ge(S("c_o"), u * 2 + (j + 1))
                nc.scalar.activation(co[C_DIM * j:C_DIM * (j + 1), :], bank[CO][C_DIM:P, :],
                                     ACT.Copy).then_inc(S("c_lower"), 1)

            def cout_act(u, j):
                act.wait_ge(S("c_out"), u * 2 + (j + 1))
                r = slice(C_DIM * j, C_DIM * (j + 1))
                nc.scalar.activation(tile_at(mhi, u, r), as3(co[r, :], u), ACT.Copy).then_inc(S("c_mhi"), 1)

            c_act(None, 0, lambda c: hi_static(act, G_C + 3 + c))
            c_act(0, 1, lambda c: hi_static(act, G_C + 6 + c))
            with act.Fori(1, C_PAIRS - 1) as i:
                c_act(i, i + 1, lambda c: hi_at(act, G_C + 6 + c, i, 3))
            c_act(C_PAIRS - 1, None, None)
            out_act(act, G_OUT1, 1, 3)
            rs_act(act, RS_NORM[3], 1)
            ffn_act(act, 1, None)

        @block.vector
        def _(dve):
            nc.vector.memset(qhi[64:128, 0, :].bitcast(F32), 0.0)
            nc.vector.memset(qhi[0:64, 1, :].bitcast(F32), 0.0)
            nc.vector.memset(qlo[64:128, 0, :].bitcast(F32), 0.0)
            nc.vector.memset(qlo[0:64, 1, :].bitcast(F32), 0.0)
            nc.vector.memset(pthi[:, TO[3]:TO[3] + P].bitcast(F32), 0.0)
            nc.vector.memset(ptlo[:, TO[3]:TO[3] + P].bitcast(F32), 0.0)
            dve.wait_ge(S("vec_in"), 16)
            nc.vector.tensor_tensor(tiny[:, T_LP:T_LP + 1], v(V_LAM), v(V_LAM + 1), ALU.mult).then_inc(S("lam_prod"), 1)
            nc.vector.tensor_tensor(tiny[:, T_LP + 1:T_LP + 2], v(V_LAM + 2), v(V_LAM + 3),
                                    ALU.mult).then_inc(S("lam_prod"), 1)
            nc.vector.tensor_scalar(tiny[:, T_OG:T_OG + 1], v(V_AO), 1.0 - LAM0, None,
                                    ALU.mult).then_inc(S("head_og"), 1)
            for d in range(KT):
                norm_dve(dve, 0, d)
            dve.wait_ge(S("mat_in"), 16)
            nc.vector.tensor_copy(ident_r[:], M["ident"])
            dve.wait_ge(S("lam_exp"), 1)
            nc.vector.tensor_tensor(tiny[:, T_LD:T_LD + 1], tiny[:, T_LE:T_LE + 1], tiny[:, T_LE + 1:T_LE + 2],
                                    ALU.subtract).then_inc(S("lam_dif"), 1)
            dve.wait_ge(S("lam_dif"), 1)
            nc.vector.tensor_scalar(tiny[:, T_LAM:T_LAM + 1], tiny[:, T_LD:T_LD + 1], LAM0, None,
                                    ALU.add).then_inc(S("lam"), 1)
            dve.wait_ge(S("lam"), 1)
            norm_rstd_dve(dve, 0, MMB)
            for c in range(3):
                dve.wait_ge(S("chunk_done"), c + 1)
                nc.vector.tensor_tensor((yq, yk, yv)[c][:], bank[(2, 3, 0)[c]][:], rstd[:],
                                        ALU.mult).then_inc(S("l_y"), 1)
            rs_mean_dve(dve, RS_QL, 1.0 / B_QRANK, 1, MMB)
            rs_newton_dve(dve, RS_QL, 1)
            dve.wait_ge(S("rs_spread"), RS_QL + 1)
            for k in range(2):
                y = (yq, yk)[k]
                nc.vector.scalar_tensor_tensor(y[:], y[:], v(V_BQL + k), bank[MMB][:], ALU.mult,
                                               ALU.mult).then_inc(S("l_n"), 1)
                dve.wait_ge(S("l_hi"), k + 1)
                nc.vector.tensor_tensor(qllo[:, k, :], y[:], qlhi[:, k, :], ALU.subtract).then_inc(S("l_lo"), 1)
            dve.wait_ge(S("chunk_done"), 4)
            nc.vector.tensor_tensor(on[:], bank[1][:], rstd[:], ALU.mult).then_inc(S("l_y"), 1)
            rs_mean_dve(dve, RS_KVL, 1.0 / B_KVRANK, 1, 5)
            rs_newton_dve(dve, RS_KVL, 1)
            a_y_dve(dve, 0, "q")
            dve.wait_ge(S("rs_spread"), RS_KVL + 1)
            nc.vector.scalar_tensor_tensor(yv[:], yv[:], v(V_BKVL), bank[6][:], ALU.mult, ALU.mult).then_inc(S("l_n"),
                                           1)
            dve.wait_ge(S("l_hi"), 3)
            nc.vector.tensor_tensor(kvlo[:], yv[:], kvhi[:], ALU.subtract).then_inc(S("l_lo"), 1)
            rs_mean_dve(dve, RS_ROPE, 1.0, 2, OB)
            rs_newton_dve(dve, RS_ROPE, 2)
            dve.wait_ge(S("masks_in"), 16)
            nc.vector.tensor_copy(cmask[:], rawm[:])
            a_y_dve(dve, 0, "k")
            dve.wait_ge(S("tabb_in"), 16)
            qk_t_dve(dve, "r", "q", 0, RS_ROPE, B_QK, on, v(V_BKR, rows=B_QK), MMB, tb)
            rs_mean_dve(dve, rs_a(0, "q"), 1.0 / A_DIM, 2, OB)
            rs_newton_dve(dve, rs_a(0, "q"), 2)
            qk_rope_dve(dve, "r", "q", 0, B_QK, on, tabb)
            nc.vector.tensor_copy(rope_keep[64:96, :], on[64:96, :]).then_inc(S("head_kept"), 1)
            dve.wait_ge(*at_head("r", "kept", 1))
            dve.wait_ge(S("taba_in"), 16)
            qk_t_dve(dve, "a", "q", 0, rs_a(0, "q"), P, yq, v(V_AQ), QMB, tb)
            rs_mean_dve(dve, rs_a(0, "k"), 1.0 / A_DIM, 2, KSB)
            rs_newton_dve(dve, rs_a(0, "k"), 2, 1)
            a_y_dve(dve, 0, "v")
            qk_rope_dve(dve, "a", "q", 0, P, yq, taba)
            qk_t_dve(dve, "a", "k", 0, rs_a(0, "k"), P, yk, v(V_AK), KMB, tb)
            a_qslot_dve(dve, 0)
            qk_rope_dve(dve, "a", "k", 0, P, yk, taba)
            a_kslot_dve(dve, 0)
            v_dve(dve, "a", 0, 0, VTA)

            def a_dve(u, nxt):
                softmax_dve(dve, "a", u, 0, A_SCALE)
                if not is_first(u):
                    a_osum_dve(dve, u - 1)
                softmax_dve(dve, "a", u, 1, A_SCALE)
                probs_dve(dve, "a", u, 0)
                probs_dve(dve, "a", u, 1)
                a_y_dve(dve, nxt, "q")
                if not is_first(u):
                    a_on_dve(dve, u - 1)
                softmax_dve(dve, "a", u, 2, A_SCALE)
                softmax_dve(dve, "a", u, 3, A_SCALE)
                probs_dve(dve, "a", u, 2)
                rs_mean_dve(dve, rs_a(nxt, "q"), 1.0 / A_DIM, 2, OB)
                if not is_first(u):
                    a_mlo_dve(dve, u - 1)
                probs_dve(dve, "a", u, 3)
                rs_newton_dve(dve, rs_a(nxt, "q"), 2)
                a_y_dve(dve, nxt, "k")
                qk_t_dve(dve, "a", "q", nxt, rs_a(nxt, "q"), P, yq, v(V_AQ), MMB, tb)
                ptrans_dve(dve, "a", u, 0)
                rs_mean_dve(dve, rs_a(nxt, "k"), 1.0 / A_DIM, 2, KSB)
                ptrans_dve(dve, "a", u, 1)
                qk_rope_dve(dve, "a", "q", nxt, P, yq, taba)
                rs_newton_dve(dve, rs_a(nxt, "k"), 2, 1)
                a_y_dve(dve, nxt, "v")
                qk_t_dve(dve, "a", "k", nxt, rs_a(nxt, "k"), P, yk, v(V_AK), KMB, tb)
                a_qslot_dve(dve, nxt)
                ptrans_dve(dve, "a", u, 2)
                ptrans_dve(dve, "a", u, 3)
                qk_rope_dve(dve, "a", "k", nxt, P, yk, taba)
                a_kslot_dve(dve, nxt)
                v_dve(dve, "a", nxt, 0, VTA)

            a_dve(0, 1)
            with dve.Fori(1, A_HEADS - 1) as i:
                a_dve(i, i + 1)

            u = A_HEADS - 1
            softmax_dve(dve, "a", u, 0, A_SCALE)
            a_osum_dve(dve, u - 1)
            softmax_dve(dve, "a", u, 1, A_SCALE)
            probs_dve(dve, "a", u, 0)
            probs_dve(dve, "a", u, 1)
            a_on_dve(dve, u - 1)
            a_mlo_dve(dve, u - 1)
            softmax_dve(dve, "a", u, 2, A_SCALE)
            softmax_dve(dve, "a", u, 3, A_SCALE)
            probs_dve(dve, "a", u, 2)
            rs_mean_dve(dve, rs_b(0), 1.0, 3, MMB)
            probs_dve(dve, "a", u, 3)
            rs_newton_dve(dve, rs_b(0), 3)
            dve.wait_ge(S("kr_hi"), 1)
            nc.vector.tensor_tensor(klo[64:96, :], rope_keep[64:96, :], khi[64:96, :],
                                    ALU.subtract).then_inc(S("kr_lo"), 1)
            ptrans_dve(dve, "a", u, 0)
            b_q_dve(dve, 0)
            b_k_dve(dve, 0)
            for kb in range(1, NB):
                ptrans_dve(dve, "a", u, kb)
            qk_rope_dve(dve, "b", "q", 0, B_QK, yq, tabb)
            a_osum_dve(dve, u)
            a_on_dve(dve, u)
            v_dve(dve, "b", 0)
            a_mlo_dve(dve, u)

            def b_dve(u, n, s, k):
                if n:
                    rs_mean_dve(dve, rs_b(u + 1), 1.0, 3, MMB)
                softmax_dve(dve, "b", u, 0, B_SCALE)
                if n:
                    rs_newton_dve(dve, rs_b(u + 1), 3)
                softmax_dve(dve, "b", u, 1, B_SCALE)
                probs_dve(dve, "b", u, 0)
                softmax_dve(dve, "b", u, 2, B_SCALE)
                probs_dve(dve, "b", u, 1)
                softmax_dve(dve, "b", u, 3, B_SCALE)
                probs_dve(dve, "b", u, 2)
                probs_dve(dve, "b", u, 3)
                if n:
                    b_q_dve(dve, u + 1)
                ptrans_dve(dve, "b", u, 0)
                if n:
                    b_k_dve(dve, u + 1)
                if n > 1:
                    out_ahead_dve(dve, u)
                ptrans_dve(dve, "b", u, 1)
                ptrans_dve(dve, "b", u, 2)
                if n:
                    qk_rope_dve(dve, "b", "q", u + 1, B_QK, yq, tabb)
                    v_dve(dve, "b", u + 1, 1 - s, VTB)
                ptrans_dve(dve, "b", u, 3)
                head_out_dve(dve, "b", u, s, k)

            with dve.Fori(0, B_LOOP) as i:
                for s in range(2):
                    b_dve(i * 2 + s, 2, s, i + 4)
            for u in range(2 * B_LOOP, B_HEADS):
                b_dve(u, min(2, B_HEADS - 1 - u), u % 2, A_HEADS + u // 2)
            out_dve(dve, G_OUT0, 0, 1)
            ffn_dve(dve, 0, 1, 2)

            def c_prepare():
                dve.wait_ge(S("crawm_in"), 16)
                nc.vector.tensor_copy(cmats[:].rearrange("p m n -> p (m n)"), crawm[:, 0:256])
                nc.vector.tensor_copy(csmask[:].rearrange("p m n -> p (m n)"), crawm[:, 256:768])
            norm_rstd_dve(dve, 2, CO, c_prepare)

            def c_out(u, j):
                dve.wait_ge(S("c_lower"), u * 2 + (j + 1))
                r = slice(C_DIM * j, C_DIM * (j + 1))
                nc.vector.tensor_tensor(co[r, :], bank[CO][0:C_DIM, :], co[r, :], ALU.add).then_inc(S("c_out"), 1)

            def c_out_lo(u, j):
                dve.wait_ge(S("c_mhi"), u * 2 + (j + 1))
                r = slice(C_DIM * j, C_DIM * (j + 1))
                nc.vector.tensor_tensor(tile_at(mlo, u, r), as3(co[r, :], u), tile_at(mhi, u, r),
                                        ALU.subtract).then_inc(S("c_mlo"), 1)
                dve.wait_ge(S("c_mlo"), u * 2 + (j + 1))

            def c_dve(u, nxt):
                if u is not None:
                    for b in range(3):
                        c_chain_dve(dve, u, 0, b)
                    if not is_first(u):
                        c_out(u - 1, 1)
                    c_chain_dve(dve, u, 1, 0)
                if nxt is not None:
                    c_y_dve(dve, nxt, "q")
                if u is not None:
                    if not is_first(u):
                        c_out_lo(u - 1, 1)
                    c_chain_dve(dve, u, 1, 1)
                    c_chain_dve(dve, u, 1, 2)
                if nxt is not None:
                    c_slot_dve(dve, nxt, "q")
                if u is not None:
                    c_w_dve(dve, u, 0, 0)
                    c_v_dve(dve, u)
                    for b in range(1, 3):
                        c_w_dve(dve, u, 0, b)
                if nxt is not None:
                    c_y_dve(dve, nxt, "k")
                    c_slot_dve(dve, nxt, "k")
                if u is not None:
                    c_out(u, 0)
                    for b in range(3):
                        c_w_dve(dve, u, 1, b)
                if nxt is not None:
                    c_y_dve(dve, nxt, "v")
                if u is not None:
                    c_out_lo(u, 0)
                if nxt is None:
                    c_out(u, 1)
                    c_out_lo(u, 1)

            c_dve(None, 0)
            c_dve(0, 1)
            with dve.Fori(1, C_PAIRS - 1) as i:
                c_dve(i, i + 1)
            c_dve(C_PAIRS - 1, None)
            out_dve(dve, G_OUT1, 1, 3)
            ffn_dve(dve, 1, 3, None)

        @block.tensor
        def _(pe):
            project(pe, 0, 0, bank[2][:], h_hi, h_lo, need_h(pe, 0))
            pe.wait_ge(S("mat_in"), 16)
            pe.wait_ge(S("lam_prod"), 2)
            nc.tensor.matmul(bank[5][:, 0:2], M["ones"], tiny[:, T_LP:T_LP + 2], start=True,
                             stop=True).then_inc(S("lam_sum"), 1)
            norm_pe(pe, 0, MMB)
            project(pe, 1, 1, bank[3][:], h_hi, h_lo)
            rs_spread_pe(pe, RS_NORM[0], 1, MMB)
            project(pe, 2, 2, bank[0][:], h_hi, h_lo)
            pe.wait_ge(S("l_sq"), 2)
            rs_sum_pe(RS_QL, [(sqb, P), (tb, P)], M["ones"][:, 0:1], 1, MMB)
            project(pe, 3, 0, bank[1][:], h_hi, h_lo)
            rs_spread_pe(pe, RS_QL, 1, MMB)
            pe.wait_ge(S("lam_exp"), 1)
            pe.wait_ge(S("l_sq"), 3)
            rs_sum_pe(RS_KVL, [(sqb, P)], M["ones"][:, 0:1], 1, 5)

            a_proj_pe(pe, 0, "q")
            rs_spread_pe(pe, RS_KVL, 1, 6)
            qk_sum_pe(pe, "r", "q", 0, RS_ROPE, B_QK, "blk_b", 2, OB)
            a_proj_pe(pe, 0, "k")
            rs_spread_pe(pe, RS_ROPE, 2, MMB)
            qk_sum_pe(pe, "a", "q", 0, rs_a(0, "q"), P, "blk64", 2, OB)
            qk_rot_pe(pe, "r", "q", 0, B_QK, "rot_b")
            a_proj_pe(pe, 0, "v")
            rs_spread_pe(pe, rs_a(0, "q"), 2, QMB)
            qk_sum_pe(pe, "a", "k", 0, rs_a(0, "k"), P, "blk64", 2, KSB)
            pe.wait_ge(*at_head("r", "qs", 1))
            qk_rot_pe(pe, "a", "q", 0, P, "rot_a")
            rs_spread_pe(pe, rs_a(0, "k"), 2, KMB, 1)
            pe.wait_ge(*at_head("a", "qs", 1))
            qk_rot_pe(pe, "a", "k", 0, P, "rot_a")
            vtrans_pe(pe, "a", 0, VTA)

            def a_pe(u, nxt):
                scores_pe(pe, "a", u, 0)
                if not is_first(u):
                    a_osum_pe(pe, u - 1)
                scores_pe(pe, "a", u, 1)
                a_proj_pe(pe, nxt, "q")
                if not is_first(u):
                    rs_spread_pe(pe, rs_a(u - 1, "out"), 1, MMB)
                scores_pe(pe, "a", u, 2)
                scores_pe(pe, "a", u, 3)
                qk_sum_pe(pe, "a", "q", nxt, rs_a(nxt, "q"), P, "blk64", 2, OB)
                a_proj_pe(pe, nxt, "k")
                if not is_first(u):
                    pe.wait_ge(*at_head("a", "on", u))
                rs_spread_pe(pe, rs_a(nxt, "q"), 2, MMB)
                ptrans_pe(pe, "a", u, 0)
                qk_sum_pe(pe, "a", "k", nxt, rs_a(nxt, "k"), P, "blk64", 2, KSB)
                ptrans_pe(pe, "a", u, 1)
                qk_rot_pe(pe, "a", "q", nxt, P, "rot_a")
                a_proj_pe(pe, nxt, "v")
                rs_spread_pe(pe, rs_a(nxt, "k"), 2, KMB, 1)
                values_pe(pe, "a", u, 0)
                ptrans_pe(pe, "a", u, 2)
                ptrans_pe(pe, "a", u, 3)
                pe.wait_ge(*at_head("a", "qs", nxt + 1))
                qk_rot_pe(pe, "a", "k", nxt, P, "rot_a")
                for b in range(1, NB):
                    values_pe(pe, "a", u, b)
                vtrans_pe(pe, "a", nxt, VTA)

            a_pe(0, 1)
            with pe.Fori(1, A_HEADS - 1) as i:
                a_pe(i, i + 1)

            u = A_HEADS - 1
            scores_pe(pe, "a", u, 0)
            a_osum_pe(pe, u - 1)
            scores_pe(pe, "a", u, 1)
            pe.wait_ge(*at_head("a", "vlo", A_HEADS))
            b_proj_pe(pe, 0, 0)
            b_proj_kv_pe(pe, 0)
            rs_spread_pe(pe, rs_a(u - 1, "out"), 1, MMB)
            scores_pe(pe, "a", u, 2)
            scores_pe(pe, "a", u, 3)
            pe.wait_ge(*at_head("a", "on", A_HEADS - 1))
            b_sums_pe(pe, 0)
            b_proj_pe(pe, 1, 1)
            b_proj_kv_pe(pe, 1)
            ptrans_pe(pe, "a", u, 0)
            rs_spread_pe(pe, rs_b(0), 2, MMB, step=3)
            b_spread_k_pe(pe, 0)
            ptrans_pe(pe, "a", u, 1)
            ptrans_pe(pe, "a", u, 2)
            values_pe(pe, "a", u, 0)
            ptrans_pe(pe, "a", u, 3)
            qk_rot_pe(pe, "b", "q", 0, B_QK, "rot_b")
            for kb in range(1, NB):
                values_pe(pe, "a", u, kb)
            vtrans_pe(pe, "b", 0)
            a_osum_pe(pe, u)
            rs_spread_pe(pe, rs_a(u, "out"), 1, MMB)
            pe.wait_ge(S("kr_lo"), 1)
            pe.wait_ge(*at_head("a", "on", A_HEADS))

            def b_pe(u, n, s):
                if n:
                    pe.wait_ge(*at_head("b", "qs", u + 1))
                    b_sums_pe(pe, u + 1)
                for b in range(NB):
                    scores_pe(pe, "b", u, b)
                if n:
                    rs_spread_pe(pe, rs_b(u + 1), 2, MMB, step=3)
                    pe.wait_ge(*at_head("b", "e", u * NB + 2))
                    b_spread_k_pe(pe, u + 1)
                else:
                    out_early_pe(pe, G_OUT0, 0, 0, range(KT - A_HEADS - 1))
                if n > 1:
                    out_ahead_pe(pe, u, s, range(0, AHEAD_FIRST))
                ptrans_pe(pe, "b", u, 0)
                ptrans_pe(pe, "b", u, 1)
                if n > 1:
                    out_ahead_pe(pe, u, s, range(AHEAD_FIRST, A_HEADS))
                ptrans_pe(pe, "b", u, 2)
                values_pe(pe, "b", u, 0, s)
                if n:
                    qk_rot_pe(pe, "b", "q", u + 1, B_QK, "rot_b")
                values_pe(pe, "b", u, 1, s)
                if n > 1:
                    pe.wait_ge(S("ahead_x"), u + 1)
                if n:
                    vtrans_pe(pe, "b", u + 1, VTB)
                ptrans_pe(pe, "b", u, 3)
                if n == 0:
                    out_early_pe(pe, G_OUT0, 0, 1, range(KT - A_HEADS - 1))
                if n > 1:
                    b_proj_pe(pe, u + 2, s)
                    b_proj_kv_pe(pe, s)
                values_pe(pe, "b", u, 2, s)
                values_pe(pe, "b", u, 3, s)

            with pe.Fori(0, B_LOOP) as i:
                for s in range(2):
                    b_pe(i * 2 + s, 2, s)
            for u in range(2 * B_LOOP, B_HEADS):
                b_pe(u, min(2, B_HEADS - 1 - u), u % 2)
            out_pe(pe, G_OUT0, 0, at_head("b", "mlo", B_HEADS))
            ffn_pe(pe, 0, 1)

            def c_pe(u, nxt):
                if u is not None:
                    c_scores_pe(pe, u, 0)
                    c_scores_pe(pe, u, 1)
                if u is None:
                    pe.wait_ge(*at_net(0, "x", KT + 7))
                if nxt is not None:
                    c_proj_pe(pe, nxt, "q", need_h(pe, 2) if u is None else None)
                if u is not None:
                    if nxt is None:
                        pe.wait_ge(S("c_vy"), C_PAIRS)
                        out_early_pe(pe, G_OUT1, 1, 0, range(KT - 2))
                    c_tail_pe(pe, u, 0)
                    c_vt_pe(pe, u)
                else:
                    norm_pe(pe, 2, CO)
                if nxt is not None:
                    c_proj_pe(pe, nxt, "k")
                if u is None:
                    rs_spread_pe(pe, RS_NORM[2], 1, CO)
                if u is not None:
                    c_tail_pe(pe, u, 1)
                    c_values_pe(pe, u, 0)
                    if nxt is None:
                        pe.wait_ge(S("c_mlo"), C_HEADS - 2)
                        out_early_pe(pe, G_OUT1, 1, 1, range(KT - 1))
                if nxt is not None:
                    c_proj_pe(pe, nxt, "v")
                if u is not None:
                    c_values_pe(pe, u, 1)
                if nxt is None:
                    out_early_pe(pe, G_OUT1, 1, 0, (KT - 2,))

            c_pe(None, 0)
            pe.wait_ge(S("c_vy"), 1)
            c_pe(0, 1)
            with pe.Fori(1, C_PAIRS - 1) as i:
                c_pe(i, i + 1)
            c_pe(C_PAIRS - 1, None)
            out_pe(pe, G_OUT1, 1, (S("c_mlo"), C_HEADS))
            ffn_pe(pe, 1, 3)


def constants():
    f = np.float32
    i = np.arange(P)

    def rot(first, rows, half):
        m = np.zeros((P, P), f)
        for r in range(first, first + rows):
            up = (r - first) % (2 * half) < half
            m[r + half if up else r - half, r] = -1.0 if up else 1.0
        return m
    blk64 = (i[:, None] // 64 == i[None, :] // 64).astype(f)
    blk_b = np.zeros((P, P), f)
    blk_b[:B_NOPE, :B_NOPE] = 1.0 / B_NOPE
    blk_b[B_NOPE:B_QK, B_NOPE:B_QK] = 1.0 / B_ROPE
    mats = np.stack([np.eye(P, dtype=f), rot(0, P, A_DIM // 2), rot(B_NOPE, B_ROPE, B_ROPE // 2), blk64,
                     blk_b, np.ones((P, P), f)], axis=1)
    hidden = np.where(i[:, None] // CHUNK < i[None, :] // CHUNK, f(BIG), f(0))
    masks_a = np.zeros((P, 2, 256), f)
    masks_a[:, 0, :P], masks_a[:, 0, P:], masks_a[:, 1, P:] = hidden, BIG, hidden
    later = np.where(i[None, :] <= i[:, None], f(BIG), f(0))
    masks_c = np.zeros((P, 768), f)
    masks_c[:, 0:P] = -(i[:, None] >= i[None, :]).astype(f)
    masks_c[:, P:2 * P] = -1.0
    masks_c[:, 256:384] = later
    masks_c[:, 512:640] = BIG
    masks_c[:, 640:768] = later

    def table(half, rows):
        freq = np.power(f(THETA), -np.arange(half, dtype=f) / f(half)).astype(f)
        ang = (np.arange(SEQ, dtype=f)[:, None] * freq[None, :]).astype(f)
        r = np.arange(rows) % half
        return np.cos(ang).T[r], np.sin(ang).T[r]
    tabs_a = np.stack(table(A_DIM // 2, P), axis=1).astype(f)
    tabs_b = np.zeros((P, 2, SEQ), f)
    tabs_b[:B_NOPE, 0] = 1.0
    c, s = table(B_ROPE // 2, B_ROPE)
    tabs_b[B_NOPE:B_QK, 0], tabs_b[B_NOPE:B_QK, 1] = c, s
    return mats, masks_a, masks_c, tabs_a, tabs_b


def layout(i):
    f = np.float32
    a = {k: np.asarray(t) for k, t in i.items()}

    def chunks(w, tiles=None):
        k, n = w.shape
        return w.reshape(k // P, P, n // P, P).transpose(2, 1, 0, 3).reshape(n // P, P, k)
    w = a["ab_w_in"][0]
    aq, ak, av = w[:, 0:512], w[:, 512:1024], w[:, 1024:1536]
    kr = np.zeros((D, P), f)
    kr[:, B_NOPE:B_QK] = w[:, 1920:1952]
    rows = [chunks(w[:, 1536:1920]), chunks(kr)]
    rows.append(np.stack([chunks(aq), chunks(ak), chunks(av)], axis=1).reshape(-1, P, W_IN))
    wo = chunks(a["ab_w_out"][0])
    rows.append(np.concatenate([np.roll(wo[:OUT_AHEAD], -W_AHEAD, axis=2), wo[OUT_AHEAD:]]))
    down = []

    def network(l):
        gate, up = chunks(a["ffn_w_gate"][l]), chunks(a["ffn_w_up"][l])
        rows.append(np.stack([gate, up], axis=1).reshape(-1, P, W_IN))
        for s in range(2):
            down.append(chunks(a["ffn_w_down"][l][s * HALF_F * P:(s + 1) * HALF_F * P]))
    network(0)
    c = a["c_w_in"][0]
    rows.append(np.stack([chunks(c[:, t * D:(t + 1) * D]) for t in range(3)], axis=1).reshape(-1, P, W_IN))
    rows.append(chunks(a["c_w_out"][0]))
    network(1)
    w_in, w_down = np.concatenate(rows), np.concatenate(down)

    qb = a["b_w_q_b"][0].reshape(2, P, B_HEADS, B_QK).transpose(2, 1, 0, 3).reshape(B_HEADS, P, 2 * B_QK)
    kvb = a["b_w_kv_b"][0].reshape(P, B_HEADS, P).transpose(1, 0, 2)
    ahead = np.zeros((B_HEADS, P, W_AHEAD), f)
    ahead[2:] = wo[:OUT_AHEAD, :, :W_AHEAD]
    w_b = np.concatenate([qb, kvb, ahead], axis=2)

    vecs = np.zeros((P, V_N), f)
    gains = [a["norm_mix"][0], a["norm_ffn"][0], a["norm_mix"][1], a["norm_ffn"][1]]
    vecs[:, V_GAIN:V_GAIN + 4 * KT] = np.stack(gains).reshape(4 * KT, P).T
    vecs[:, V_AQ] = np.concatenate([a["a_q_norm"][0]] * 2)
    vecs[:, V_AK] = np.concatenate([a["a_k_norm"][0]] * 2)
    vecs[:, V_AO] = a["a_out_norm"][0]
    vecs[:, V_BQL:V_BQL + 2] = a["b_q_a_norm"][0].reshape(2, P).T
    vecs[:, V_BKVL] = a["b_kv_a_norm"][0]
    vecs[:B_NOPE, V_BQ], vecs[B_NOPE:B_QK, V_BQ] = a["b_q_nope_norm"][0], a["b_q_rope_norm"][0]
    vecs[:B_NOPE, V_BK] = a["b_k_nope_norm"][0]
    vecs[B_NOPE:B_QK, V_BKR] = a["b_k_rope_norm"][0]
    vecs[:A_DIM, V_LAM:V_LAM + 4] = a["a_lambda"][0].T
    xt = a["x"][0].T.reshape(KT, P, SEQ)
    return dict(xt=xt, w_in=w_in, w_b=w_b, w_down=w_down, vecs=vecs)


def kernel(**inputs):
    import concourse.bacc as bacc
    from concourse.bass_utils import run_bass_kernel_spmd

    arrays = layout(inputs)
    for name, value in zip(("mats", "masks_a", "masks_c", "tabs_a", "tabs_b"), constants()):
        arrays[name] = value
    arrays = {n: np.ascontiguousarray(t) for n, t in arrays.items()}
    nc = bacc.Bacc("TRN2", target_bir_lowering=False, num_devices=1)
    aps = {n: nc.dram_tensor(f"in_{n}", t.shape, mybir.dt.from_np(t.dtype), kind="ExternalInput").ap()
           for n, t in arrays.items()}
    out = nc.dram_tensor("out", (KT, P, SEQ), F32, kind="ExternalOutput").ap()
    trunk(nc, out=out, **aps)
    r = run_bass_kernel_spmd(nc, [{f"in_{n}": t for n, t in arrays.items()}], core_ids=[0])
    return r.results[0]["out"].reshape(D, SEQ).T.reshape(1, SEQ, D)
```
